# Optimizing a Trainium2 kernel written in Bass

```python
import jax, jax.numpy as jnp
from jax import lax
import numpy as np

D_MODEL = 1024
BATCH = 1
SEQ = 256
DEPTH = 1
DEC_BATCH = 1
DEC_SEQ = 1024
PAST_LEN = 128

D_A = 1024
A_CHUNK = 128
A_GROUPS = 8
A_GROUP_DIM = D_A // A_GROUPS
D_B = 1024
B_HEAD_DIM = 128
B_HEADS = D_B // B_HEAD_DIM
B_CHUNK = 16
N_EXPERTS = 16
EXPERT_FF = 1024
CAPACITY_FACTOR = 2
EPS = 1e-6
SPLIT_SIZES = (D_A, D_A, D_B, D_B, D_B, D_B, D_B, D_MODEL, D_MODEL)
D_IN = 2 * D_A + 5 * D_B + 2 * D_MODEL

kernel_name = "hybrid_gmlp_hgrn2_ec_encoder"

def rmsnorm(x, g):
    xf = x.astype(jnp.float32)
    y = xf * lax.rsqrt(jnp.mean(xf * xf, axis=-1, keepdims=True) + EPS)
    return (y * g.astype(jnp.float32)).astype(x.dtype)

def split_cols(z):
    out = []
    start = 0
    for s in SPLIT_SIZES:
        out.append(z[..., start:start + s])
        start += s
    return out

def lower_bounds(lb_logits):
    p = jax.nn.softmax(lb_logits.astype(jnp.float32), axis=1)
    c = jnp.cumsum(p, axis=1)
    return c - c[:, :1]

def gmlp_branch(u, v, vnorm_g, w_s, b_s):
    Bn, L, _ = v.shape
    n = L // A_CHUNK
    v = rmsnorm(v, vnorm_g)
    vc = v.reshape(Bn, n, A_CHUNK, A_GROUPS, A_GROUP_DIM)
    s = jnp.einsum('gts,bnsgc->bntgc', w_s, vc) + b_s.T[None, None, :, :, None]
    return u * s.reshape(Bn, L, D_A)

def chunk_gla(q, k, v, g):
    Bn, H, L, K = q.shape
    V = v.shape[-1]
    n = L // B_CHUNK

    def to_chunks(t):
        return t.reshape(Bn, H, n, B_CHUNK, t.shape[-1]).transpose(2, 0, 1, 3, 4)

    tri = jnp.tril(jnp.ones((B_CHUNK, B_CHUNK), dtype=bool))[:, :, None]

    def step(S, inp):
        qt, kt, vt, gt = inp
        G = jnp.cumsum(gt, axis=2)
        G_last = G[:, :, -1:, :]
        o_inter = jnp.einsum('bhtk,bhkv->bhtv', qt * jnp.exp(G), S)
        D = G[:, :, :, None, :] - G[:, :, None, :, :]
        decay = jnp.exp(jnp.where(tri, D, -jnp.inf))
        A = jnp.einsum('bhtk,bhtsk->bhts', qt, decay * kt[:, :, None, :, :])
        o = o_inter + jnp.einsum('bhts,bhsv->bhtv', A, vt)
        S = jnp.exp(G_last[:, :, 0, :])[..., None] * S + jnp.einsum(
            'bhsk,bhsv->bhkv', kt * jnp.exp(G_last - G), vt)
        return S, o

    S0 = jnp.zeros((Bn, H, K, V), jnp.float32)
    _, o = lax.scan(step, S0, (to_chunks(q), to_chunks(k), to_chunks(v), to_chunks(g)))
    return o.transpose(1, 2, 0, 3, 4).reshape(Bn, H, L, V)

def hgrn2_branch(q, i, z_fwd, z_bwd, lb, onorm_g, g_out):
    Bn, L, _ = q.shape

    def heads(t):
        return t.astype(jnp.float32).reshape(Bn, L, B_HEADS, B_HEAD_DIM).transpose(0, 2, 1, 3)

    def gates(z, lb_dir):
        lbh = lb_dir.reshape(1, B_HEADS, 1, B_HEAD_DIM)
        zh = heads(z)
        log_f = jnp.logaddexp(jnp.log(lbh), jnp.log1p(-lbh) + jax.nn.log_sigmoid(zh))
        k = (1.0 - lbh) * jax.nn.sigmoid(-zh)
        return k, log_f

    def rev(t):
        return jnp.flip(t, axis=2)

    qh, vh = heads(q), heads(i)
    k_f, g_f = gates(z_fwd, lb[0])
    k_b, g_b = gates(z_bwd, lb[1])
    o = chunk_gla(jnp.concatenate([qh, rev(qh)], axis=1),
                  jnp.concatenate([k_f, rev(k_b)], axis=1),
                  jnp.concatenate([vh, rev(vh)], axis=1),
                  jnp.concatenate([g_f, rev(g_b)], axis=1))
    o = o[:, :B_HEADS] + rev(o[:, B_HEADS:])
    o = o * lax.rsqrt(jnp.mean(o * o, axis=-1, keepdims=True) + EPS) * onorm_g.astype(jnp.float32)
    o = o.transpose(0, 2, 1, 3).reshape(Bn, L, D_B).astype(g_out.dtype)
    return o * jax.nn.silu(g_out)

def expert_choice_ffn(x, w_r, w_g, w_u, w_d):
    Bn, L, D = x.shape
    T = Bn * L
    C = CAPACITY_FACTOR * T // N_EXPERTS
    xt = x.reshape(T, D)
    aff = jax.nn.softmax(jnp.einsum('td,de->te', xt, w_r).astype(jnp.float32), axis=-1)
    gate, idx = lax.top_k(aff.T, C)
    xe = xt[idx]
    h = jax.nn.silu(jnp.einsum('ecd,edf->ecf', xe, w_g)) * jnp.einsum('ecd,edf->ecf', xe, w_u)
    ye = jnp.einsum('ecf,efd->ecd', h, w_d) * gate[..., None].astype(x.dtype)
    y = jnp.zeros_like(xt).at[idx.reshape(-1)].add(ye.reshape(-1, D))
    return y.reshape(Bn, L, D)

def trunk(x, norm1_g, w_in, a_vnorm_g, a_spatial_w, a_spatial_b, b_lb_logits, b_onorm_g,
          w_branch_a, w_branch_b, w_out, norm2_g, w_router, w_exp_gate, w_exp_up,
          w_exp_down, final_g):
    lbs = lower_bounds(b_lb_logits)
    for l in range(DEPTH):
        h = rmsnorm(x, norm1_g[l])
        z = jnp.einsum('bld,de->ble', h, w_in[l])
        u, v, q, i, z_f, z_b, g_o, g_a, g_b = split_cols(z)
        ya = gmlp_branch(jax.nn.gelu(u), jax.nn.gelu(v), a_vnorm_g[l], a_spatial_w[l], a_spatial_b[l])
        yb = hgrn2_branch(q, i, z_f, z_b, lbs[:, l], b_onorm_g[l], g_o)
        m = (jax.nn.sigmoid(g_a) * jnp.einsum('bla,ad->bld', ya, w_branch_a[l])
             + jax.nn.sigmoid(g_b) * jnp.einsum('blc,cd->bld', yb, w_branch_b[l]))
        x = x + jnp.einsum('bld,de->ble', m, w_out[l])
        x = x + expert_choice_ffn(rmsnorm(x, norm2_g[l]), w_router[l], w_exp_gate[l],
                                  w_exp_up[l], w_exp_down[l])
    return rmsnorm(x, final_g)

def setup_inputs(seed: int = 0) -> dict:
    key = jax.random.key(seed)
    ks = jax.random.split(key, 20)
    f32 = jnp.float32

    def nrm(k, shape, scale):
        return jax.random.normal(k, shape, f32) * scale

    return {
        'x_prompt': nrm(ks[0], (BATCH, SEQ, D_MODEL), 1.0),
        'x_sample': nrm(ks[1], (DEC_BATCH, DEC_SEQ, D_MODEL), 1.0),
        'norm1_g': 1.0 + nrm(ks[2], (DEPTH, D_MODEL), 0.02),
        'w_in': nrm(ks[3], (DEPTH, D_MODEL, D_IN), D_MODEL ** -0.5),
        'a_vnorm_g': 1.0 + nrm(ks[4], (DEPTH, D_A), 0.02),
        'a_spatial_w': nrm(ks[5], (DEPTH, A_GROUPS, A_CHUNK, A_CHUNK), A_CHUNK ** -0.5),
        'a_spatial_b': 1.0 + nrm(ks[6], (DEPTH, A_GROUPS, A_CHUNK), 0.02),
        'b_lb_logits': 1.0 + nrm(ks[7], (2, DEPTH, D_B), 0.1),
        'b_onorm_g': 1.0 + nrm(ks[8], (DEPTH, B_HEAD_DIM), 0.02),
        'w_branch_a': nrm(ks[9], (DEPTH, D_A, D_MODEL), D_A ** -0.5),
        'w_branch_b': nrm(ks[10], (DEPTH, D_B, D_MODEL), D_B ** -0.5),
        'w_out': nrm(ks[11], (DEPTH, D_MODEL, D_MODEL), D_MODEL ** -0.5),
        'norm2_g': 1.0 + nrm(ks[12], (DEPTH, D_MODEL), 0.02),
        'w_router': nrm(ks[13], (DEPTH, D_MODEL, N_EXPERTS), D_MODEL ** -0.5),
        'w_exp_gate': nrm(ks[14], (DEPTH, N_EXPERTS, D_MODEL, EXPERT_FF), D_MODEL ** -0.5),
        'w_exp_up': nrm(ks[15], (DEPTH, N_EXPERTS, D_MODEL, EXPERT_FF), D_MODEL ** -0.5),
        'w_exp_down': nrm(ks[16], (DEPTH, N_EXPERTS, EXPERT_FF, D_MODEL), EXPERT_FF ** -0.5),
        'final_g': 1.0 + nrm(ks[17], (D_MODEL,), 0.02),
    }

def reference(x_prompt, x_sample, norm1_g, w_in, a_vnorm_g, a_spatial_w, a_spatial_b,
              b_lb_logits, b_onorm_g, w_branch_a, w_branch_b, w_out, norm2_g, w_router,
              w_exp_gate, w_exp_up, w_exp_down, final_g):
    y_prompt = trunk(x_prompt, norm1_g, w_in, a_vnorm_g, a_spatial_w, a_spatial_b, b_lb_logits,
                     b_onorm_g, w_branch_a, w_branch_b, w_out, norm2_g, w_router, w_exp_gate,
                     w_exp_up, w_exp_down, final_g)
    y_sample = trunk(x_sample, norm1_g, w_in, a_vnorm_g, a_spatial_w, a_spatial_b, b_lb_logits,
                     b_onorm_g, w_branch_a, w_branch_b, w_out, norm2_g, w_router, w_exp_gate,
                     w_exp_up, w_exp_down, final_g)
    return (y_prompt, y_sample)


_drawn_inputs = setup_inputs


def setup_inputs(seed=0):
    import zlib

    import numpy as np

    out = dict(_drawn_inputs(seed))
    spreads = {}
    factors = {'a_vnorm_g': 5.754,
     'a_spatial_b': 5.931,
     'b_onorm_g': 4.906,
     'norm2_g': 3.549,
     'final_g': 2.871}
    for name, (base, spread) in spreads.items():
        noise = np.random.default_rng([zlib.crc32(name.encode()), seed]).standard_normal(out[name].shape)
        drawn = base * np.exp(spread * noise) if base else spread * noise
        out[name] = __import__('jax').numpy.asarray(drawn.astype(out[name].dtype))
    for name, factor in factors.items():
        out[name] = (out[name] * factor).astype(out[name].dtype)
    return out
```

```python
from contextlib import ExitStack

import concourse.bass as bass
from concourse import mybir

F32 = mybir.dt.float32
F32R = mybir.dt.float32r
U32 = mybir.dt.uint32
I32 = mybir.dt.int32
U8 = mybir.dt.uint8
ALU = mybir.AluOpType
ACT = mybir.ActivationFunctionType
AX = mybir.AxisListType

P = 128
D = 1024
KC = D // P
T_PROMPT = 256
T_SAMPLE = 1024
T = T_PROMPT + T_SAMPLE
NT = T // P
NT_PROMPT = T_PROMPT // P
GROUPS = D // P
HEADS = D // P
NE = 16
CAP_S = 2 * T_SAMPLE // NE
CAP_P = 2 * T_PROMPT // NE
SLOTS = CAP_S + CAP_P
EPS = 1e-6
PART = 320
PARTS = T // PART
LEVELS = 7
CREDIT = 8
COL_U, COL_V, COL_Q, COL_I, COL_ZF, COL_ZB, COL_GO, COL_GA, COL_GB = (j * D for j in range(9))
SEQS = ((0, NT_PROMPT), (NT_PROMPT, NT))


def cols(w, c0):
    return w.rearrange("(k p) n -> p k n", p=P)[:, :, bass.ds(c0, P)]


class Stage:

    def __init__(self, nc, name):
        self.nc, self.name, self.ctx, self.sems = nc, name, ExitStack(), []
        self.waited = None

    def __enter__(self):
        self.ctx.__enter__()
        return self

    def __exit__(self, *a):
        if self.sems and a[0] is None:
            for sem in self.sems:
                self.nc.gpsimd.sem_clear(sem)
                self.nc.release_semaphore(sem)
        return self.ctx.__exit__(*a)

    def sb(self, name, shape, dt=F32):
        return self.ctx.enter_context(self.nc.sbuf_tensor(f"{self.name}_{name}", shape, dt))

    def ps(self, name, shape, dt=F32):
        return self.ctx.enter_context(self.nc.psum_tensor(f"{self.name}_{name}", shape, dt))

    def sem(self, name):
        self.sems.append(self.nc.alloc_semaphore(f"{self.name}_{name}"))
        return self.sems[-1]

    def stand(self, eng):
        self.waited = self.waited or self.sem("waited")
        eng.sem_inc(self.waited, 1)

    def block(self):
        return self.nc.Block()


class WeightStream:

    def __init__(self, st, per):
        self.st, self.per = st, per
        ring = 2 if per % 2 == 0 else 3
        self.raw_slot = [t % 2 for t in range(per)]
        self.slot = [t % ring for t in range(per)]
        self.raw = [st.sb(f"w_raw{i}", [P, KC, P]) for i in range(2)]
        self.hi = [st.sb(f"w_hi{i}", [P, KC, P], F32R) for i in range(ring)]
        self.lo = [st.sb(f"w_lo{i}", [P, KC, P], F32R) for i in range(ring)]
        self.out = [st.ps(f"proj{i}", [P, 512]) for i in range(2)]
        self.loaded = [st.sem(f"w_loaded{i}") for i in range(2)]
        self.hi_ready = st.sem("w_hi_ready")
        self.lo_ready = st.sem("w_lo_ready")
        self.group_done = st.sem("proj_group_done")
        self.bank_free = [st.sem(f"proj_bank_free{i}") for i in range(2)]

    def back(self, slots, t):
        return next(d for d in range(1, self.per + 1) if slots[(t - d) % self.per] == slots[t])

    def load(self, sp, r, t, src):
        n = self.per * r + t - self.back(self.raw_slot, t)
        sp.wait_ge(self.hi_ready, n + 1 + CREDIT)
        sp.wait_ge(self.lo_ready, n + 1 + CREDIT)
        self.st.stand(sp)
        sp.dma_start(self.raw[self.raw_slot[t]][:], src).then_inc(self.loaded[self.raw_slot[t]], 16)

    def split_hi(self, nc, act, r, t):
        rs, s = self.raw_slot[t], self.slot[t]
        n = self.per * r + t - self.back(self.slot, t)
        turn = self.raw_slot.count(rs) * r + self.raw_slot[:t + 1].count(rs)
        act.wait_ge(self.group_done, PARTS * (n + 1 + CREDIT))
        act.wait_ge(self.loaded[rs], 16 * turn)
        nc.scalar.activation(self.hi[s][:], self.raw[rs][:], ACT.Copy).then_inc(self.hi_ready, 1)

    def split_lo(self, nc, pool, r, t):
        rs, s = self.raw_slot[t], self.slot[t]
        pool.wait_ge(self.hi_ready, self.per * r + t + 1 + CREDIT)
        nc.gpsimd.tensor_tensor(self.lo[s][:], self.raw[rs][:], self.hi[s][:].bitcast(F32),
                                ALU.subtract).then_inc(self.lo_ready, 1)

    def multiply(self, nc, pe, r, t, part, x_hi, x_lo):
        g = PARTS * t + part
        s, b = self.slot[t], g % 2
        if part == 0:
            pe.wait_ge(self.lo_ready, self.per * r + t + 1 + CREDIT)
        pe.wait_ge(self.bank_free[b], PARTS // 2 * self.per * r + g // 2 + CREDIT)
        out, c = self.out[b][:, 0:PART], slice(part * PART, (part + 1) * PART)
        for k in range(KC):
            nc.tensor.matmul(out, self.hi[s][:, k, :], x_hi[:, k, c], start=(k == 0), stop=False)
            nc.tensor.matmul(out, self.hi[s][:, k, :], x_lo[:, k, c], start=False, stop=False)
            mm = nc.tensor.matmul(out, self.lo[s][:, k, :], x_hi[:, k, c], start=False, stop=(k == KC - 1))
        mm.then_inc(self.group_done, 1)

    def result(self, eng, r, t, part):
        g = PARTS * t + part
        eng.wait_ge(self.group_done, PARTS * self.per * r + g + 1 + PARTS * CREDIT)
        return self.out[g % 2][:, 0:PART], self.bank_free[g % 2]

    def moved(self, eng, r, t):
        for b in range(2):
            eng.wait_ge(self.bank_free[b], PARTS // 2 * (self.per * r + t + 1) + CREDIT)

    def pe_credit(self, pe):
        pe.sem_inc(self.group_done, PARTS * CREDIT)

    def act_credit(self, act):
        act.sem_inc(self.hi_ready, CREDIT)
        for b in range(2):
            act.sem_inc(self.bank_free[b], CREDIT)

    def pool_credit(self, pool):
        pool.sem_inc(self.lo_ready, CREDIT)


def norm_in(nc, C, x_prompt, x_sample, norm1_g, h_hi, h_lo):
    PAIRS = NT // 2
    with Stage(nc, "n1") as st:
        x = st.sb("x", [P, NT, D])
        gain = st.sb("gain", [P, D])
        junk = st.sb("junk", [P, D])
        xn = st.sb("xn", [P, 2, D])
        ssq, var, std, rstd = (st.sb(n, [P, NT]) for n in ("ssq", "var", "std", "rstd"))
        xT = st.ps("xT", [P, 2, KC, P])
        x_loaded = [st.sem(f"x_loaded{j}") for j in range(PAIRS)]
        gain_loaded, ssq_ready, var_ready, std_ready = (st.sem(n) for n in ("gain_loaded", "ssq_ready", "var_ready", "std_ready"))
        rstd_ready, xn_ready, xT_ready, hi_ready, lo_ready = (st.sem(n) for n in ("rstd_ready", "xn_ready", "xT_ready", "hi_ready", "lo_ready"))
        with st.block() as block:

            @block.sync
            def _(sp):
                sp.dma_start(x[:, 0:2, :], x_prompt.rearrange("b (t p) d -> p (b t) d", p=P)).then_inc(x_loaded[0], 16)
                sp.dma_start(gain[:], norm1_g.broadcast_to([P, D])).then_inc(gain_loaded, 16)
                xs = x_sample.rearrange("b (t p) d -> p (b t) d", p=P)
                for j in range(1, PAIRS):
                    sp.dma_start(x[:, 2 * j:2 * j + 2, :], xs[:, 2 * j - 2:2 * j, :]).then_inc(x_loaded[j], 16)

            @block.scalar
            def _(act):
                def square(t):
                    act.wait_ge(x_loaded[t // 2], 16)
                    if t:
                        act.wait_ge(ssq_ready, t)
                    nc.scalar.activation(junk[:], x[:, t, :], ACT.Square,
                                         accum_out=ssq[:, t:t + 1]).then_inc(ssq_ready, 1)

                def root(t):
                    act.wait_ge(var_ready, t + 1)
                    nc.scalar.activation(std[:, t:t + 1], var[:, t:t + 1], ACT.Sqrt).then_inc(std_ready, 1)

                square(0)
                root(0)
                for t in range(NT):
                    if t + 1 < NT:
                        square(t + 1)
                        root(t + 1)
                    act.wait_ge(xT_ready, t + 1)
                    nc.scalar.activation(h_hi[:, :, t * P:(t + 1) * P], xT[:, t % 2], ACT.Copy).then_inc(hi_ready, 1)

            @block.vector
            def _(dve):
                def scale(t):
                    dve.wait_ge(ssq_ready, t + 1)
                    nc.vector.tensor_scalar(var[:, t:t + 1], ssq[:, t:t + 1], 1.0 / D, EPS, ALU.mult,
                                            ALU.add).then_inc(var_ready, 1)
                    dve.wait_ge(std_ready, t + 1)
                    nc.vector.reciprocal(rstd[:, t:t + 1], std[:, t:t + 1]).then_inc(rstd_ready, 1)
                    dve.wait_ge(rstd_ready, t + 1)
                    if t >= 2:
                        dve.wait_ge(xT_ready, t - 1)
                    nc.vector.scalar_tensor_tensor(out=xn[:, t % 2, :], in0=x[:, t, :], scalar=rstd[:, t:t + 1],
                                                   in1=gain[:], op0=ALU.mult, op1=ALU.mult).then_inc(xn_ready, 1)

                dve.wait_ge(gain_loaded, 16)
                scale(0)
                for t in range(NT):
                    if t + 1 < NT:
                        scale(t + 1)
                    dve.wait_ge(hi_ready, t + 1)
                    c = slice(t * P, (t + 1) * P)
                    nc.vector.tensor_tensor(h_lo[:, :, c], xT[:, t % 2], h_hi[:, :, c].bitcast(F32),
                                            ALU.subtract).then_inc(lo_ready, 1)

            @block.tensor
            def _(pe):
                for t in range(NT):
                    pe.wait_ge(xn_ready, t + 1)
                    if t >= 2:
                        pe.wait_ge(lo_ready, t - 1)
                    for k in range(KC):
                        mm = nc.tensor.transpose(xT[:, t % 2, k, :], xn[:, t % 2, k * P:(k + 1) * P], C.ident[:])
                    mm.then_inc(xT_ready, 1)


def constants(nc, C, st, b_lb_logits, b_onorm_g, a_vnorm_g):
    C.ident = st.sb("ident", [P, P])
    C.ones = st.sb("ones", [P, P])
    C.eps = st.sb("eps", [P, 1])
    C.mask = st.sb("mask", [P, LEVELS + 1, P], U8)
    C.lb = st.sb("lb", [P, 2, HEADS])
    C.one_minus_lb = st.sb("one_minus_lb", [P, 2, HEADS])
    C.onorm = st.sb("onorm", [P, 1])
    C.vnorm = st.sb("vnorm", [P, GROUPS])
    with Stage(nc, "const") as s:
        logits = s.sb("logits", [P, 2, HEADS])
        top, expo, prob = (s.sb(n, [P, 2, HEADS]) for n in ("top", "expo", "prob"))
        same = s.sb("same", [P, LEVELS + 1, P])
        diff = s.sb("diff", [P, LEVELS + 1, P])
        cut = s.sb("cut", [P, LEVELS + 1, P])
        loaded, filled, half, made, lb_step = (s.sem(n) for n in ("loaded", "filled", "half", "made", "lb_step"))
        expo_ready = s.sem("expo_ready")
        with s.block() as block:

            @block.sync
            def _(sp):
                sp.dma_start(logits[:], b_lb_logits.rearrange("z a (h p) -> p (z a) h", p=P), allow_slow_non_contiguous=True).then_inc(loaded, 16)
                sp.dma_start(C.onorm[:], b_onorm_g.rearrange("a p -> p a"), allow_slow_non_contiguous=True).then_inc(loaded, 16)
                sp.dma_start(C.vnorm[:], a_vnorm_g.rearrange("a (g p) -> p (a g)", p=P), allow_slow_non_contiguous=True).then_inc(loaded, 16)
                sp.wait_ge(loaded, 48)

            @block.gpsimd
            def _(pool):
                nc.gpsimd.memset(C.ones[:], 1.0)
                nc.gpsimd.memset(C.eps[:], EPS)
                nc.gpsimd.memset(same[:], 1.0).then_inc(filled, 1)
                pool.wait_ge(filled, 1)
                for l in range(LEVELS):
                    b = 1 << l
                    blocks = cut[:, l, :].rearrange("p (n b) -> p n b", b=b)
                    ones = same[:, l, :].rearrange("p (n b) -> p n b", b=b)
                    nc.gpsimd.affine_select(out=blocks, in_=ones, compare_op=ALU.is_ge, fill=0.0, base=0,
                                            pattern=[[-b, P // b], [0, b]], channel_multiplier=1).then_inc(half, 1)
                pool.wait_ge(half, LEVELS)
                for l in range(LEVELS):
                    b = 1 << l
                    blocks = cut[:, l, :].rearrange("p (n b) -> p n b", b=b)
                    ones = same[:, l, :].rearrange("p (n b) -> p n b", b=b)
                    nc.gpsimd.affine_select(out=ones, in_=blocks, compare_op=ALU.is_ge, fill=0.0, base=b - 1,
                                            pattern=[[b, P // b], [0, b]], channel_multiplier=-1).then_inc(made, 1)

            @block.vector
            def _(dve):
                dve.wait_ge(made, LEVELS)
                nc.vector.tensor_copy(C.ident[:], same[:, 0, :])
                nc.vector.tensor_copy(C.mask[:, 0, :], same[:, 0, :])
                nc.vector.tensor_tensor(diff[:, 1:, :], same[:, 1:, :], same[:, 0:LEVELS, :], ALU.subtract).then_inc(lb_step, 1)
                dve.wait_ge(lb_step, 1)
                nc.vector.tensor_copy(C.mask[:, 1:, :], diff[:, 1:, :])
                dve.wait_ge(loaded, 48)
                nc.vector.tensor_copy(top[:], logits[:]).then_inc(lb_step, 1)
                dve.wait_ge(lb_step, 2)
                nc.vector.tensor_tensor(logits[:], logits[:], top[:], ALU.subtract).then_inc(lb_step, 1)
                dve.wait_ge(expo_ready, 1)
                nc.vector.reciprocal(top[:], expo[:]).then_inc(lb_step, 1)
                dve.wait_ge(lb_step, 4)
                nc.vector.tensor_tensor(prob[:], expo[:], top[:], ALU.mult).then_inc(lb_step, 1)
                dve.wait_ge(lb_step, 5)
                nc.vector.tensor_tensor(C.lb[:], prob[:], prob[:], ALU.subtract).then_inc(lb_step, 1)
                dve.wait_ge(lb_step, 6)
                nc.vector.tensor_scalar(C.one_minus_lb[:], C.lb[:], -1.0, 1.0, ALU.mult, ALU.add)

            @block.scalar
            def _(act):
                act.wait_ge(lb_step, 3)
                nc.scalar.activation(expo[:], logits[:], ACT.Exp).then_inc(expo_ready, 1)


def pairs(ap, b):
    return ap.rearrange("p (n two b) -> p n two b", two=2, b=b)


def over(ap, n):
    return ap.unsqueeze(2).broadcast_to([P, ap.shape[1], n])


def hgrn2(nc, C, w_in, h_hi, h_lo, yb_dram):
    order = (COL_I, COL_Q, COL_ZF, COL_ZB, COL_GO)
    TI, TQ, TZF, TZB, TGO = range(5)
    with Stage(nc, "hg") as st:
        W = WeightStream(st, len(order))
        q, f_f, f_b, k_f, k_b, vT, v, so = (st.sb(n, [P, T]) for n in ("q", "f_f", "f_b", "k_f", "k_b", "vT", "v", "so"))
        Q_f, Q_b, A, tot_f, tot_b, Kt_f, Kt_b, y = (st.sb(n, [P, T]) for n in ("Q_f", "Q_b", "A", "tot_f", "tot_b", "Kt_f", "Kt_b", "y"))
        S_f = st.sb("S_f", [P, NT, P])
        S_b = st.sb("S_b", [P, NT, P])
        k_sum, sq, rt = Kt_f, tot_f, tot_b
        G = st.ps("G", [P, 6, 4, P])
        Gc = G[:].rearrange("p b c t -> p (b c) t")

        def bank_cols(base, c):
            return Gc[:, 4 * base + c, :]

        def spans(base):
            return [(G[:, base + j, 0:min(4, NT - 4 * j), :], 4 * j, min(4 * j + 4, NT)) for j in range(3)]

        names = ("v_ready", "gates_ready", "Q_ready", "K_ready",
                 "tot_ready", "k_sum_ready", "A_merged", "gla_step", "v_step", "Kt_ready", "S_ready", "sq_ready",
                 "rt_ready", "y_ready", "y_stored", "A_clear", "sg_ready")
        s = {n: st.sem(n) for n in names}
        STEPS = 13
        DIAG, KTF, KTB, STATE, OUT, ONES = 0, 8, 9, 10, 11, 12
        NQ = 2 * (LEVELS + 1)
        NY = 3
        state_f = [c for a, z in SEQS for c in range(a, z - 1)]
        state_b = [c for a, z in SEQS for c in range(z - 1, a, -1)]
        firsts_f, firsts_b = [a for a, _ in SEQS], [z - 1 for _, z in SEQS]
        after = {j: [j] for j in range(STEPS)}

        def sp_round(sp, r):
            for t, c in enumerate(order):
                W.load(sp, r, t, cols(w_in, c + r * P))

        def store(sp, g):
            sp.wait_ge(s["y_ready"], NY * (g + 1) + CREDIT)
            st.stand(sp)
            sp.dma_start(yb_dram[bass.ds(g * P, P), :], y[:]).then_inc(s["y_stored"], 16)

        def act_buffers(act, r, t):
            if t == TI:
                act.wait_ge(s["v_step"], r + CREDIT)
            if t == TQ:
                act.wait_ge(s["gla_step"], STEPS * (r - 1) + DIAG + 1 + 2 * STEPS)
                act.wait_ge(s["Q_ready"], NQ * (r - 1) + 2 + 2 * NQ)
            if t == TZF:
                act.wait_ge(s["gla_step"], STEPS * (r - 1) + KTF + 1 + 2 * STEPS)
                act.wait_ge(s["Q_ready"], NQ * (r - 1) + 4 + 2 * NQ)
            if t == TZB:
                act.wait_ge(s["gla_step"], STEPS * (r - 1) + KTB + 1 + 2 * STEPS)
            if t in (TZF, TZB):
                act.wait_ge(s["K_ready"], 2 * LEVELS * (r - 1) + 2 + 2 * 2 * LEVELS)
            if t == TGO:
                act.wait_ge(s["y_ready"], NY * r + CREDIT)

        def act_move(act, r, t, part):
            out, free = W.result(act, r, t, part)
            c = slice(part * PART, (part + 1) * PART)
            if t == TI:
                nc.scalar.activation(vT[:, c], out, ACT.Copy).then_inc(free, 1)
            elif t == TQ:
                nc.scalar.activation(q[:, c], out, ACT.Copy).then_inc(free, 1)
            elif t in (TZF, TZB):
                f, k = ((f_f, k_f), (f_b, k_b))[t == TZB]
                nc.scalar.activation(f[:, c], out, ACT.Sigmoid)
                nc.scalar.activation(k[:, c], out, ACT.Sigmoid, scale=-1.0).then_inc(free, 1)
            else:
                nc.scalar.activation(so[:, c], out, ACT.Sigmoid).then_inc(s["sg_ready"], 1)

        def dve_project(dve, r):
            for z, (f, k, t) in enumerate(((f_f, k_f, TZF), (f_b, k_b, TZB))):
                lb, om = C.lb[:, z, bass.ds(r, 1)], C.one_minus_lb[:, z, bass.ds(r, 1)]
                for b in range(2):
                    dve.wait_ge(W.bank_free[b], PARTS // 2 * (W.per * r + t + 1) + CREDIT)
                nc.vector.tensor_scalar(f[:], f[:], om, lb, ALU.mult, ALU.add).then_inc(s["gates_ready"], 1)
                nc.vector.tensor_scalar(k[:], k[:], om, None, ALU.mult).then_inc(s["gates_ready"], 1)

        def dve_output_gate(dve, r):
            for part in range(PARTS):
                dve.wait_ge(s["sg_ready"], PARTS * r + part + 1)
                out, free = W.result(dve, r, TGO, part)
                c = slice(part * PART, (part + 1) * PART)
                nc.vector.tensor_tensor(so[:, c], out, so[:, c], ALU.mult).then_inc(free, 1)

        def pe_values(pe, r):
            for b in range(2):
                pe.wait_ge(W.bank_free[b], PARTS // 2 * (W.per * r + TI + 1) + CREDIT)
            pe.wait_ge(s["y_ready"], NY * r + CREDIT)
            for c in range(NT):
                mm = nc.tensor.transpose(bank_cols(0, c), vT[:, c * P:(c + 1) * P], C.ident[:])
            mm.then_inc(s["v_step"], 1)

        def act_values(act, r):
            act.wait_ge(s["v_step"], r + 1 + CREDIT)
            act.wait_ge(s["gla_step"], STEPS * (r - 1) + OUT + 1 + 2 * STEPS)
            nc.scalar.activation(v[:].rearrange("p (c t) -> p c t", t=P), Gc[:, 0:NT, :], ACT.Copy).then_inc(s["v_ready"], 1)

        def gla_at(g, step):
            return STEPS * g + step + 1 + 2 * STEPS

        def pe_step(pe, g, j):
            base = 3 * (j % 2)
            if j == DIAG:
                pe.wait_ge(s["v_ready"], g + 1)
                pe.wait_ge(s["k_sum_ready"], g + 1)
                for c in range(NT):
                    t = slice(c * P, (c + 1) * P)
                    mm = nc.tensor.matmul(bank_cols(0, c), k_sum[:, t], q[:, t], start=True, stop=True)
            elif j <= LEVELS:
                pe.wait_ge(s["Q_ready"], NQ * g + 2 * j + 2 * NQ)
                if j == 1:
                    pe.wait_ge(s["rt_ready"], g + CREDIT)
                    pe.wait_ge(s["gates_ready"], 4 * (g + 1))
                else:
                    pe.wait_ge(s["K_ready"], 2 * LEVELS * g + 2 * (j - 1) + 4 * LEVELS)
                    pe.wait_ge(s["A_merged"], 8 * g + j - 1)
                b = 1 << (j - 1)
                for c in range(NT):
                    t = slice(c * P, (c + 1) * P)
                    out = pairs(bank_cols(base, c), b)
                    nc.tensor.matmul(out[:, :, 1, :], k_f[:, t], pairs(Q_f[:, t], b)[:, :, 1, :], start=True, stop=True)
                    mm = nc.tensor.matmul(out[:, :, 0, :], k_b[:, t], pairs(Q_b[:, t], b)[:, :, 0, :], start=True, stop=True)
            elif j in (KTF, KTB):
                pe.wait_ge(s["A_merged"], 8 * g + j - 1)
                pe.wait_ge(s["K_ready"], 2 * LEVELS * g + 2 * LEVELS + 4 * LEVELS)
                K = (k_f, k_b)[j == KTB]
                for c in range(NT):
                    mm = nc.tensor.transpose(bank_cols(base, c), K[:, c * P:(c + 1) * P], C.ident[:])
            elif j == STATE:
                pe.wait_ge(s["Kt_ready"], 2 * g + 2)
                for n, (Kt, c) in enumerate([(Kt_f, c) for c in state_f] + [(Kt_b, c) for c in state_b]):
                    t = slice(c * P, (c + 1) * P)
                    mm = nc.tensor.matmul(Gc[:, n, :], Kt[:, t], v[:, t], start=True, stop=True)
            elif j == OUT:
                pe.wait_ge(s["S_ready"], 16 * (g + 1))
                pe.wait_ge(s["A_merged"], 8 * g + 8)
                pe.wait_ge(s["Q_ready"], NQ * g + NQ + 2 * NQ)
                for c in range(NT):
                    t = slice(c * P, (c + 1) * P)
                    terms = [(v[:, t], A[:, t])]
                    if c not in firsts_f:
                        terms.append((S_f[:, c, :], Q_f[:, t]))
                    if c not in firsts_b:
                        terms.append((S_b[:, c, :], Q_b[:, t]))
                    for n, (lhs, rhs) in enumerate(terms):
                        mm = nc.tensor.matmul(bank_cols(0, c), lhs, rhs, start=(n == 0), stop=(n == len(terms) - 1))
            else:
                pe.wait_ge(s["sq_ready"], g + 1)
                for a in range(0, T, 512):
                    z = min(a + 512, T)
                    mm = nc.tensor.matmul(G[:, 3 + a // 512, :, :].rearrange("p c t -> p (c t)")[:, 0:z - a],
                                          C.ones[:], sq[:, a:z], start=True, stop=True)
            mm.then_inc(s["gla_step"], 1)

        def pe_round(pe, r, g, project, gla):
            for t in range(len(order)):
                for part in range(PARTS):
                    if project:
                        W.multiply(nc, pe, r, t, part, h_hi, h_lo)
                    n = PARTS * t + part
                    if gla and n in after:
                        for j in after[n]:
                            pe_step(pe, g, j)
            if project:
                pe_values(pe, r)

        def act_gla(act, g, j):
            if j in (KTF, KTB):
                act.wait_ge(s["gla_step"], gla_at(g, j))
                Kt = (Kt_f, Kt_b)[j == KTB]
                base = 12 * (j % 2)
                nc.scalar.activation(Kt[:].rearrange("p (c t) -> p c t", t=P), Gc[:, base:base + NT, :],
                                     ACT.Copy).then_inc(s["Kt_ready"], 1)
            elif j == OUT:
                act.wait_ge(s["gla_step"], gla_at(g, OUT))
                nc.scalar.activation(sq[:].rearrange("p (c t) -> p c t", t=P), Gc[:, 0:NT, :],
                                     ACT.Square).then_inc(s["sq_ready"], 1)
            elif j == ONES:
                act.wait_ge(s["gla_step"], gla_at(g, ONES))
                nc.scalar.activation(rt[:].rearrange("p (c t) -> p c t", t=P), Gc[:, 12:12 + NT, :], ACT.Sqrt,
                                     bias=C.eps[:], scale=1.0 / P).then_inc(s["rt_ready"], 1)

        def act_round(act, r, g, project, gla):
            if project:
                W.split_hi(nc, act, r, 0)
            for t in range(len(order)):
                if project:
                    if t + 1 < len(order):
                        W.split_hi(nc, act, r, t + 1)
                    act_buffers(act, r, t)
                for part in range(PARTS):
                    if project:
                        act_move(act, r, t, part)
                    if gla:
                        for j in after.get(PARTS * t + part, ()):
                            act_gla(act, g, j)
            if project:
                act_values(act, r)

        def pool_round(pool, r, g, project, gla):
            levels = list(range(1, LEVELS + 1))
            if gla:
                pool.wait_ge(s["gates_ready"], 4 * (g + 1))
                pool.wait_ge(s["gla_step"], gla_at(g - 1, STATE))
                nc.gpsimd.tensor_tensor(k_sum[:], k_f[:], k_b[:], ALU.add).then_inc(s["k_sum_ready"], 1)
            for t in range(len(order)):
                if project:
                    W.split_lo(nc, pool, r, t)
                if not gla:
                    continue
                for j in levels[2 * t:2 * t + 2]:
                    pool_level(pool, g, j)

        def pool_level(pool, g, j):
            b = 1 << (j - 1)
            pool.wait_ge(s["gla_step"], gla_at(g, j))
            if j >= 2:
                pool.wait_ge(s["K_ready"], 2 * LEVELS * g + 2 * (j - 1) + 4 * LEVELS)
            pool.wait_ge(s["tot_ready"], 2 * (LEVELS * g + j))
            for K, F, tot, side in ((k_f, f_f, tot_f, 0), (k_b, f_b, tot_b, 1)):
                total = level_total(F, tot, j)
                half = pairs(K[:], b)[:, :, side, :]
                nc.gpsimd.tensor_tensor(half, half, over(total[:, :, 1 - side], b), ALU.mult).then_inc(s["K_ready"], 1)

        tot_at = [0]
        for l in range(1, LEVELS + 1):
            tot_at.append(tot_at[-1] + (T >> l))

        def total_of(F, tot, l):
            return F[:] if l == 0 else tot[:, tot_at[l - 1]:tot_at[l]]

        def level_total(F, tot, j):
            return total_of(F, tot, j - 1).rearrange("p (n two) -> p n two", two=2)

        def dve_start(dve, g):
            dve.wait_ge(s["gates_ready"], 4 * (g + 1))
            for b in range(2):
                dve.wait_ge(W.bank_free[b], PARTS // 2 * (W.per * g + TQ + 1) + CREDIT)
            dve.wait_ge(s["gla_step"], gla_at(g - 1, OUT))
            dve.wait_ge(s["rt_ready"], g + CREDIT)
            nc.vector.tensor_tensor(Q_f[:], q[:], f_f[:], ALU.mult).then_inc(s["Q_ready"], 1)
            nc.vector.tensor_tensor(Q_b[:], q[:], f_b[:], ALU.mult).then_inc(s["Q_ready"], 1)
            for l in range(1, LEVELS + 1):
                if l >= 2:
                    dve.wait_ge(s["tot_ready"], 2 * (LEVELS * g + l - 1))
                for F, tot in ((f_f, tot_f), (f_b, tot_b)):
                    two = level_total(F, tot, l)
                    nc.vector.tensor_tensor(total_of(F, tot, l), two[:, :, 0], two[:, :, 1], ALU.mult).then_inc(s["tot_ready"], 1)

        def dve_merge(dve, g, j):
            if j == DIAG:
                dve.wait_ge(s["A_clear"], 1)
            else:
                dve.wait_ge(s["A_merged"], 8 * g + j)
            dve.wait_ge(s["gla_step"], gla_at(g, j))
            st.stand(dve)
            for out, c0, c1 in spans(3 * (j % 2)):
                n = c1 - c0
                cp = nc.vector.copy_predicated(A[:, c0 * P:c1 * P].rearrange("p (c t) -> p c t", t=P),
                                               C.mask[:, j, :].unsqueeze(1).broadcast_to([P, n, P]), out)
            cp.then_inc(s["A_merged"], 1)

        def dve_level(dve, g, j):
            b = 1 << (j - 1)
            dve.wait_ge(s["Q_ready"], NQ * g + 2 * j + 2 * NQ)
            for Q, F, tot, side in ((Q_f, f_f, tot_f, 1), (Q_b, f_b, tot_b, 0)):
                total = level_total(F, tot, j)
                half = pairs(Q[:], b)[:, :, side, :]
                nc.vector.tensor_tensor(half, half, over(total[:, :, 1 - side], b), ALU.mult).then_inc(s["Q_ready"], 1)

        def dve_states(dve, g):
            dve.wait_ge(s["gla_step"], gla_at(g, STATE))
            totf, totb = total_of(f_f, tot_f, LEVELS), total_of(f_b, tot_b, LEVELS)
            runs = [(n, c, c + 1, S_f, totf, c in firsts_f) for n, c in enumerate(state_f)]
            runs += [(n + len(state_f), c, c - 1, S_b, totb, c in firsts_b) for n, c in enumerate(state_b)]
            half = len(state_f)
            for i in range(half):
                for n, c, to, S, tot, first in (runs[i], runs[i + half]):
                    done = 2 * i + (S is S_b)
                    if not first:
                        dve.wait_ge(s["S_ready"], 16 * g + done - 1)
                    if first:
                        nc.vector.tensor_copy(S[:, to, :], Gc[:, n, :]).then_inc(s["S_ready"], 1)
                    else:
                        nc.vector.scalar_tensor_tensor(out=S[:, to, :], in0=S[:, c, :], scalar=tot[:, c:c + 1],
                                                       in1=Gc[:, n, :], op0=ALU.mult, op1=ALU.add).then_inc(s["S_ready"], 1)

        def dve_output(dve, g):
            dve.wait_ge(s["rt_ready"], g + 1 + CREDIT)
            nc.vector.reciprocal(rt[:], rt[:]).then_inc(s["y_ready"], 1)
            dve.wait_ge(s["y_ready"], NY * g + 1 + CREDIT)
            dve.wait_ge(s["y_stored"], 16 * (g + CREDIT))
            y3, rt3 = (x[:].rearrange("p (c t) -> p c t", t=P) for x in (y, rt))
            nc.vector.scalar_tensor_tensor(out=y[:], in0=rt[:], scalar=C.onorm[:], in1=so[:], op0=ALU.mult,
                                           op1=ALU.mult).then_inc(s["y_ready"], 1)
            dve.wait_ge(s["y_ready"], NY * g + 2 + CREDIT)
            nc.vector.tensor_tensor(y3, Gc[:, 0:NT, :], y3, ALU.mult).then_inc(s["y_ready"], 1)

        def dve_round(dve, r, g, project, gla):
            if gla:
                dve_start(dve, g)
                for j in range(LEVELS + 1):
                    dve_merge(dve, g, j)
                    if j:
                        dve_level(dve, g, j)
                dve_states(dve, g)
                dve_output(dve, g)
            if project:
                dve_project(dve, r)
                dve_output_gate(dve, r)

        with st.block() as block:

            @block.sync
            def _(sp):
                sp.sem_inc(s["y_stored"], 16 * CREDIT)
                sp_round(sp, 0)
                with sp.Fori(0, HEADS - 1) as g:
                    sp_round(sp, g + 1)
                    store(sp, g)
                store(sp, HEADS - 1)
                sp.wait_ge(s["y_stored"], 16 * (HEADS + CREDIT))

            @block.scalar
            def _(act):
                W.act_credit(act)
                act.sem_inc(s["rt_ready"], CREDIT)
                act_round(act, 0, None, True, False)
                with act.Fori(0, HEADS - 1) as g:
                    act_round(act, g + 1, g, True, True)
                act_round(act, None, HEADS - 1, False, True)

            @block.gpsimd
            def _(pool):
                W.pool_credit(pool)
                pool.sem_inc(s["K_ready"], 4 * LEVELS)
                nc.gpsimd.memset(A[:], 0.0).then_inc(s["A_clear"], 1)
                pool_round(pool, 0, None, True, False)
                with pool.Fori(0, HEADS - 1) as g:
                    pool_round(pool, g + 1, g, True, True)
                pool_round(pool, None, HEADS - 1, False, True)

            @block.tensor
            def _(pe):
                W.pe_credit(pe)
                pe.sem_inc(s["gla_step"], 2 * STEPS)
                pe.sem_inc(s["v_step"], CREDIT)
                pe_round(pe, 0, None, True, False)
                with pe.Fori(0, HEADS - 1) as g:
                    pe_round(pe, g + 1, g, True, True)
                pe_round(pe, None, HEADS - 1, False, True)

            @block.vector
            def _(dve):
                dve.sem_inc(s["Q_ready"], 2 * NQ)
                dve.sem_inc(s["y_ready"], CREDIT)
                dve_round(dve, 0, None, True, False)
                with dve.Fori(0, HEADS - 1) as g:
                    dve_round(dve, g + 1, g, True, True)
                dve_round(dve, None, HEADS - 1, False, True)


def chunks(ap):
    return ap.rearrange("p (c t) -> p c t", t=P)


def gmlp(nc, C, w_in, w_s, b_s, h_hi, h_lo, ya_dram):
    PER, ROUNDS = 2, GROUPS // 2
    with Stage(nc, "gm") as st:
        W = WeightStream(st, PER)
        v = st.sb("v", [P, GROUPS, T])
        act_out = [st.sb(f"act_out{t}", [P, T]) for t in range(PER)]
        vn = [st.sb(f"vn{t}", [P, T]) for t in range(PER)]
        ya = [st.sb(f"ya{t}", [P, T]) for t in range(PER)]
        sq = ya
        ws = [st.sb(f"ws{t}", [P, P]) for t in range(PER)]
        wsT = [st.sb(f"wsT{t}", [P, P]) for t in range(PER)]
        bias = [st.sb(f"bias{t}", [P, P]) for t in range(PER)]
        ssq = st.sb("ssq", [P, GROUPS, NT])
        var, std, rstd = (st.sb(n, [P, NT]) for n in ("var", "std", "rstd"))
        G = st.ps("G", [P, 6, 4, P])
        Gc = G[:].rearrange("p b c t -> p (b c) t")
        s = {n: st.sem(n) for n in ("v_turned", "v_copied", "v_squared", "v_summed", "var_ready", "std_ready",
                                    "rstd_ready", "vn_ready", "ws_turned", "wsT_ready", "mixed", "mix_scaled",
                                    "ya_ready")}
        ws_loaded = [st.sem(f"ws_loaded{t}") for t in range(PER)]
        bias_loaded = [st.sem(f"bias_loaded{t}") for t in range(PER)]
        ya_stored = [st.sem(f"ya_stored{t}") for t in range(PER)]

        def bank_set(t):
            return Gc[:, 12 * t:12 * t + NT, :], Gc[:, 12 * t + NT, :]

        def pe_turn_v(pe, r, t):
            n = PER * r + t
            W.moved(pe, r, t)
            pe.wait_ge(s["v_copied"], n - 1 + CREDIT)
            out, _ = bank_set(t)
            for c in range(NT):
                mm = nc.tensor.transpose(out[:, c, :], act_out[t][:, c * P:(c + 1) * P], C.ident[:])
            mm.then_inc(s["v_turned"], 1)

        def pe_v_round(pe, r, first):
            for t in range(PER):
                for part in range(PARTS):
                    W.multiply(nc, pe, r, t, part, h_hi, h_lo)
                    if part == 1 and not (first and t == 0):
                        pe_turn_v(pe, *((r, 0) if t == 1 else (r - 1, 1)))

        def act_move(act, r, t):
            for part in range(PARTS):
                out, free = W.result(act, r, t, part)
                nc.scalar.activation(act_out[t][:, part * PART:(part + 1) * PART], out,
                                     ACT.Gelu_apprx_tanh).then_inc(free, 1)

        def act_v_round(act, r):
            for t in range(PER):
                W.split_hi(nc, act, r + t, (t + 1) % PER)
                act.wait_ge(s["v_turned"], PER * r + t - 1 + CREDIT)
                act_move(act, r, t)

        def dve_v_round(dve, r):
            for t in range(PER):
                n = PER * r + t
                dve.wait_ge(s["v_turned"], n + 1 + CREDIT)
                out, _ = bank_set(t)
                nc.vector.tensor_copy(chunks(v[:, bass.ds(n, 1), :].rearrange("p a t -> p (a t)")), out).then_inc(s["v_copied"], 1)
                dve.wait_ge(s["v_squared"], n + 1)
                nc.vector.tensor_reduce(ssq[:, bass.ds(n, 1), :].rearrange("p a c -> p (a c)"), chunks(sq[t][:]),
                                        AX.X, ALU.add).then_inc(s["v_summed"], 1)

        def pool_v_round(pool, r):
            for t in range(PER):
                n = PER * r + t
                pool_split(pool, r + t, (t + 1) % PER)
                pool.wait_ge(s["v_copied"], n + 1 + CREDIT)
                pool.wait_ge(s["v_summed"], n - 1 + CREDIT)
                src = v[:, bass.ds(n, 1), :].rearrange("p a t -> p (a t)")
                nc.gpsimd.tensor_tensor(sq[t][:], src, src, ALU.mult).then_inc(s["v_squared"], 1)

        def pool_split(pool, r, t):
            W.split_lo(nc, pool, r, t)

        def sp_u_round(sp, i):
            for t in range(PER):
                n = PER * i + t
                W.load(sp, ROUNDS + i, t, cols(w_in, COL_U + n * P))
                sp.wait_ge(s["ws_turned"], n - 1 + CREDIT)
                st.stand(sp)
                sp.dma_start(ws[t][:], w_s[bass.ds(n, 1)].rearrange("g t s -> (g t) s")).then_inc(ws_loaded[t], 16)
                sp.wait_ge(s["mix_scaled"], n - 1 + CREDIT)
                st.stand(sp)
                sp.dma_start(bias[t][:], b_s[bass.ds(n, 1), :].broadcast_to([P, P])).then_inc(bias_loaded[t], 16)

        def sp_store(sp, i):
            for t in range(PER):
                n = PER * i + t
                sp.wait_ge(s["ya_ready"], n + 1 + CREDIT)
                st.stand(sp)
                sp.dma_start(ya_dram[bass.ds(n * P, P), :], ya[t][:]).then_inc(ya_stored[t], 16)

        def pe_u_round(pe, i):
            for t in range(PER):
                n = PER * i + t
                out, turned = bank_set(t)
                for part in range(PARTS):
                    W.multiply(nc, pe, ROUNDS + i, t, part, h_hi, h_lo)
                    if part == 0:
                        pe.wait_ge(ws_loaded[t], 16 * (i + 1))
                        pe.wait_ge(s["wsT_ready"], n - 1 + CREDIT)
                        nc.tensor.transpose(turned, ws[t][:], C.ident[:]).then_inc(s["ws_turned"], 1)
                    if part == 2:
                        pe.wait_ge(s["wsT_ready"], n + 1 + CREDIT)
                        pe.wait_ge(s["vn_ready"], n + 1)
                        pe.wait_ge(s["mix_scaled"], n - 1 + CREDIT)
                        for c in range(NT):
                            mm = nc.tensor.matmul(out[:, c, :], vn[t][:, c * P:(c + 1) * P], wsT[t][:], start=True, stop=True)
                        mm.then_inc(s["mixed"], 1)

        def act_u_round(act, i, last):
            for t in range(PER):
                n = PER * i + t
                if not (last and t == PER - 1):
                    W.split_hi(nc, act, ROUNDS + i + t, (t + 1) % PER)
                _, turned = bank_set(t)
                act.wait_ge(s["ws_turned"], n + 1 + CREDIT)
                act.wait_ge(s["mixed"], n - 1 + CREDIT)
                nc.scalar.activation(wsT[t][:], turned, ACT.Copy).then_inc(s["wsT_ready"], 1)
                act.wait_ge(s["ya_ready"], n - 1 + CREDIT)
                act_move(act, ROUNDS + i, t)

        def dve_u_round(dve, i):
            for t in range(PER):
                n = PER * i + t
                out, _ = bank_set(t)
                dve.wait_ge(s["mixed"], n - 1 + CREDIT)
                vg = chunks(v[:, bass.ds(n, 1), :].rearrange("p a t -> p (a t)"))
                nc.vector.tensor_tensor(chunks(vn[t][:]), vg, over(rstd[:], P), ALU.mult).then_inc(s["vn_ready"], 1)
                dve.wait_ge(s["mixed"], n + 1 + CREDIT)
                dve.wait_ge(bias_loaded[t], 16 * (i + 1))
                dve.wait_ge(ya_stored[t], 16 * (i + CREDIT))
                nc.vector.scalar_tensor_tensor(out=chunks(ya[t][:]), in0=out, scalar=C.vnorm[:, bass.ds(n, 1)],
                                               in1=bias[t][:].unsqueeze(1).broadcast_to([P, NT, P]),
                                               op0=ALU.mult, op1=ALU.add).then_inc(s["mix_scaled"], 1)
                W.moved(dve, ROUNDS + i, t)
                dve.wait_ge(s["mix_scaled"], n + 1 + CREDIT)
                nc.vector.tensor_tensor(ya[t][:], ya[t][:], act_out[t][:], ALU.mult).then_inc(s["ya_ready"], 1)

        with st.block() as block:

            @block.sync
            def _(sp):
                for t in range(PER):
                    sp.sem_inc(ya_stored[t], 16 * CREDIT)
                with sp.Fori(0, ROUNDS) as r:
                    for t in range(PER):
                        W.load(sp, r, t, cols(w_in, COL_V + (PER * r + t) * P))
                sp_u_round(sp, 0)
                with sp.Fori(1, ROUNDS) as i:
                    sp_u_round(sp, i)
                    sp_store(sp, i - 1)
                sp_store(sp, ROUNDS - 1)
                for t in range(PER):
                    sp.wait_ge(ya_stored[t], 16 * (ROUNDS + CREDIT))

            @block.scalar
            def _(act):
                W.act_credit(act)
                act.sem_inc(s["wsT_ready"], CREDIT)
                W.split_hi(nc, act, 0, 0)
                with act.Fori(0, ROUNDS) as r:
                    act_v_round(act, r)
                act.wait_ge(s["var_ready"], 1)
                nc.scalar.activation(std[:], var[:], ACT.Sqrt).then_inc(s["std_ready"], 1)
                with act.Fori(0, ROUNDS - 1) as i:
                    act_u_round(act, i, False)
                act_u_round(act, ROUNDS - 1, True)

            @block.gpsimd
            def _(pool):
                W.pool_credit(pool)
                W.split_lo(nc, pool, 0, 0)
                with pool.Fori(0, ROUNDS) as r:
                    pool_v_round(pool, r)
                with pool.Fori(0, ROUNDS - 1) as i:
                    for t in range(PER):
                        pool_split(pool, ROUNDS + i + t, (t + 1) % PER)
                pool_split(pool, 2 * ROUNDS - 1, 1)

            @block.tensor
            def _(pe):
                W.pe_credit(pe)
                for n in ("v_turned", "ws_turned", "mixed"):
                    pe.sem_inc(s[n], CREDIT)
                pe_v_round(pe, 0, True)
                with pe.Fori(1, ROUNDS) as r:
                    pe_v_round(pe, r, False)
                pe_turn_v(pe, ROUNDS - 1, 1)
                with pe.Fori(0, ROUNDS) as i:
                    pe_u_round(pe, i)

            @block.vector
            def _(dve):
                for n in ("v_copied", "v_summed", "mix_scaled", "ya_ready"):
                    dve.sem_inc(s[n], CREDIT)
                with dve.Fori(0, ROUNDS) as r:
                    dve_v_round(dve, r)
                dve.wait_ge(s["v_summed"], GROUPS + CREDIT)
                nc.vector.tensor_reduce(var[:], ssq[:].rearrange("p g c -> p c g"), AX.X, ALU.add).then_inc(s["rstd_ready"], 1)
                dve.wait_ge(s["rstd_ready"], 1)
                nc.vector.tensor_scalar(var[:], var[:], 1.0 / D, EPS, ALU.mult, ALU.add).then_inc(s["var_ready"], 1)
                dve.wait_ge(s["std_ready"], 1)
                nc.vector.reciprocal(rstd[:], std[:]).then_inc(s["rstd_ready"], 1)
                dve.wait_ge(s["rstd_ready"], 2)
                with dve.Fori(0, ROUNDS) as i:
                    dve_u_round(dve, i)


def split_rows(nc, st, sp=None, act=None, pool=None, dve=None, S=None):
    src, raw, hi, lo, loaded, hi_ready, lo_even, lo_odd = S
    for k in range(KC):
        b = k % 2
        if sp is not None:
            if k >= 2:
                sp.wait_ge(hi_ready, k - 1)
                sp.wait_ge((lo_even, lo_odd)[b], k // 2)
            sp.dma_start(raw[b][:], src[k * P:(k + 1) * P, :]).then_inc(loaded[b], 16)
        if act is not None:
            act.wait_ge(loaded[b], 16 * (k // 2 + 1))
            nc.scalar.activation(hi[:, k, :], raw[b][:], ACT.Copy).then_inc(hi_ready, 1)
        if pool is not None and b == 0:
            pool.wait_ge(hi_ready, k + 1)
            nc.gpsimd.tensor_tensor(lo[:, k, :], raw[b][:], hi[:, k, :].bitcast(F32), ALU.subtract).then_inc(lo_even, 1)
        if dve is not None and b == 1:
            dve.wait_ge(hi_ready, k + 1)
            nc.vector.tensor_tensor(lo[:, k, :], raw[b][:], hi[:, k, :].bitcast(F32), ALU.subtract).then_inc(lo_odd, 1)


def merge(nc, name, w_in, col_gate, w_branch, y_dram, m_in, m_out, h_hi, h_lo):
    PER = 2
    GATE, BRANCH = 0, 1
    with Stage(nc, name) as st:
        W = WeightStream(st, PER)
        y_hi = st.sb("y_hi", [P, KC, T], F32R)
        y_lo = st.sb("y_lo", [P, KC, T], F32R)
        sg, m, m_prev = (st.sb(n, [P, T]) for n in ("sg", "m", "m_prev"))
        s = {n: st.sem(n) for n in ("y_hi_ready", "y_lo_even", "y_lo_odd", "added", "m_stored", "m_prev_loaded")}
        S = (y_dram, (m, m_prev), y_hi, y_lo, [st.sem("y_loaded0"), st.sem("y_loaded1")],
             s["y_hi_ready"], s["y_lo_even"], s["y_lo_odd"])
        adds = m_in is not None

        def sp_round(sp, r):
            W.load(sp, r, GATE, cols(w_in, col_gate + r * P))
            W.load(sp, r, BRANCH, cols(w_branch, r * P))

        def sp_tail(sp, r):
            if adds:
                sp.wait_ge(s["added"], PARTS * (r + 1) + PARTS * CREDIT)
            else:
                W.moved(sp, r, BRANCH)
            sp.dma_start(m_out[bass.ds(r * P, P), :], m[:]).then_inc(s["m_stored"], 16)

        def sp_prev(sp, r):
            if adds:
                sp.wait_ge(s["added"], PARTS * (r + CREDIT))
                st.stand(sp)
                sp.dma_start(m_prev[:], m_in[bass.ds(r * P, P), :]).then_inc(s["m_prev_loaded"], 16)

        def act_round(act, r, last):
            W.split_hi(nc, act, r, BRANCH)
            W.moved(act, r - 1, BRANCH)
            for part in range(PARTS):
                out, free = W.result(act, r, GATE, part)
                nc.scalar.activation(sg[:, part * PART:(part + 1) * PART], out, ACT.Sigmoid).then_inc(free, 1)
            if not last:
                W.split_hi(nc, act, r + 1, GATE)

        def dve_round(dve, r):
            W.moved(dve, r, GATE)
            dve.wait_ge(s["m_stored"], 16 * (r + CREDIT))
            if adds:
                dve.wait_ge(s["m_prev_loaded"], 16 * (r + 1))
            for part in range(PARTS):
                c = slice(part * PART, (part + 1) * PART)
                out, free = W.result(dve, r, BRANCH, part)
                nc.vector.tensor_tensor(m[:, c], out, sg[:, c], ALU.mult).then_inc(free, 1)
                if adds:
                    W_done = PARTS // 2 * (PER * r + BRANCH) + part // 2 + 1 + CREDIT
                    dve.wait_ge(W.bank_free[(PARTS * BRANCH + part) % 2], W_done)
                    nc.vector.tensor_tensor(m[:, c], m[:, c], m_prev[:, c], ALU.add).then_inc(s["added"], 1)

        with st.block() as block:

            @block.sync
            def _(sp):
                sp.sem_inc(s["m_stored"], 16 * CREDIT)
                sp_round(sp, 0)
                split_rows(nc, st, sp=sp, S=S)
                sp.wait_ge(s["y_hi_ready"], KC)
                sp.wait_ge(s["y_lo_odd"], KC // 2)
                sp_prev(sp, 0)
                with sp.Fori(1, KC) as r:
                    sp_round(sp, r)
                    sp_tail(sp, r - 1)
                    sp_prev(sp, r)
                sp_tail(sp, KC - 1)
                sp.wait_ge(s["m_stored"], 16 * (KC + CREDIT))

            @block.scalar
            def _(act):
                W.act_credit(act)
                W.split_hi(nc, act, 0, GATE)
                split_rows(nc, st, act=act, S=S)
                with act.Fori(0, KC - 1) as r:
                    act_round(act, r, False)
                act_round(act, KC - 1, True)

            @block.gpsimd
            def _(pool):
                W.pool_credit(pool)
                W.split_lo(nc, pool, 0, GATE)
                split_rows(nc, st, pool=pool, S=S)
                W.split_lo(nc, pool, 0, BRANCH)
                with pool.Fori(1, KC) as r:
                    W.split_lo(nc, pool, r, GATE)
                    W.split_lo(nc, pool, r, BRANCH)

            @block.tensor
            def _(pe):
                W.pe_credit(pe)

                def pe_round(r):
                    for part in range(PARTS):
                        W.multiply(nc, pe, r, GATE, part, h_hi, h_lo)
                    pe.wait_ge(s["y_lo_even"], KC // 2)
                    pe.wait_ge(s["y_lo_odd"], KC // 2)
                    for part in range(PARTS):
                        W.multiply(nc, pe, r, BRANCH, part, y_hi, y_lo)

                with pe.Fori(0, KC) as r:
                    pe_round(r)

            @block.vector
            def _(dve):
                dve.sem_inc(s["added"], PARTS * CREDIT)
                split_rows(nc, st, dve=dve, S=S)
                dve.wait_ge(s["y_hi_ready"], KC)
                dve.wait_ge(s["y_lo_even"], KC // 2)
                with dve.Fori(0, KC) as r:
                    dve_round(dve, r)


def residual(nc, C, x_prompt, x_sample, w_out, m_dram, x2):
    PER, ROUNDS = 2, KC // 2
    with Stage(nc, "wo") as st:
        W = WeightStream(st, PER)
        m_hi = st.sb("m_hi", [P, KC, T], F32R)
        m_lo = st.sb("m_lo", [P, KC, T], F32R)
        o = [st.sb(f"o{t}", [P, T]) for t in range(PER)]
        G = st.ps("G", [P, 6, 4, P])
        Gc = G[:].rearrange("p b c t -> p (b c) t")
        s = {n: st.sem(n) for n in ("m_hi_ready", "m_lo_even", "m_lo_odd", "turned", "added", "x_loaded")}
        S = (m_dram, o, m_hi, m_lo, [st.sem("m_loaded0"), st.sem("m_loaded1")],
             s["m_hi_ready"], s["m_lo_even"], s["m_lo_odd"])

        def pe_turn(pe, r, t):
            W.moved(pe, r, t)
            pe.wait_ge(s["added"], PER * r + t - 1 + CREDIT)
            for c in range(NT):
                mm = nc.tensor.transpose(Gc[:, 12 * t + c, :], o[t][:, c * P:(c + 1) * P], C.ident[:])
            mm.then_inc(s["turned"], 1)

        def pe_round(pe, r, first):
            for t in range(PER):
                for part in range(PARTS):
                    W.multiply(nc, pe, r, t, part, m_hi, m_lo)
                    if part == 1 and not (first and t == 0):
                        pe_turn(pe, *((r, 0) if t == 1 else (r - 1, 1)))

        def act_round(act, r, last):
            for t in range(PER):
                if not (last and t == PER - 1):
                    W.split_hi(nc, act, r + t, (t + 1) % PER)
                act.wait_ge(s["turned"], PER * r + t - 1 + CREDIT)
                for part in range(PARTS):
                    out, free = W.result(act, r, t, part)
                    nc.scalar.activation(o[t][:, part * PART:(part + 1) * PART], out, ACT.Copy).then_inc(free, 1)

        with st.block() as block:

            @block.sync
            def _(sp):
                for t in range(PER):
                    W.load(sp, 0, t, cols(w_out, t * P))
                split_rows(nc, st, sp=sp, S=S)
                sp.dma_start(x2[:, 0:NT_PROMPT, :], x_prompt.rearrange("b (t p) d -> p (b t) d", p=P)).then_inc(s["x_loaded"], 16)
                sp.dma_start(x2[:, NT_PROMPT:NT, :], x_sample.rearrange("b (t p) d -> p (b t) d", p=P)).then_inc(s["x_loaded"], 16)
                with sp.Fori(1, ROUNDS) as r:
                    for t in range(PER):
                        W.load(sp, r, t, cols(w_out, (PER * r + t) * P))

            @block.scalar
            def _(act):
                W.act_credit(act)
                W.split_hi(nc, act, 0, 0)
                split_rows(nc, st, act=act, S=S)
                act.wait_ge(s["m_lo_even"], KC // 2)
                act.wait_ge(s["m_lo_odd"], KC // 2)
                with act.Fori(0, ROUNDS - 1) as r:
                    act_round(act, r, False)
                act_round(act, ROUNDS - 1, True)

            @block.gpsimd
            def _(pool):
                W.pool_credit(pool)
                W.split_lo(nc, pool, 0, 0)
                split_rows(nc, st, pool=pool, S=S)
                W.split_lo(nc, pool, 0, 1)
                with pool.Fori(1, ROUNDS) as r:
                    for t in range(PER):
                        W.split_lo(nc, pool, r, t)

            @block.tensor
            def _(pe):
                W.pe_credit(pe)
                pe.sem_inc(s["turned"], CREDIT)
                pe.wait_ge(s["m_lo_even"], KC // 2)
                pe.wait_ge(s["m_lo_odd"], KC // 2)
                pe_round(pe, 0, True)
                with pe.Fori(1, ROUNDS) as r:
                    pe_round(pe, r, False)
                pe_turn(pe, ROUNDS - 1, 1)

            @block.vector
            def _(dve):
                dve.sem_inc(s["added"], CREDIT)
                split_rows(nc, st, dve=dve, S=S)
                dve.wait_ge(s["x_loaded"], 32)
                with dve.Fori(0, ROUNDS) as r:
                    for t in range(PER):
                        n = PER * r + t
                        dve.wait_ge(s["turned"], n + 1 + CREDIT)
                        x = x2[:, :, bass.ds(n * P, P)]
                        nc.vector.tensor_tensor(x, Gc[:, 12 * t:12 * t + NT, :], x, ALU.add).then_inc(s["added"], 1)


def route(nc, C, norm2_g, w_router, x2, x3, h2, aff):
    with Stage(nc, "rt") as st:
        gain, junk = st.sb("gain", [P, D]), st.sb("junk", [P, D])
        wr = st.sb("wr", [P, KC, NE])
        h = [st.sb(f"h{b}", [P, D]) for b in range(2)]
        hT = [st.sb(f"hT{b}", [P, KC, P]) for b in range(2)]
        small = {n: st.sb(n, [P, 2]) for n in ("ssq", "var", "std", "rstd", "neg_max", "total", "inv")}
        expo, prob = st.sb("expo", [P, 2, NE]), st.sb("prob", [P, 2, NE])
        turned = st.ps("turned", [P, 2, KC, P])
        logits = st.ps("logits", [P, 2, 512])
        affT = st.ps("affT", [P, 2, 512])
        s = {n: st.sem(n) for n in ("loaded", "x3_stored", "ssq_ready", "var_ready", "std_ready", "rstd_ready",
                                    "h_ready", "h_turned", "hT_ready", "logits_ready", "max_ready", "exp_ready",
                                    "inv_ready", "prob_ready", "aff_turned", "aff_ready")}
        h_stored = [st.sem(f"h_stored{b}") for b in range(2)]

        def tile_of(x, t):
            return x[:, bass.ds(t, 1), :].rearrange("p a d -> p (a d)")

        with st.block() as block:

            @block.sync
            def _(sp):
                for b in range(2):
                    sp.sem_inc(h_stored[b], 16 * CREDIT)
                sp.dma_start(gain[:], norm2_g.broadcast_to([P, D])).then_inc(s["loaded"], 16)
                sp.dma_start(wr[:], w_router.rearrange("(k p) e -> p k e", p=P)).then_inc(s["loaded"], 16)
                for dst, a, z in ((x3[0], 0, NT_PROMPT), (x3[1], NT_PROMPT, NT)):
                    sp.dma_start(dst.rearrange("(t p) d -> p t d", p=P), x2[:, a:z, :]).then_inc(s["x3_stored"], 16)
                for b in range(2):
                    sp.wait_ge(s["h_ready"], b + 1 + CREDIT)
                    sp.dma_start(h2[0][b * P:(b + 1) * P, :], h[b][:]).then_inc(h_stored[b], 16)
                with sp.Fori(0, NT // 2 - 1) as i:
                    for b in range(2):
                        sp.wait_ge(s["h_ready"], 2 * i + b + 3 + CREDIT)
                        st.stand(sp)
                        sp.dma_start(h2[1][bass.ds((2 * i + b) * P, P), :], h[b][:]).then_inc(h_stored[b], 16)
                sp.wait_ge(s["x3_stored"], 32)
                for b in range(2):
                    sp.wait_ge(h_stored[b], 16 * (NT // 2 + CREDIT))

            @block.scalar
            def _(act):
                act.sem_inc(s["hT_ready"], CREDIT)
                act.sem_inc(s["ssq_ready"], CREDIT)
                with act.Fori(0, NT // 2) as i:
                    for b in range(2):
                        n = 2 * i + b
                        act.wait_ge(s["ssq_ready"], n + CREDIT)
                        act.wait_ge(s["var_ready"], n - 1 + CREDIT)
                        st.stand(act)
                        nc.scalar.activation(junk[:], tile_of(x2, n), ACT.Square,
                                             accum_out=small["ssq"][:, b:b + 1]).then_inc(s["ssq_ready"], 1)
                        act.wait_ge(s["var_ready"], n + 1 + CREDIT)
                        nc.scalar.activation(small["std"][:, b:b + 1], small["var"][:, b:b + 1], ACT.Sqrt).then_inc(s["std_ready"], 1)
                    for b in range(2):
                        n = 2 * i + b
                        act.wait_ge(s["h_turned"], n + 1)
                        act.wait_ge(s["logits_ready"], n - 1 + CREDIT)
                        nc.scalar.activation(hT[b][:], turned[:, b], ACT.Copy).then_inc(s["hT_ready"], 1)
                    for b in range(2):
                        n = 2 * i + b
                        act.wait_ge(s["max_ready"], n + 1)
                        nc.scalar.activation(expo[:, b, :], logits[:, b, 0:NE], ACT.Exp, bias=small["neg_max"][:, b:b + 1],
                                             accum_out=small["total"][:, b:b + 1]).then_inc(s["exp_ready"], 1)

            @block.tensor
            def _(pe):
                pe.sem_inc(s["logits_ready"], CREDIT)
                with pe.Fori(0, NT // 2) as i:
                    for b in range(2):
                        n = 2 * i + b
                        pe.wait_ge(s["h_ready"], n + 1 + CREDIT)
                        pe.wait_ge(s["hT_ready"], n - 1 + CREDIT)
                        for k in range(KC):
                            mm = nc.tensor.transpose(turned[:, b, k, :], h[b][:, k * P:(k + 1) * P], C.ident[:])
                        mm.then_inc(s["h_turned"], 1)
                    for b in range(2):
                        n = 2 * i + b
                        pe.wait_ge(s["hT_ready"], n + 1 + CREDIT)
                        pe.wait_ge(s["prob_ready"], n - 1 + CREDIT)
                        for k in range(KC):
                            mm = nc.tensor.matmul(logits[:, b, 0:NE], hT[b][:, k, :], wr[:, k, :], start=(k == 0), stop=(k == KC - 1))
                        mm.then_inc(s["logits_ready"], 1)
                    for b in range(2):
                        n = 2 * i + b
                        pe.wait_ge(s["prob_ready"], n + 1 + CREDIT)
                        pe.wait_ge(s["aff_ready"], n - 1 + CREDIT)
                        nc.tensor.transpose(affT[0:NE, b, 0:P], prob[:, b, :], C.ident[:]).then_inc(s["aff_turned"], 1)

            @block.vector
            def _(dve):
                for n in ("var_ready", "h_ready", "prob_ready", "aff_ready"):
                    dve.sem_inc(s[n], CREDIT)
                dve.wait_ge(s["loaded"], 32)
                with dve.Fori(0, NT // 2) as i:
                    for b in range(2):
                        n = 2 * i + b
                        one = {k: a[:, b:b + 1] for k, a in small.items()}
                        dve.wait_ge(s["ssq_ready"], n + 1 + CREDIT)
                        nc.vector.tensor_scalar(one["var"], one["ssq"], 1.0 / D, EPS, ALU.mult, ALU.add).then_inc(s["var_ready"], 1)
                        dve.wait_ge(s["std_ready"], n + 1)
                        nc.vector.reciprocal(one["rstd"], one["std"]).then_inc(s["rstd_ready"], 1)
                        dve.wait_ge(s["rstd_ready"], n + 1)
                        dve.wait_ge(h_stored[b], 16 * (i + CREDIT))
                        nc.vector.scalar_tensor_tensor(out=h[b][:], in0=tile_of(x2, n), scalar=one["rstd"], in1=gain[:],
                                                       op0=ALU.mult, op1=ALU.mult).then_inc(s["h_ready"], 1)
                    for b in range(2):
                        n = 2 * i + b
                        one = {k: a[:, b:b + 1] for k, a in small.items()}
                        dve.wait_ge(s["logits_ready"], n + 1 + CREDIT)
                        nc.vector.tensor_reduce(one["neg_max"], logits[:, b, 0:NE], AX.X, ALU.max, negate=True).then_inc(s["max_ready"], 1)
                        dve.wait_ge(s["exp_ready"], n + 1)
                        nc.vector.reciprocal(one["inv"], one["total"]).then_inc(s["inv_ready"], 1)
                        dve.wait_ge(s["inv_ready"], n + 1)
                        nc.vector.tensor_scalar(prob[:, b, :], expo[:, b, :], one["inv"], None, ALU.mult).then_inc(s["prob_ready"], 1)
                    for b in range(2):
                        n = 2 * i + b
                        dve.wait_ge(s["aff_turned"], n + 1)
                        nc.vector.tensor_copy(aff[:, bass.ds(n * P, P)], affT[0:NE, b, 0:P]).then_inc(s["aff_ready"], 1)


def experts(nc, C, aff, h2, x3, w_g, w_u, w_d):
    WAVES_S, WAVES_P = CAP_S // 8, CAP_P // 8
    TILES = 3 * KC
    FIRST_DOWN = 2 * KC
    WIDTH = 2 * P
    PIECES = 3 * D // WIDTH
    RAW = PIECES // 2
    FIRST_DOWN_PIECE = 2 * D // WIDTH
    RING, BANKS = 12, 3
    AHEAD = 10
    DVE_AHEAD = 6
    BANKX = 3
    CR = TILES
    TURN_X = FIRST_DOWN + 2
    ADD, GATHER = 1, 3

    def piece_of(t):
        if t < FIRST_DOWN:
            j, which = t // 2, t % 2
            return 2 * (j // 2) + which, (j % 2) * P
        j = t - FIRST_DOWN
        return FIRST_DOWN_PIECE + j // 2, (j % 2) * P

    def lo_done(e, t):
        return s["w_lo_pool"] if t % 2 else s["w_lo_dve"], TILES // 2 * e + t // 2 + 1

    with Stage(nc, "ex") as st:
        work_s, work_p = st.sb("work_s", [NE, T_SAMPLE]), st.sb("work_p", [NE, T_PROMPT])
        val_s, val_p = st.sb("val_s", [NE, CAP_S]), st.sb("val_p", [NE, CAP_P])
        idx_s, idx_p = st.sb("idx_s", [NE, CAP_S], U32), st.sb("idx_p", [NE, CAP_P], U32)
        idxf_s, idxf_p = st.sb("idxf_s", [NE, CAP_S]), st.sb("idxf_p", [NE, CAP_P])
        gate_s, gate_p = st.sb("gate_s", [P, NE]), st.sb("gate_p", [CAP_P, NE])
        col_s, col_p = st.sb("col_s", [P, NE], U32), st.sb("col_p", [CAP_P, NE], U32)
        cur_s, cur_p = st.sb("cur_s", [P, 1], U32), st.sb("cur_p", [CAP_P, 1], U32)
        out_s, out_p = st.sb("out_s", [P, 1], U32), st.sb("out_p", [CAP_P, 1], U32)
        raw = [st.sb(f"raw{p}", [P, KC, WIDTH]) for p in range(RAW)]
        w_hi = [st.sb(f"w_hi{i}", [P, KC, P], F32R) for i in range(RING)]
        w_lo = [st.sb(f"w_lo{i}", [P, KC, P], F32R) for i in range(RING)]
        x_s, x_p = st.sb("x_s", [P, D]), st.sb("x_p", [CAP_P, D])
        xT = st.sb("xT", [P, KC, 2 * SLOTS], F32R)
        hT = st.sb("hT", [P, KC, 2 * SLOTS], F32R)
        gs, sig, us = (st.sb(n, [P, 2, SLOTS]) for n in ("gs", "sig", "us"))
        yT = st.sb("yT", [P, 2, SLOTS])
        y_s, y_p = st.sb("y_s", [P, D]), st.sb("y_p", [CAP_P, D])
        out = [st.ps(f"out{i}", [P, 512]) for i in range(BANKS)]
        X = st.ps("X", [P, 3, 512])
        Y = [st.ps(f"Y{b}", [P, 4, P]) for b in range(2)]
        s = {n: st.sem(n) for n in (
            "max_found", "index_found", "replaced", "listed", "turned", "columns_ready", "cur_ready", "gathered_s",
            "gathered_p", "x_turned", "xT_hi", "xT_lo", "w_hi_ready", "w_lo_dve", "w_lo_pool", "tile_done",
            "summed", "sig_ready", "u_gated", "h_made", "h_hi_ready", "h_ready", "y_turned", "y_moved", "out_ready",
            "added_s", "added_p", "work_ready")}
        loaded = [st.sem(f"loaded{p}") for p in range(RAW)]

        def sp_load(sp, e, p):
            w = (w_g, w_u)[p % 2] if p < FIRST_DOWN_PIECE else w_d
            c = (p // 2 if p < FIRST_DOWN_PIECE else p - FIRST_DOWN_PIECE) * WIDTH
            src = w[bass.ds(e, 1), :, c:c + WIDTH].rearrange("a (k p) n -> p (a k) n", p=P)
            sp.dma_start(raw[p % RAW][:], src).then_inc(loaded[p % RAW], 16)

        def sp_reload(sp, e, p):
            old_e, old_p = (e, p - RAW) if p >= RAW else (e - 1, p + RAW)
            tiles = [t for t in range(TILES) if piece_of(t)[0] == old_p]
            for parity in {t % 2 for t in tiles}:
                sp.wait_ge(*lo_done(old_e, max(t for t in tiles if t % 2 == parity)))
                st.stand(sp)
            sp_load(sp, e, p)

        def split_hi(act, e, t):
            p, c = piece_of(t)
            act.wait_ge(loaded[p % RAW], 16 * (2 * e + p // RAW + 1))
            act.wait_ge(s["tile_done"], TILES * e + t - RING + 1 + CR)
            nc.scalar.activation(w_hi[t % RING][:], raw[p % RAW][:, :, c:c + P], ACT.Copy).then_inc(s["w_hi_ready"], 1)

        def split_lo(eng, ops, e, t):
            p, c = piece_of(t)
            eng.wait_ge(s["w_hi_ready"], TILES * e + t + 1)
            ops.tensor_tensor(w_lo[t % RING][:], raw[p % RAW][:, :, c:c + P], w_hi[t % RING][:].bitcast(F32),
                              ALU.subtract).then_inc(lo_done(e, t)[0], 1)

        def x_chunks(b):
            ks = slice(BANKX * b, min(BANKX * b + BANKX, KC))
            return ks, X[:, b, 0:(ks.stop - ks.start) * SLOTS].rearrange("p (k c) -> p k c", c=SLOTS)

        def act_x(act, e):
            act.wait_ge(s["x_turned"], e + 1)
            for b in range(3):
                ks, src = x_chunks(b)
                nc.scalar.activation(xT[:, ks, 0:SLOTS], src, ACT.Copy).then_inc(s["xT_hi"], 1)

        def dve_x(dve, e):
            for b in range(3):
                ks, src = x_chunks(b)
                dve.wait_ge(s["xT_hi"], 3 * e + b + 1)
                nc.vector.tensor_tensor(xT[:, ks, SLOTS:], src, xT[:, ks, 0:SLOTS].bitcast(F32),
                                        ALU.subtract).then_inc(s["xT_lo"], 1)

        def act_sigmoid(act, e, j):
            act.wait_ge(s["summed"], TILES * e + 2 * j + 1 + CR)
            act.wait_ge(s["h_made"], KC * e + j - 1 + CR)
            nc.scalar.activation(sig[:, j % 2, :], gs[:, j % 2, :], ACT.Sigmoid).then_inc(s["sig_ready"], 1)

        def act_move_y(act, e, d, first):
            act.wait_ge(s["y_turned"], KC * e + d + 1)
            if d == 0 and not first:
                act.wait_ge(s["added_s"], 16 * e)
                act.wait_ge(s["added_p"], 16 * e)
            c = slice(d * P, (d + 1) * P)
            st.stand(act)
            nc.scalar.activation(y_s[:, c], Y[d % 2][:, 0, :], ACT.Copy, scale=gate_s[:, bass.ds(e, 1)])
            nc.scalar.activation(y_p[:, c], Y[d % 2][0:CAP_P, 1, :], ACT.Copy, scale=gate_p[:, bass.ds(e, 1)]).then_inc(s["y_moved"], 1)

        def act_expert(act, e, first, last):
            for t in range(TILES):
                if t == FIRST_DOWN - 1:
                    act_sigmoid(act, e, KC - 1)
                if t + AHEAD < TILES:
                    split_hi(act, e, t + AHEAD)
                elif not last:
                    split_hi(act, e + 1, t + AHEAD - TILES)
                if t < FIRST_DOWN and t % 2 == 0 and t:
                    act_sigmoid(act, e, t // 2 - 1)
                if t == TURN_X + 1 and not last:
                    act_x(act, e + 1)
                if t == 1 and not first:
                    act_move_y(act, e - 1, KC - 1, False)
                if t >= FIRST_DOWN + 2:
                    act_move_y(act, e, t - FIRST_DOWN - 2, first)
            act_move_y(act, e, KC - 2, first)
            if last:
                act_move_y(act, e, KC - 1, first)

        def dve_sum(dve, e, t, first):
            halves = out[t % BANKS][:, 0:2 * SLOTS].rearrange("p (two c) -> p c two", two=2)
            if t < FIRST_DOWN:
                j = t // 2
                dst = (gs, us)[t % 2][:, j % 2, :]
                dve.wait_ge(s["h_made" if t % 2 else "u_gated"], KC * e + j - 1 + CR)
            else:
                d = t - FIRST_DOWN
                dst = yT[:, d % 2, :]
                if d >= 2 or not first:
                    dve.wait_ge(s["y_turned"], KC * e + d - 1)
            dve.wait_ge(s["tile_done"], TILES * e + t + 1 + CR)
            nc.vector.tensor_reduce(dst, halves, AX.X, ALU.add).then_inc(s["summed"], 1)

        def dve_gate(dve, e, j):
            u, g = us[:, j % 2, :], gs[:, j % 2, :]
            dve.wait_ge(s["summed"], TILES * e + 2 * j + 2 + CR)
            nc.vector.tensor_tensor(u, u, g, ALU.mult).then_inc(s["u_gated"], 1)

        def dve_h(dve, e, j):
            u = us[:, j % 2, :]
            dve.wait_ge(s["u_gated"], KC * e + j + 1 + CR)
            dve.wait_ge(s["sig_ready"], KC * e + j + 1)
            nc.vector.tensor_tensor(u, u, sig[:, j % 2, :], ALU.mult).then_inc(s["h_made"], 1)
            dve.wait_ge(s["h_made"], KC * e + j + 1 + CR)
            nc.vector.tensor_copy(hT[:, j, 0:SLOTS], u).then_inc(s["h_hi_ready"], 1)
            dve.wait_ge(s["h_hi_ready"], KC * e + j + 1)
            nc.vector.tensor_tensor(hT[:, j, SLOTS:], u, hT[:, j, 0:SLOTS].bitcast(F32),
                                    ALU.subtract).then_inc(s["h_ready"], 1)

        def dve_expert(dve, e, first, last):
            for t in range(TILES):
                n = t + DVE_AHEAD
                if n % 2 == 0 and not (last and n >= TILES):
                    split_lo(dve, nc.vector, e + n // TILES, n % TILES)
                dve_sum(dve, e, t, first)
                if t < FIRST_DOWN and t % 2:
                    dve_gate(dve, e, t // 2)
                    if t == FIRST_DOWN - 1:
                        dve_h(dve, e, KC - 1)
                if t < FIRST_DOWN and t % 2 == 0 and t:
                    dve_h(dve, e, t // 2 - 1)
                if t == TURN_X + 1 and not last:
                    dve_x(dve, e + 1)

        def pool_gather(pool, e):
            nc.gpsimd.tensor_copy(cur_s[:], col_s[:, bass.ds(e, 1)])
            nc.gpsimd.tensor_copy(cur_p[:], col_p[:, bass.ds(e, 1)]).then_inc(s["cur_ready"], 1)
            pool.wait_ge(s["cur_ready"], e + 1)
            st.stand(pool)
            nc.gpsimd.indirect_dma_start(x_s[:], None, h2[1], bass.IndirectOffsetOnAxis(ap=cur_s[:], axis=0)).then_inc(s["gathered_s"], 16)
            nc.gpsimd.indirect_dma_start(x_p[:], None, h2[0], bass.IndirectOffsetOnAxis(ap=cur_p[:], axis=0)).then_inc(s["gathered_p"], 16)

        def pool_add(pool, e, first):
            if not first:
                pool.wait_ge(s["added_s"], 16 * e)
                pool.wait_ge(s["added_p"], 16 * e)
            nc.gpsimd.tensor_copy(out_s[:], col_s[:, bass.ds(e, 1)])
            nc.gpsimd.tensor_copy(out_p[:], col_p[:, bass.ds(e, 1)]).then_inc(s["out_ready"], 1)
            pool.wait_ge(s["out_ready"], e + 1)
            pool.wait_ge(s["y_moved"], KC * (e + 1) + CR)
            st.stand(pool)
            nc.gpsimd.indirect_dma_start(x3[1], bass.IndirectOffsetOnAxis(ap=out_s[:], axis=0), y_s[:], None,
                                         compute_op=ALU.add).then_inc(s["added_s"], 16)
            nc.gpsimd.indirect_dma_start(x3[0], bass.IndirectOffsetOnAxis(ap=out_p[:], axis=0), y_p[:], None,
                                         compute_op=ALU.add).then_inc(s["added_p"], 16)

        def pool_expert(pool, e, first, last):
            for t in range(TILES):
                n = t + AHEAD
                if n % 2 and not (last and n >= TILES):
                    split_lo(pool, nc.gpsimd, e + n // TILES, n % TILES)
                if t == ADD and not first:
                    pool_add(pool, e - 1, False)
                if t == GATHER and not last:
                    pool.wait_ge(s["x_turned"], e + 1)
                    pool.wait_ge(s["gathered_s"], 16 * (e + 1))
                    pool.wait_ge(s["gathered_p"], 16 * (e + 1))
                    pool_gather(pool, e + 1)

        def pe_turn_x(pe, e):
            pe.wait_ge(s["gathered_s"], 16 * (e + 1))
            pe.wait_ge(s["gathered_p"], 16 * (e + 1))
            for k in range(KC):
                dst = X[:, k // BANKX, (k % BANKX) * SLOTS:(k % BANKX + 1) * SLOTS]
                nc.tensor.transpose(dst[:, 0:CAP_S], x_s[:, k * P:(k + 1) * P], C.ident[:])
                mm = nc.tensor.transpose(dst[:, CAP_S:], x_p[:, k * P:(k + 1) * P], C.ident[0:CAP_P, 0:CAP_P])
            mm.then_inc(s["x_turned"], 1)

        def pe_turn_y(pe, e, d):
            pe.wait_ge(s["summed"], TILES * e + FIRST_DOWN + d + 1 + CR)
            pe.wait_ge(s["y_moved"], KC * e + d - 1 + CR)
            nc.tensor.transpose(Y[d % 2][:, 0, :], yT[:, d % 2, 0:CAP_S], C.ident[:])
            nc.tensor.transpose(Y[d % 2][0:CAP_P, 1, :], yT[:, d % 2, CAP_S:], C.ident[:]).then_inc(s["y_turned"], 1)

        def pe_tile(pe, e, t):
            i, bank = t % RING, out[t % BANKS]
            if t == 0:
                pe.wait_ge(s["xT_lo"], 3 * (e + 1))
            pe.wait_ge(*lo_done(e, t))
            pe.wait_ge(s["summed"], TILES * e + t - BANKS + 1 + CR)
            B = xT if t < FIRST_DOWN else hT
            for k in range(KC):
                if t == FIRST_DOWN:
                    pe.wait_ge(s["h_ready"], KC * e + k + 1)
                nc.tensor.matmul(bank[:, 0:2 * SLOTS], w_hi[i][:, k, :], B[:, k, :], start=(k == 0), stop=False)
                mm = nc.tensor.matmul(bank[:, SLOTS:2 * SLOTS], w_lo[i][:, k, :], B[:, k, 0:SLOTS], start=False,
                                      stop=(k == KC - 1))
            mm.then_inc(s["tile_done"], 1)

        def pe_expert(pe, e, first, last):
            for t in range(TILES):
                pe_tile(pe, e, t)
                if t == 0 and not first:
                    pe_turn_y(pe, e - 1, KC - 1)
                if t > FIRST_DOWN:
                    pe_turn_y(pe, e, t - FIRST_DOWN - 1)
                if t == TURN_X and not last:
                    pe_turn_x(pe, e + 1)
            if last:
                pe_turn_y(pe, e, KC - 1)

        def find(dve, work, val, idx, waves, done):
            for w in range(waves):
                c = slice(8 * w, 8 * w + 8)
                if done + w:
                    dve.wait_ge(s["replaced"], done + w)
                nc.vector.max(val[:, c], work[:]).then_inc(s["max_found"], 1)
                dve.wait_ge(s["max_found"], done + w + 1)
                nc.vector.max_index(idx[:, c], val[:, c], work[:]).then_inc(s["index_found"], 1)
                dve.wait_ge(s["index_found"], done + w + 1)
                nc.vector.match_replace(work[:], val[:, c], work[:], -1.0).then_inc(s["replaced"], 1)

        lists = ((val_s, gate_s, CAP_S, out[0]), (idxf_s, col_s, CAP_S, out[1]),
                 (val_p, gate_p, CAP_P, out[2]), (idxf_p, col_p, CAP_P, X[:, 0, :]))

        with st.block() as block:

            @block.sync
            def _(sp):
                for p in range(RAW):
                    sp_load(sp, 0, p)
                for p in range(RAW, PIECES):
                    sp_reload(sp, 0, p)
                with sp.Fori(1, NE) as e:
                    for p in range(PIECES):
                        sp_reload(sp, e, p)
                sp.wait_ge(s["added_s"], 16 * NE)
                sp.wait_ge(s["added_p"], 16 * NE)

            @block.scalar
            def _(act):
                act.sem_inc(s["y_moved"], CR)
                for t in range(AHEAD):
                    split_hi(act, 0, t)
                act_x(act, 0)
                act_expert(act, 0, True, False)
                with act.Fori(1, NE - 1) as e:
                    act_expert(act, e, False, False)
                act_expert(act, NE - 1, False, True)

            @block.gpsimd
            def _(pool):
                nc.gpsimd.tensor_copy(work_s[:], aff[:, T_PROMPT:]).then_inc(s["work_ready"], 1)
                nc.gpsimd.tensor_copy(work_p[:], aff[:, 0:T_PROMPT]).then_inc(s["work_ready"], 1)
                for t in range(1, AHEAD, 2):
                    split_lo(pool, nc.gpsimd, 0, t)
                pool.wait_ge(s["columns_ready"], 4)
                pool_gather(pool, 0)
                pool_expert(pool, 0, True, False)
                with pool.Fori(1, NE - 1) as e:
                    pool_expert(pool, e, False, False)
                pool_expert(pool, NE - 1, False, True)
                pool_add(pool, NE - 1, False)

            @block.tensor
            def _(pe):
                pe.sem_inc(s["tile_done"], CR)
                pe.wait_ge(s["listed"], 2)
                for src, _, cap, dst in lists:
                    nc.tensor.transpose(dst[0:cap, 0:NE], src[:], C.ident[0:NE, 0:NE]).then_inc(s["turned"], 1)
                pe_turn_x(pe, 0)
                pe_expert(pe, 0, True, False)
                with pe.Fori(1, NE - 1) as e:
                    pe_expert(pe, e, False, False)
                pe_expert(pe, NE - 1, False, True)

            @block.vector
            def _(dve):
                for n in ("summed", "u_gated", "h_made"):
                    dve.sem_inc(s[n], CR)
                dve.wait_ge(s["work_ready"], 2)
                find(dve, work_s, val_s, idx_s, WAVES_S, 0)
                find(dve, work_p, val_p, idx_p, WAVES_P, WAVES_S)
                nc.vector.tensor_copy(idxf_s[:], idx_s[:]).then_inc(s["listed"], 1)
                nc.vector.tensor_copy(idxf_p[:], idx_p[:]).then_inc(s["listed"], 1)
                for n, (_, dst, cap, src) in enumerate(lists):
                    dve.wait_ge(s["turned"], n + 1)
                    nc.vector.tensor_copy(dst[0:cap, :], src[0:cap, 0:NE]).then_inc(s["columns_ready"], 1)
                for t in range(0, DVE_AHEAD, 2):
                    split_lo(dve, nc.vector, 0, t)
                dve_x(dve, 0)
                dve_expert(dve, 0, True, False)
                with dve.Fori(1, NE - 1) as e:
                    dve_expert(dve, e, False, False)
                dve_expert(dve, NE - 1, False, True)


def norm_out(nc, C, x3, final_g, y_prompt, y_sample):
    with Stage(nc, "no") as st:
        x = st.sb("x", [P, NT, D])
        gain, junk = st.sb("gain", [P, D]), st.sb("junk", [P, D])
        ssq, var, std, rstd = (st.sb(n, [P, NT]) for n in ("ssq", "var", "std", "rstd"))
        x_loaded = [st.sem(f"x_loaded{t}") for t in range(NT)]
        s = {n: st.sem(n) for n in ("gain_loaded", "ssq_ready", "var_ready", "std_ready", "rstd_ready", "y_ready", "y_stored")}

        def rows(pair, t):
            a, n = (pair[0], t) if t < NT_PROMPT else (pair[1], t - NT_PROMPT)
            return a[n * P:(n + 1) * P, :]

        with st.block() as block:

            @block.sync
            def _(sp):
                for t in range(NT):
                    sp.dma_start(x[:, t, :], rows(x3, t)).then_inc(x_loaded[t], 16)
                    if t == 0:
                        sp.dma_start(gain[:], final_g.rearrange("(a d) -> a d", a=1).broadcast_to([P, D])).then_inc(s["gain_loaded"], 16)
                for t in range(NT):
                    sp.wait_ge(s["y_ready"], t + 1)
                    sp.dma_start(rows((y_prompt[0], y_sample[0]), t), x[:, t, :]).then_inc(s["y_stored"], 16)
                sp.wait_ge(s["y_stored"], 16 * NT)

            @block.scalar
            def _(act):
                for t in range(NT):
                    act.wait_ge(x_loaded[t], 16)
                    if t:
                        act.wait_ge(s["ssq_ready"], t)
                    nc.scalar.activation(junk[:], x[:, t, :], ACT.Square, accum_out=ssq[:, t:t + 1]).then_inc(s["ssq_ready"], 1)
                    act.wait_ge(s["var_ready"], t + 1)
                    nc.scalar.activation(std[:, t:t + 1], var[:, t:t + 1], ACT.Sqrt).then_inc(s["std_ready"], 1)

            @block.vector
            def _(dve):
                dve.wait_ge(s["gain_loaded"], 16)
                for t in range(NT):
                    dve.wait_ge(s["ssq_ready"], t + 1)
                    nc.vector.tensor_scalar(var[:, t:t + 1], ssq[:, t:t + 1], 1.0 / D, EPS, ALU.mult, ALU.add).then_inc(s["var_ready"], 1)
                    dve.wait_ge(s["std_ready"], t + 1)
                    nc.vector.reciprocal(rstd[:, t:t + 1], std[:, t:t + 1]).then_inc(s["rstd_ready"], 1)
                    dve.wait_ge(s["rstd_ready"], t + 1)
                    nc.vector.scalar_tensor_tensor(out=x[:, t, :], in0=x[:, t, :], scalar=rstd[:, t:t + 1], in1=gain[:],
                                                   op0=ALU.mult, op1=ALU.mult).then_inc(s["y_ready"], 1)


def build(nc, I, y_prompt, y_sample):
    class C:
        pass

    def scratch(name, shape):
        return nc.dram_tensor(name, shape, F32).ap()

    ya, yb, m_a, m_ab = (scratch(n, (D, T)) for n in ("ya", "yb", "m_a", "m_ab"))
    x3 = scratch("x3_prompt", (T_PROMPT, D)), scratch("x3_sample", (T_SAMPLE, D))
    h2 = scratch("h2_prompt", (T_PROMPT, D)), scratch("h2_sample", (T_SAMPLE, D))
    w_in = I["w_in"][0]
    with Stage(nc, "all") as top:
        constants(nc, C, top, I["b_lb_logits"], I["b_onorm_g"], I["a_vnorm_g"])
        with Stage(nc, "trunk") as st:
            h_hi = st.sb("h_hi", [P, KC, T], F32R)
            h_lo = st.sb("h_lo", [P, KC, T], F32R)
            norm_in(nc, C, I["x_prompt"], I["x_sample"], I["norm1_g"], h_hi, h_lo)
            gmlp(nc, C, w_in, I["a_spatial_w"][0], I["a_spatial_b"][0], h_hi, h_lo, ya)
            merge(nc, "ma", w_in, COL_GA, I["w_branch_a"][0], ya, None, m_a, h_hi, h_lo)
            hgrn2(nc, C, w_in, h_hi, h_lo, yb)
            merge(nc, "mb", w_in, COL_GB, I["w_branch_b"][0], yb, m_a, m_ab, h_hi, h_lo)
        aff = top.sb("aff", [NE, T])
        with Stage(nc, "mixed") as st:
            x2 = st.sb("x2", [P, NT, D])
            residual(nc, C, I["x_prompt"], I["x_sample"], I["w_out"][0], m_ab, x2)
            route(nc, C, I["norm2_g"], I["w_router"][0], x2, x3, h2, aff)
        experts(nc, C, aff, h2, x3, I["w_exp_gate"][0], I["w_exp_up"][0], I["w_exp_down"][0])
        norm_out(nc, C, x3, I["final_g"], y_prompt, y_sample)


_INS = ["x_prompt", "x_sample", "norm1_g", "w_in", "a_vnorm_g", "a_spatial_w", "a_spatial_b", "b_lb_logits",
        "b_onorm_g", "w_branch_a", "w_branch_b", "w_out", "norm2_g", "w_router", "w_exp_gate", "w_exp_up",
        "w_exp_down", "final_g"]
_OUTS = [((1, T_PROMPT, D), "float32"), ((1, T_SAMPLE, D), "float32")]


def kernel(**inputs):
    import numpy as _np
    import concourse.bacc as _bacc
    from concourse import mybir as _mybir
    from concourse.bass_utils import run_bass_kernel_spmd as _run

    nc = _bacc.Bacc("TRN2", target_bir_lowering=False, num_devices=1)
    arrays, aps = {}, {}
    for name in _INS:
        a = _np.ascontiguousarray(inputs[name])
        arrays[f"in_{name}_dram"] = a
        aps[name] = nc.dram_tensor(f"in_{name}_dram", a.shape, _mybir.dt.from_np(a.dtype), kind="ExternalInput").ap()
    outs = [nc.dram_tensor(f"out_{i}_dram", shape, _mybir.dt.from_np(_np.dtype(dtype)), kind="ExternalOutput").ap()
            for i, (shape, dtype) in enumerate(_OUTS)]
    build(nc, aps, *outs)
    r = _run(nc, [arrays], core_ids=[0])
    return tuple(r.results[0][f"out_{i}_dram"] for i in range(len(_OUTS)))
```

```python
from contextlib import ExitStack

import concourse.bass as bass
from concourse import mybir

F32 = mybir.dt.float32
F32R = mybir.dt.float32r
U32 = mybir.dt.uint32
I32 = mybir.dt.int32
U8 = mybir.dt.uint8
ALU = mybir.AluOpType
ACT = mybir.ActivationFunctionType
AX = mybir.AxisListType

P = 128
D = 1024
KC = D // P
T_PROMPT = 256
T_SAMPLE = 1024
T = T_PROMPT + T_SAMPLE
NT = T // P
NT_PROMPT = T_PROMPT // P
GROUPS = D // P
HEADS = D // P
NE = 16
CAP_S = 2 * T_SAMPLE // NE
CAP_P = 2 * T_PROMPT // NE
SLOTS = CAP_S + CAP_P
EPS = 1e-6
PART = 320
PARTS = T // PART
LEVELS = 7
CREDIT = 8
COL_U, COL_V, COL_Q, COL_I, COL_ZF, COL_ZB, COL_GO, COL_GA, COL_GB = (j * D for j in range(9))
SEQS = ((0, NT_PROMPT), (NT_PROMPT, NT))


def cols(w, c0):
    return w.rearrange("(k p) n -> p k n", p=P)[:, :, bass.ds(c0, P)]


class Stage:

    def __init__(self, nc, name):
        self.nc, self.name, self.ctx, self.sems = nc, name, ExitStack(), []
        self.waited = None

    def __enter__(self):
        self.ctx.__enter__()
        return self

    def __exit__(self, *a):
        if self.sems and a[0] is None:
            for sem in self.sems:
                self.nc.gpsimd.sem_clear(sem)
                self.nc.release_semaphore(sem)
        return self.ctx.__exit__(*a)

    def sb(self, name, shape, dt=F32):
        return self.ctx.enter_context(self.nc.sbuf_tensor(f"{self.name}_{name}", shape, dt))

    def ps(self, name, shape, dt=F32):
        return self.ctx.enter_context(self.nc.psum_tensor(f"{self.name}_{name}", shape, dt))

    def sem(self, name):
        self.sems.append(self.nc.alloc_semaphore(f"{self.name}_{name}"))
        return self.sems[-1]

    def stand(self, eng):
        self.waited = self.waited or self.sem("waited")
        eng.sem_inc(self.waited, 1)

    def block(self):
        return self.nc.Block()


class WeightStream:

    def __init__(self, st, per):
        self.st, self.per = st, per
        ring = 2 if per % 2 == 0 else 3
        self.raw_slot = [t % 2 for t in range(per)]
        self.slot = [t % ring for t in range(per)]
        self.raw = [st.sb(f"w_raw{i}", [P, KC, P]) for i in range(2)]
        self.hi = [st.sb(f"w_hi{i}", [P, KC, P], F32R) for i in range(ring)]
        self.lo = [st.sb(f"w_lo{i}", [P, KC, P], F32R) for i in range(ring)]
        self.out = [st.ps(f"proj{i}", [P, 512]) for i in range(2)]
        self.loaded = [st.sem(f"w_loaded{i}") for i in range(2)]
        self.hi_ready = st.sem("w_hi_ready")
        self.lo_ready = st.sem("w_lo_ready")
        self.group_done = st.sem("proj_group_done")
        self.bank_free = [st.sem(f"proj_bank_free{i}") for i in range(2)]

    def back(self, slots, t):
        return next(d for d in range(1, self.per + 1) if slots[(t - d) % self.per] == slots[t])

    def load(self, sp, r, t, src):
        n = self.per * r + t - self.back(self.raw_slot, t)
        sp.wait_ge(self.hi_ready, n + 1 + CREDIT)
        sp.wait_ge(self.lo_ready, n + 1 + CREDIT)
        self.st.stand(sp)
        sp.dma_start(self.raw[self.raw_slot[t]][:], src).then_inc(self.loaded[self.raw_slot[t]], 16)

    def split_hi(self, nc, act, r, t):
        rs, s = self.raw_slot[t], self.slot[t]
        n = self.per * r + t - self.back(self.slot, t)
        turn = self.raw_slot.count(rs) * r + self.raw_slot[:t + 1].count(rs)
        act.wait_ge(self.group_done, PARTS * (n + 1 + CREDIT))
        act.wait_ge(self.loaded[rs], 16 * turn)
        nc.scalar.activation(self.hi[s][:], self.raw[rs][:], ACT.Copy).then_inc(self.hi_ready, 1)

    def split_lo(self, nc, pool, r, t):
        rs, s = self.raw_slot[t], self.slot[t]
        pool.wait_ge(self.hi_ready, self.per * r + t + 1 + CREDIT)
        nc.gpsimd.tensor_tensor(self.lo[s][:], self.raw[rs][:], self.hi[s][:].bitcast(F32),
                                ALU.subtract).then_inc(self.lo_ready, 1)

    def multiply(self, nc, pe, r, t, part, x_hi, x_lo, rows=None):
        g = PARTS * t + part
        s, b = self.slot[t], g % 2
        if part == 0:
            pe.wait_ge(self.lo_ready, self.per * r + t + 1 + CREDIT)
        pe.wait_ge(self.bank_free[b], PARTS // 2 * self.per * r + g // 2 + CREDIT)
        out, c = self.out[b][:, 0:PART], slice(part * PART, (part + 1) * PART)
        for k in range(KC):
            if rows is not None:
                rows.ready(pe, k)
            nc.tensor.matmul(out, self.hi[s][:, k, :], x_hi[:, k, c], start=(k == 0), stop=False)
            nc.tensor.matmul(out, self.hi[s][:, k, :], x_lo[:, k, c], start=False, stop=False)
            mm = nc.tensor.matmul(out, self.lo[s][:, k, :], x_hi[:, k, c], start=False, stop=(k == KC - 1))
        mm.then_inc(self.group_done, 1)

    def result(self, eng, r, t, part):
        g = PARTS * t + part
        eng.wait_ge(self.group_done, PARTS * self.per * r + g + 1 + PARTS * CREDIT)
        return self.out[g % 2][:, 0:PART], self.bank_free[g % 2]

    def moved(self, eng, r, t):
        for b in range(2):
            eng.wait_ge(self.bank_free[b], PARTS // 2 * (self.per * r + t + 1) + CREDIT)

    def pe_credit(self, pe):
        pe.sem_inc(self.group_done, PARTS * CREDIT)

    def act_credit(self, act):
        act.sem_inc(self.hi_ready, CREDIT)
        for b in range(2):
            act.sem_inc(self.bank_free[b], CREDIT)

    def pool_credit(self, pool):
        pool.sem_inc(self.lo_ready, CREDIT)


def norm_in(nc, C, x_prompt, x_sample, norm1_g, h_hi, h_lo):
    PAIRS = NT // 2
    with Stage(nc, "n1") as st:
        x = st.sb("x", [P, NT, D])
        gain = st.sb("gain", [P, D])
        junk = st.sb("junk", [P, D])
        xn = st.sb("xn", [P, 2, D])
        ssq, var, std, rstd = (st.sb(n, [P, NT]) for n in ("ssq", "var", "std", "rstd"))
        xT = st.ps("xT", [P, 2, KC, P])
        x_loaded = [st.sem(f"x_loaded{j}") for j in range(PAIRS)]
        gain_loaded, ssq_ready, var_ready, std_ready = (st.sem(n) for n in ("gain_loaded", "ssq_ready", "var_ready", "std_ready"))
        rstd_ready, xn_ready, xT_ready, hi_ready, lo_ready = (st.sem(n) for n in ("rstd_ready", "xn_ready", "xT_ready", "hi_ready", "lo_ready"))
        with st.block() as block:

            @block.sync
            def _(sp):
                sp.dma_start(x[:, 0:2, :], x_prompt.rearrange("b (t p) d -> p (b t) d", p=P)).then_inc(x_loaded[0], 16)
                sp.dma_start(gain[:], norm1_g.broadcast_to([P, D])).then_inc(gain_loaded, 16)
                xs = x_sample.rearrange("b (t p) d -> p (b t) d", p=P)
                for j in range(1, PAIRS):
                    sp.dma_start(x[:, 2 * j:2 * j + 2, :], xs[:, 2 * j - 2:2 * j, :]).then_inc(x_loaded[j], 16)

            @block.scalar
            def _(act):
                def square(t):
                    act.wait_ge(x_loaded[t // 2], 16)
                    if t:
                        act.wait_ge(ssq_ready, t)
                    nc.scalar.activation(junk[:], x[:, t, :], ACT.Square,
                                         accum_out=ssq[:, t:t + 1]).then_inc(ssq_ready, 1)

                def root(t):
                    act.wait_ge(var_ready, t + 1)
                    nc.scalar.activation(std[:, t:t + 1], var[:, t:t + 1], ACT.Sqrt).then_inc(std_ready, 1)

                square(0)
                root(0)
                for t in range(NT):
                    if t + 1 < NT:
                        square(t + 1)
                        root(t + 1)
                    act.wait_ge(xT_ready, t + 1)
                    nc.scalar.activation(h_hi[:, :, t * P:(t + 1) * P], xT[:, t % 2], ACT.Copy).then_inc(hi_ready, 1)

            @block.vector
            def _(dve):
                def scale(t):
                    dve.wait_ge(ssq_ready, t + 1)
                    nc.vector.tensor_scalar(var[:, t:t + 1], ssq[:, t:t + 1], 1.0 / D, EPS, ALU.mult,
                                            ALU.add).then_inc(var_ready, 1)
                    dve.wait_ge(std_ready, t + 1)
                    nc.vector.reciprocal(rstd[:, t:t + 1], std[:, t:t + 1]).then_inc(rstd_ready, 1)
                    dve.wait_ge(rstd_ready, t + 1)
                    if t >= 2:
                        dve.wait_ge(xT_ready, t - 1)
                    nc.vector.scalar_tensor_tensor(out=xn[:, t % 2, :], in0=x[:, t, :], scalar=rstd[:, t:t + 1],
                                                   in1=gain[:], op0=ALU.mult, op1=ALU.mult).then_inc(xn_ready, 1)

                dve.wait_ge(gain_loaded, 16)
                scale(0)
                for t in range(NT):
                    if t + 1 < NT:
                        scale(t + 1)
                    dve.wait_ge(hi_ready, t + 1)
                    c = slice(t * P, (t + 1) * P)
                    nc.vector.tensor_tensor(h_lo[:, :, c], xT[:, t % 2], h_hi[:, :, c].bitcast(F32),
                                            ALU.subtract).then_inc(lo_ready, 1)

            @block.tensor
            def _(pe):
                for t in range(NT):
                    pe.wait_ge(xn_ready, t + 1)
                    if t >= 2:
                        pe.wait_ge(lo_ready, t - 1)
                    for k in range(KC):
                        mm = nc.tensor.transpose(xT[:, t % 2, k, :], xn[:, t % 2, k * P:(k + 1) * P], C.ident[:])
                    mm.then_inc(xT_ready, 1)


def constants(nc, C, st, b_lb_logits, b_onorm_g, a_vnorm_g):
    C.ident = st.sb("ident", [P, P])
    C.ones = st.sb("ones", [P, P])
    C.eps = st.sb("eps", [P, 1])
    C.mask = st.sb("mask", [P, LEVELS + 1, P], U8)
    C.lb = st.sb("lb", [P, 2, HEADS])
    C.one_minus_lb = st.sb("one_minus_lb", [P, 2, HEADS])
    C.onorm = st.sb("onorm", [P, 1])
    C.vnorm = st.sb("vnorm", [P, GROUPS])
    with Stage(nc, "const") as s:
        logits = s.sb("logits", [P, 2, HEADS])
        top, expo, prob = (s.sb(n, [P, 2, HEADS]) for n in ("top", "expo", "prob"))
        same = s.sb("same", [P, LEVELS + 1, P])
        diff = s.sb("diff", [P, LEVELS + 1, P])
        cut = s.sb("cut", [P, LEVELS + 1, P])
        loaded, filled, half, made, lb_step = (s.sem(n) for n in ("loaded", "filled", "half", "made", "lb_step"))
        expo_ready = s.sem("expo_ready")
        with s.block() as block:

            @block.sync
            def _(sp):
                sp.dma_start(logits[:], b_lb_logits.rearrange("z a (h p) -> p (z a) h", p=P), allow_slow_non_contiguous=True).then_inc(loaded, 16)
                sp.dma_start(C.onorm[:], b_onorm_g.rearrange("a p -> p a"), allow_slow_non_contiguous=True).then_inc(loaded, 16)
                sp.dma_start(C.vnorm[:], a_vnorm_g.rearrange("a (g p) -> p (a g)", p=P), allow_slow_non_contiguous=True).then_inc(loaded, 16)
                sp.wait_ge(loaded, 48)

            @block.gpsimd
            def _(pool):
                nc.gpsimd.memset(C.ones[:], 1.0)
                nc.gpsimd.memset(C.eps[:], EPS)
                nc.gpsimd.memset(same[:], 1.0).then_inc(filled, 1)
                pool.wait_ge(filled, 1)
                for l in range(LEVELS):
                    b = 1 << l
                    blocks = cut[:, l, :].rearrange("p (n b) -> p n b", b=b)
                    ones = same[:, l, :].rearrange("p (n b) -> p n b", b=b)
                    nc.gpsimd.affine_select(out=blocks, in_=ones, compare_op=ALU.is_ge, fill=0.0, base=0,
                                            pattern=[[-b, P // b], [0, b]], channel_multiplier=1).then_inc(half, 1)
                pool.wait_ge(half, LEVELS)
                for l in range(LEVELS):
                    b = 1 << l
                    blocks = cut[:, l, :].rearrange("p (n b) -> p n b", b=b)
                    ones = same[:, l, :].rearrange("p (n b) -> p n b", b=b)
                    nc.gpsimd.affine_select(out=ones, in_=blocks, compare_op=ALU.is_ge, fill=0.0, base=b - 1,
                                            pattern=[[b, P // b], [0, b]], channel_multiplier=-1).then_inc(made, 1)

            @block.vector
            def _(dve):
                dve.wait_ge(made, LEVELS)
                nc.vector.tensor_copy(C.ident[:], same[:, 0, :])
                nc.vector.tensor_copy(C.mask[:, 0, :], same[:, 0, :])
                nc.vector.tensor_tensor(diff[:, 1:, :], same[:, 1:, :], same[:, 0:LEVELS, :], ALU.subtract).then_inc(lb_step, 1)
                dve.wait_ge(lb_step, 1)
                nc.vector.tensor_copy(C.mask[:, 1:, :], diff[:, 1:, :])
                dve.wait_ge(loaded, 48)
                nc.vector.tensor_copy(top[:], logits[:]).then_inc(lb_step, 1)
                dve.wait_ge(lb_step, 2)
                nc.vector.tensor_tensor(logits[:], logits[:], top[:], ALU.subtract).then_inc(lb_step, 1)
                dve.wait_ge(expo_ready, 1)
                nc.vector.reciprocal(top[:], expo[:]).then_inc(lb_step, 1)
                dve.wait_ge(lb_step, 4)
                nc.vector.tensor_tensor(prob[:], expo[:], top[:], ALU.mult).then_inc(lb_step, 1)
                dve.wait_ge(lb_step, 5)
                nc.vector.tensor_tensor(C.lb[:], prob[:], prob[:], ALU.subtract).then_inc(lb_step, 1)
                dve.wait_ge(lb_step, 6)
                nc.vector.tensor_scalar(C.one_minus_lb[:], C.lb[:], -1.0, 1.0, ALU.mult, ALU.add)

            @block.scalar
            def _(act):
                act.wait_ge(lb_step, 3)
                nc.scalar.activation(expo[:], logits[:], ACT.Exp).then_inc(expo_ready, 1)


def pairs(ap, b):
    return ap.rearrange("p (n two b) -> p n two b", two=2, b=b)


def crossed(both, row, t0, n, b):
    ap = both[:]
    return bass.AP(tensor=ap.tensor, offset=ap.offset + t0, ap=[list(ap.ap[0]), [2 * b, n // (2 * b)], [row + b, 2], [1, b]])


def over(ap, n):
    return ap.unsqueeze(2).broadcast_to([P, ap.shape[1], n])


def hgrn2(nc, C, w_in, h_hi, h_lo, yb_dram):
    order = (COL_I, COL_Q, COL_ZF, COL_ZB, COL_GO)
    TI, TQ, TZF, TZB, TGO = range(5)
    with Stage(nc, "hg") as st:
        W = WeightStream(st, len(order))
        q, vT, v, so, A, Kt_f, Kt_b = (st.sb(n, [P, T]) for n in ("q", "vT", "v", "so", "A", "Kt_f", "Kt_b"))
        f_f, f_b, tot_f, tot_b = (st.sb(n, [P, T]) for n in ("f_f", "f_b", "tot_f", "tot_b"))
        Q = st.sb("Q", [P, 2, T])
        Q_b, Q_f = Q[:, 0, :], Q[:, 1, :]
        K_odd, K_even, K_rest = (st.sb(n, [P, T]) for n in ("K_odd", "K_even", "K_rest"))
        go = Q_b
        k_f, k_b, K_f, K_b = K_odd, K_even, K_even, K_rest
        S_f = st.sb("S_f", [P, NT, P])
        S_b = st.sb("S_b", [P, NT, P])
        k_sum, sq, rt, y = Kt_f, tot_f, tot_b, Kt_b
        G = st.ps("G", [P, 6, 4, P])
        Gc = G[:].rearrange("p b c t -> p (b c) t")

        def K_at(j):
            return (K_even, K_odd)[j % 2]

        def quarters(x, j):
            n = 4 if j < LEVELS else 2
            return x[:].rearrange("p (m n b) -> p m n b", n=n, b=1 << (j - 1)), n

        def bank_cols(base, c):
            return Gc[:, 4 * base + c, :]

        def spans(base):
            return [(G[:, base + j, 0:min(4, NT - 4 * j), :], 4 * j, min(4 * j + 4, NT)) for j in range(3)]

        names = ("v_ready", "gates_ready", "Q_ready", "K_ready",
                 "tot_ready", "k_sum_ready", "K_copied", "A_merged", "gla_step", "v_step", "Kt_ready", "S_ready", "sq_ready",
                 "rt_ready", "y_ready", "y_stored", "A_clear", "so_used", "silu_ready")
        s = {n: st.sem(n) for n in names}
        STEPS = 13
        DIAG, KTF, KTB, STATE, OUT, ONES = 0, 8, 9, 10, 11, 12
        NQ = 2 * (LEVELS + 1)
        NY = 3
        state_f = [c for a, z in SEQS for c in range(a, z - 1)]
        state_b = [c for a, z in SEQS for c in range(z - 1, a, -1)]
        firsts_f, firsts_b = [a for a, _ in SEQS], [z - 1 for _, z in SEQS]
        after = {j: [j] for j in range(STEPS)}

        def sp_round(sp, r, done):
            for t, c in enumerate(order):
                W.load(sp, r, t, cols(w_in, c + r * P))
                if t == 1 and done is not None:
                    store(sp, done)

        def store(sp, g):
            sp.wait_ge(s["y_ready"], NY * (g + 1) + CREDIT)
            st.stand(sp)
            sp.dma_start(yb_dram[bass.ds(g * P, P), :], y[:]).then_inc(s["y_stored"], 16)

        def act_buffers(act, r, t):
            if t == TI:
                act.wait_ge(s["v_step"], r + CREDIT)
            if t == TQ:
                act.wait_ge(s["gla_step"], STEPS * (r - 1) + DIAG + 1 + 2 * STEPS)
                act.wait_ge(s["Q_ready"], NQ * (r - 1) + 2 + 2 * NQ)
            if t == TZF:
                act.wait_ge(s["gla_step"], STEPS * (r - 1) + KTF + 1 + 2 * STEPS)
                act.wait_ge(s["Q_ready"], NQ * (r - 1) + 4 + 2 * NQ)
            if t == TZB:
                act.wait_ge(s["gla_step"], STEPS * (r - 1) + KTB + 1 + 2 * STEPS)
            if t in (TZF, TZB):
                act.wait_ge(s["K_ready"], LEVELS * (r - 1) + 1 + 2 * LEVELS)
            if t == TGO:
                act.wait_ge(s["so_used"], r + CREDIT)

        def act_move(act, r, t, part):
            out, free = W.result(act, r, t, part)
            c = slice(part * PART, (part + 1) * PART)
            if t == TI:
                nc.scalar.activation(vT[:, c], out, ACT.Copy).then_inc(free, 1)
            elif t == TQ:
                nc.scalar.activation(q[:, c], out, ACT.Copy).then_inc(free, 1)
            elif t in (TZF, TZB):
                f, k = ((f_f, k_f), (f_b, k_b))[t == TZB]
                nc.scalar.activation(f[:, c], out, ACT.Sigmoid)
                nc.scalar.activation(k[:, c], out, ACT.Sigmoid, scale=-1.0).then_inc(free, 1)
            else:
                nc.scalar.activation(so[:, c], out, ACT.Sigmoid)
                nc.scalar.activation(go[:, c], out, ACT.Copy).then_inc(free, 1)

        def dve_project(dve, r):
            every = [x[:].rearrange("p (n two) -> p n two", two=2) for x in (K_odd, K_even, K_rest)]
            odd, even, rest = every
            for z, (f, k, t) in enumerate(((f_f, odd, TZF), (f_b, even, TZB))):
                lb, om = C.lb[:, z, bass.ds(r, 1)], C.one_minus_lb[:, z, bass.ds(r, 1)]
                for b in range(2):
                    dve.wait_ge(W.bank_free[b], PARTS // 2 * (W.per * r + t + 1) + CREDIT)
                nc.vector.tensor_scalar(f[:], f[:], om, lb, ALU.mult, ALU.add).then_inc(s["gates_ready"], 1)
                nc.vector.tensor_scalar(rest[:, :, 1 - z], k[:, :, 1 - z], om, None, ALU.mult).then_inc(s["gates_ready"], 1)
                if z:
                    dve.wait_ge(s["gates_ready"], 6 * r + 2)
                nc.vector.tensor_scalar(odd[:, :, z], k[:, :, z], om, None, ALU.mult).then_inc(s["gates_ready"], 1)

        def dve_output_gate(dve, r):
            W.moved(dve, r, TGO)
            nc.vector.tensor_tensor(so[:], go, so[:], ALU.mult).then_inc(s["silu_ready"], 1)

        def pe_values(pe, r):
            for b in range(2):
                pe.wait_ge(W.bank_free[b], PARTS // 2 * (W.per * r + TI + 1) + CREDIT)
            pe.wait_ge(s["y_ready"], NY * r + CREDIT)
            for c in range(NT):
                mm = nc.tensor.transpose(bank_cols(0, c), vT[:, c * P:(c + 1) * P], C.ident[:])
            mm.then_inc(s["v_step"], 1)

        def act_values(act, r):
            act.wait_ge(s["v_step"], r + 1 + CREDIT)
            act.wait_ge(s["gla_step"], STEPS * (r - 1) + OUT + 1 + 2 * STEPS)
            nc.scalar.activation(v[:].rearrange("p (c t) -> p c t", t=P), Gc[:, 0:NT, :], ACT.Copy).then_inc(s["v_ready"], 1)

        def gla_at(g, step):
            return STEPS * g + step + 1 + 2 * STEPS

        def pe_step(pe, g, j):
            base = 3 * (j % 2)
            if j == DIAG:
                pe.wait_ge(s["v_ready"], g + 1)
                pe.wait_ge(s["k_sum_ready"], g + 1)
                for c in range(NT):
                    t = slice(c * P, (c + 1) * P)
                    mm = nc.tensor.matmul(bank_cols(0, c), k_sum[:, t], q[:, t], start=True, stop=True)
            elif j <= LEVELS:
                pe.wait_ge(s["Q_ready"], NQ * g + 2 * j + 2 * NQ)
                if j == 1:
                    pe.wait_ge(s["rt_ready"], g + CREDIT)
                    pe.wait_ge(s["gates_ready"], 6 * (g + 1))
                else:
                    pe.wait_ge(s["K_ready"], LEVELS * g + j - 1 + 2 * LEVELS)
                    pe.wait_ge(s["A_merged"], 8 * g + j - 1)
                b = 1 << (j - 1)
                for c in range(NT):
                    mm = nc.tensor.matmul(bank_cols(base, c), K_at(j)[:, c * P:(c + 1) * P], crossed(Q, T, c * P, P, b),
                                          start=True, stop=True)
            elif j in (KTF, KTB):
                pe.wait_ge(s["A_merged"], 8 * g + j - 1)
                pe.wait_ge(s["K_ready"], LEVELS * g + LEVELS + 2 * LEVELS)
                k = (K_f, K_b)[j == KTB]
                for c in range(NT):
                    mm = nc.tensor.transpose(bank_cols(base, c), k[:, c * P:(c + 1) * P], C.ident[:])
            elif j == STATE:
                pe.wait_ge(s["Kt_ready"], 2 * g + 2)
                for n, (Kt, c) in enumerate([(Kt_f, c) for c in state_f] + [(Kt_b, c) for c in state_b]):
                    t = slice(c * P, (c + 1) * P)
                    mm = nc.tensor.matmul(Gc[:, n, :], Kt[:, t], v[:, t], start=True, stop=True)
            elif j == OUT:
                pe.wait_ge(s["S_ready"], 16 * (g + 1))
                pe.wait_ge(s["A_merged"], 8 * g + 8)
                pe.wait_ge(s["Q_ready"], NQ * g + NQ + 2 * NQ)
                for c in range(NT):
                    t = slice(c * P, (c + 1) * P)
                    terms = [(v[:, t], A[:, t])]
                    if c not in firsts_f:
                        terms.append((S_f[:, c, :], Q_f[:, t]))
                    if c not in firsts_b:
                        terms.append((S_b[:, c, :], Q_b[:, t]))
                    for n, (lhs, rhs) in enumerate(terms):
                        mm = nc.tensor.matmul(bank_cols(0, c), lhs, rhs, start=(n == 0), stop=(n == len(terms) - 1))
            else:
                pe.wait_ge(s["sq_ready"], g + 1)
                for a in range(0, T, 512):
                    z = min(a + 512, T)
                    mm = nc.tensor.matmul(G[:, 3 + a // 512, :, :].rearrange("p c t -> p (c t)")[:, 0:z - a],
                                          C.ones[:], sq[:, a:z], start=True, stop=True)
            mm.then_inc(s["gla_step"], 1)

        def pe_round(pe, r, g, project, gla):
            for t in range(len(order)):
                for part in range(PARTS):
                    if project:
                        W.multiply(nc, pe, r, t, part, h_hi, h_lo)
                    n = PARTS * t + part
                    if gla and n in after:
                        for j in after[n]:
                            pe_step(pe, g, j)
            if project:
                pe_values(pe, r)

        def act_gla(act, g, j):
            if j in (KTF, KTB):
                act.wait_ge(s["gla_step"], gla_at(g, j))
                Kt = (Kt_f, Kt_b)[j == KTB]
                base = 12 * (j % 2)
                if j == KTB:
                    act.wait_ge(s["y_stored"], 16 * (g + CREDIT))
                nc.scalar.activation(Kt[:].rearrange("p (c t) -> p c t", t=P), Gc[:, base:base + NT, :],
                                     ACT.Copy).then_inc(s["Kt_ready"], 1)
            elif j == OUT:
                act.wait_ge(s["gla_step"], gla_at(g, OUT))
                nc.scalar.activation(sq[:].rearrange("p (c t) -> p c t", t=P), Gc[:, 0:NT, :],
                                     ACT.Square).then_inc(s["sq_ready"], 1)
            elif j == ONES:
                act.wait_ge(s["gla_step"], gla_at(g, ONES))
                nc.scalar.activation(rt[:].rearrange("p (c t) -> p c t", t=P), Gc[:, 12:12 + NT, :], ACT.Sqrt,
                                     bias=C.eps[:], scale=1.0 / P).then_inc(s["rt_ready"], 1)

        def act_round(act, r, g, project, gla, more):
            for t in range(len(order)):
                if project:
                    if t + 1 < len(order):
                        W.split_hi(nc, act, r, t + 1)
                    elif more:
                        W.split_hi(nc, act, r + 1, 0)
                    act_buffers(act, r, t)
                for part in range(PARTS):
                    if project:
                        act_move(act, r, t, part)
                    if gla:
                        for j in after.get(PARTS * t + part, ()):
                            act_gla(act, g, j)
            if project:
                act_values(act, r)

        def pool_round(pool, r, g, project, gla, more):
            levels = list(range(1, LEVELS + 1))
            if gla:
                pool.wait_ge(s["gates_ready"], 6 * (g + 1))
                pool.wait_ge(s["gla_step"], gla_at(g - 1, STATE))
                nc.gpsimd.tensor_tensor(k_sum[:], K_odd[:], K_rest[:], ALU.add).then_inc(s["k_sum_ready"], 1)
            for t in range(len(order)):
                if project and t + 1 < len(order):
                    W.split_lo(nc, pool, r, t + 1)
                elif more:
                    W.split_lo(nc, pool, r + 1, 0)
                if not gla:
                    continue
                for j in levels[PARTS * t:PARTS * (t + 1)]:
                    pool_level(pool, g, j)

        def pool_level(pool, g, j):
            pool.wait_ge(s["K_copied"], LEVELS * g + j)
            if j >= 2:
                pool.wait_ge(s["K_ready"], LEVELS * g + j - 1 + 2 * LEVELS)
            else:
                pool.wait_ge(s["k_sum_ready"], g + 1)
            pool.wait_ge(s["tot_ready"], 2 * (LEVELS * g + j))
            (old, n), (new, _), (rest, _) = quarters(K_at(j), j), quarters(K_at(j + 1), j), quarters(K_rest, j)
            for i in range(n):
                F, tot = ((f_f, tot_f), (f_b, tot_b))[i % 2]
                total = total_of(F, tot, j - 1).rearrange("p (m n) -> p m n", n=n)[:, :, i ^ 1]
                dst = new if i in (0, 3) else rest
                op = nc.gpsimd.tensor_tensor(dst[:, :, i, :], old[:, :, i, :], over(total, 1 << (j - 1)), ALU.mult)
            op.then_inc(s["K_ready"], 1)

        def dve_copy(dve, g, j):
            if j >= 2:
                dve.wait_ge(s["gla_step"], gla_at(g, j - 1))
                dve.wait_ge(s["K_ready"], LEVELS * g + j - 1 + 2 * LEVELS)
                st.stand(dve)
            (new, n), (rest, _) = quarters(K_at(j + 1), j), quarters(K_rest, j)
            c = slice(1, 3) if n == 4 else slice(1, 2)
            nc.vector.tensor_copy(new[:, :, c, :], rest[:, :, c, :]).then_inc(s["K_copied"], 1)

        tot_at = [0]
        for l in range(1, LEVELS + 1):
            tot_at.append(tot_at[-1] + (T >> l))

        def total_of(F, tot, l):
            return F[:] if l == 0 else tot[:, tot_at[l - 1]:tot_at[l]]

        def level_total(F, tot, j):
            return total_of(F, tot, j - 1).rearrange("p (n two) -> p n two", two=2)

        def dve_start(dve, g):
            dve.wait_ge(s["gates_ready"], 6 * (g + 1))
            for b in range(2):
                dve.wait_ge(W.bank_free[b], PARTS // 2 * (W.per * g + TQ + 1) + CREDIT)
            dve.wait_ge(s["gla_step"], gla_at(g - 1, OUT))
            dve.wait_ge(s["rt_ready"], g + CREDIT)
            nc.vector.tensor_tensor(Q_f[:], q[:], f_f[:], ALU.mult).then_inc(s["Q_ready"], 1)
            dve.wait_ge(s["silu_ready"], g + 1)
            nc.vector.tensor_tensor(Q_b[:], q[:], f_b[:], ALU.mult).then_inc(s["Q_ready"], 1)
            for l in range(1, LEVELS + 1):
                if l >= 2:
                    dve.wait_ge(s["tot_ready"], 2 * (LEVELS * g + l - 1))
                for F, tot in ((f_f, tot_f), (f_b, tot_b)):
                    two = level_total(F, tot, l)
                    nc.vector.tensor_tensor(total_of(F, tot, l), two[:, :, 0], two[:, :, 1], ALU.mult).then_inc(s["tot_ready"], 1)

        def dve_merge(dve, g, j):
            if j == DIAG:
                dve.wait_ge(s["A_clear"], 1)
            else:
                dve.wait_ge(s["A_merged"], 8 * g + j)
            dve.wait_ge(s["gla_step"], gla_at(g, j))
            st.stand(dve)
            for out, c0, c1 in spans(3 * (j % 2)):
                n = c1 - c0
                cp = nc.vector.copy_predicated(A[:, c0 * P:c1 * P].rearrange("p (c t) -> p c t", t=P),
                                               C.mask[:, j, :].unsqueeze(1).broadcast_to([P, n, P]), out)
            cp.then_inc(s["A_merged"], 1)

        def dve_level(dve, g, j):
            b = 1 << (j - 1)
            dve.wait_ge(s["gla_step"], gla_at(g, j))
            dve.wait_ge(s["Q_ready"], NQ * g + 2 * j + 2 * NQ)
            for Q, F, tot, side in ((Q_f, f_f, tot_f, 1), (Q_b, f_b, tot_b, 0)):
                total = level_total(F, tot, j)
                half = pairs(Q[:], b)[:, :, side, :]
                nc.vector.tensor_tensor(half, half, over(total[:, :, 1 - side], b), ALU.mult).then_inc(s["Q_ready"], 1)

        def dve_states(dve, g):
            dve.wait_ge(s["gla_step"], gla_at(g, STATE))
            totf, totb = total_of(f_f, tot_f, LEVELS), total_of(f_b, tot_b, LEVELS)
            runs = [(n, c, c + 1, S_f, totf, c in firsts_f) for n, c in enumerate(state_f)]
            runs += [(n + len(state_f), c, c - 1, S_b, totb, c in firsts_b) for n, c in enumerate(state_b)]
            half = len(state_f)
            for i in range(half):
                for n, c, to, S, tot, first in (runs[i], runs[i + half]):
                    done = 2 * i + (S is S_b)
                    if not first:
                        dve.wait_ge(s["S_ready"], 16 * g + done - 1)
                    if first:
                        nc.vector.tensor_copy(S[:, to, :], Gc[:, n, :]).then_inc(s["S_ready"], 1)
                    else:
                        nc.vector.scalar_tensor_tensor(out=S[:, to, :], in0=S[:, c, :], scalar=tot[:, c:c + 1],
                                                       in1=Gc[:, n, :], op0=ALU.mult, op1=ALU.add).then_inc(s["S_ready"], 1)

        def dve_output(dve, g):
            dve.wait_ge(s["silu_ready"], g + 1)
            nc.vector.tensor_scalar(y[:], so[:], C.onorm[:], None, ALU.mult).then_inc(s["so_used"], 1)
            dve.wait_ge(s["rt_ready"], g + 1 + CREDIT)
            nc.vector.reciprocal(rt[:], rt[:]).then_inc(s["y_ready"], 1)
            dve.wait_ge(s["y_ready"], NY * g + 1 + CREDIT)
            dve.wait_ge(s["so_used"], g + 1 + CREDIT)
            nc.vector.tensor_tensor(y[:], y[:], rt[:], ALU.mult).then_inc(s["y_ready"], 1)
            dve.wait_ge(s["y_ready"], NY * g + 2 + CREDIT)
            y3 = y[:].rearrange("p (c t) -> p c t", t=P)
            nc.vector.tensor_tensor(y3, Gc[:, 0:NT, :], y3, ALU.mult).then_inc(s["y_ready"], 1)

        def dve_round(dve, r, g, project, gla):
            if gla:
                dve_start(dve, g)
                for j in range(LEVELS + 1):
                    if j:
                        dve_level(dve, g, j)
                    if j < LEVELS:
                        dve_copy(dve, g, j + 1)
                    dve_merge(dve, g, j)
                dve_states(dve, g)
                dve_output(dve, g)
            if project:
                dve_project(dve, r)
                dve_output_gate(dve, r)

        with st.block() as block:

            @block.sync
            def _(sp):
                sp.sem_inc(s["y_stored"], 16 * CREDIT)
                sp_round(sp, 0, None)
                sp_round(sp, 1, None)
                with sp.Fori(2, HEADS) as r:
                    sp_round(sp, r, r - 2)
                store(sp, HEADS - 2)
                store(sp, HEADS - 1)
                sp.wait_ge(s["y_stored"], 16 * (HEADS + CREDIT))

            @block.scalar
            def _(act):
                W.act_credit(act)
                act.sem_inc(s["rt_ready"], CREDIT)
                W.split_hi(nc, act, 0, 0)
                act_round(act, 0, None, True, False, True)
                with act.Fori(0, HEADS - 2) as g:
                    act_round(act, g + 1, g, True, True, True)
                act_round(act, HEADS - 1, HEADS - 2, True, True, False)
                act_round(act, None, HEADS - 1, False, True, False)

            @block.gpsimd
            def _(pool):
                W.pool_credit(pool)
                pool.sem_inc(s["K_ready"], 2 * LEVELS)
                nc.gpsimd.memset(A[:], 0.0).then_inc(s["A_clear"], 1)
                W.split_lo(nc, pool, 0, 0)
                pool_round(pool, 0, None, True, False, True)
                with pool.Fori(0, HEADS - 2) as g:
                    pool_round(pool, g + 1, g, True, True, True)
                pool_round(pool, HEADS - 1, HEADS - 2, True, True, False)
                pool_round(pool, None, HEADS - 1, False, True, False)

            @block.tensor
            def _(pe):
                W.pe_credit(pe)
                pe.sem_inc(s["gla_step"], 2 * STEPS)
                pe.sem_inc(s["v_step"], CREDIT)
                pe_round(pe, 0, None, True, False)
                with pe.Fori(0, HEADS - 1) as g:
                    pe_round(pe, g + 1, g, True, True)
                pe_round(pe, None, HEADS - 1, False, True)

            @block.vector
            def _(dve):
                dve.sem_inc(s["Q_ready"], 2 * NQ)
                dve.sem_inc(s["y_ready"], CREDIT)
                dve.sem_inc(s["so_used"], CREDIT)
                dve_round(dve, 0, None, True, False)
                with dve.Fori(0, HEADS - 1) as g:
                    dve_round(dve, g + 1, g, True, True)
                dve_round(dve, None, HEADS - 1, False, True)


def chunks(ap):
    return ap.rearrange("p (c t) -> p c t", t=P)


def gmlp(nc, C, w_in, w_s, b_s, h_hi, h_lo, ya_dram):
    PER, ROUNDS = 2, GROUPS // 2
    with Stage(nc, "gm") as st:
        W = WeightStream(st, PER)
        v = st.sb("v", [P, GROUPS, T])
        act_out = [st.sb(f"act_out{t}", [P, T]) for t in range(PER)]
        vn = [st.sb(f"vn{t}", [P, T]) for t in range(PER)]
        ya = [st.sb(f"ya{t}", [P, T]) for t in range(PER)]
        sq = ya
        ws = [st.sb(f"ws{t}", [P, P]) for t in range(PER)]
        wsT = [st.sb(f"wsT{t}", [P, P]) for t in range(PER)]
        bias = [st.sb(f"bias{t}", [P, P]) for t in range(PER)]
        ssq = st.sb("ssq", [P, GROUPS, NT])
        var, std, rstd = (st.sb(n, [P, NT]) for n in ("var", "std", "rstd"))
        G = st.ps("G", [P, 6, 4, P])
        Gc = G[:].rearrange("p b c t -> p (b c) t")
        s = {n: st.sem(n) for n in ("v_turned", "v_copied", "v_squared", "v_summed", "var_ready", "std_ready",
                                    "rstd_ready", "vn_ready", "ws_turned", "wsT_ready", "mixed", "mix_scaled",
                                    "ya_ready")}
        ws_loaded = [st.sem(f"ws_loaded{t}") for t in range(PER)]
        bias_loaded = [st.sem(f"bias_loaded{t}") for t in range(PER)]
        ya_stored = [st.sem(f"ya_stored{t}") for t in range(PER)]

        def bank_set(t):
            return Gc[:, 12 * t:12 * t + NT, :], Gc[:, 12 * t + NT, :]

        def pe_turn_v(pe, r, t):
            n = PER * r + t
            W.moved(pe, r, t)
            pe.wait_ge(s["v_copied"], n - 1 + CREDIT)
            out, _ = bank_set(t)
            for c in range(NT):
                mm = nc.tensor.transpose(out[:, c, :], act_out[t][:, c * P:(c + 1) * P], C.ident[:])
            mm.then_inc(s["v_turned"], 1)

        def pe_v_round(pe, r, first):
            for t in range(PER):
                for part in range(PARTS):
                    W.multiply(nc, pe, r, t, part, h_hi, h_lo)
                    if part == 1 and not (first and t == 0):
                        pe_turn_v(pe, *((r, 0) if t == 1 else (r - 1, 1)))

        def act_move(act, r, t):
            for part in range(PARTS):
                out, free = W.result(act, r, t, part)
                nc.scalar.activation(act_out[t][:, part * PART:(part + 1) * PART], out,
                                     ACT.Gelu_apprx_tanh).then_inc(free, 1)

        def act_v_round(act, r):
            for t in range(PER):
                W.split_hi(nc, act, r + t, (t + 1) % PER)
                act.wait_ge(s["v_turned"], PER * r + t - 1 + CREDIT)
                act_move(act, r, t)

        def dve_v_round(dve, r):
            for t in range(PER):
                n = PER * r + t
                dve.wait_ge(s["v_turned"], n + 1 + CREDIT)
                out, _ = bank_set(t)
                nc.vector.tensor_copy(chunks(v[:, bass.ds(n, 1), :].rearrange("p a t -> p (a t)")), out).then_inc(s["v_copied"], 1)
                dve.wait_ge(s["v_squared"], n + 1)
                nc.vector.tensor_reduce(ssq[:, bass.ds(n, 1), :].rearrange("p a c -> p (a c)"), chunks(sq[t][:]),
                                        AX.X, ALU.add).then_inc(s["v_summed"], 1)

        def pool_v_round(pool, r):
            for t in range(PER):
                n = PER * r + t
                pool_split(pool, r + t, (t + 1) % PER)
                pool.wait_ge(s["v_copied"], n + 1 + CREDIT)
                pool.wait_ge(s["v_summed"], n - 1 + CREDIT)
                src = v[:, bass.ds(n, 1), :].rearrange("p a t -> p (a t)")
                nc.gpsimd.tensor_tensor(sq[t][:], src, src, ALU.mult).then_inc(s["v_squared"], 1)

        def pool_split(pool, r, t):
            W.split_lo(nc, pool, r, t)

        def sp_u_round(sp, i):
            for t in range(PER):
                n = PER * i + t
                W.load(sp, ROUNDS + i, t, cols(w_in, COL_U + n * P))
                sp.wait_ge(s["ws_turned"], n - 1 + CREDIT)
                st.stand(sp)
                sp.dma_start(ws[t][:], w_s[bass.ds(n, 1)].rearrange("g t s -> (g t) s")).then_inc(ws_loaded[t], 16)
                sp.wait_ge(s["mix_scaled"], n - 1 + CREDIT)
                st.stand(sp)
                sp.dma_start(bias[t][:], b_s[bass.ds(n, 1), :].broadcast_to([P, P])).then_inc(bias_loaded[t], 16)

        def sp_store(sp, i):
            for t in range(PER):
                n = PER * i + t
                sp.wait_ge(s["ya_ready"], n + 1 + CREDIT)
                st.stand(sp)
                sp.dma_start(ya_dram[bass.ds(n * P, P), :], ya[t][:]).then_inc(ya_stored[t], 16)

        def pe_u_round(pe, i):
            for t in range(PER):
                n = PER * i + t
                out, turned = bank_set(t)
                for part in range(PARTS):
                    W.multiply(nc, pe, ROUNDS + i, t, part, h_hi, h_lo)
                    if part == 0:
                        pe.wait_ge(ws_loaded[t], 16 * (i + 1))
                        pe.wait_ge(s["wsT_ready"], n - 1 + CREDIT)
                        nc.tensor.transpose(turned, ws[t][:], C.ident[:]).then_inc(s["ws_turned"], 1)
                    if part == 2:
                        pe.wait_ge(s["wsT_ready"], n + 1 + CREDIT)
                        pe.wait_ge(s["vn_ready"], n + 1)
                        pe.wait_ge(s["mix_scaled"], n - 1 + CREDIT)
                        for c in range(NT):
                            mm = nc.tensor.matmul(out[:, c, :], vn[t][:, c * P:(c + 1) * P], wsT[t][:], start=True, stop=True)
                        mm.then_inc(s["mixed"], 1)

        def act_u_round(act, i, last):
            for t in range(PER):
                n = PER * i + t
                if not (last and t == PER - 1):
                    W.split_hi(nc, act, ROUNDS + i + t, (t + 1) % PER)
                _, turned = bank_set(t)
                act.wait_ge(s["ws_turned"], n + 1 + CREDIT)
                act.wait_ge(s["mixed"], n - 1 + CREDIT)
                nc.scalar.activation(wsT[t][:], turned, ACT.Copy).then_inc(s["wsT_ready"], 1)
                act.wait_ge(s["ya_ready"], n - 1 + CREDIT)
                act_move(act, ROUNDS + i, t)

        def dve_u_round(dve, i):
            for t in range(PER):
                n = PER * i + t
                out, _ = bank_set(t)
                dve.wait_ge(s["mixed"], n - 1 + CREDIT)
                vg = chunks(v[:, bass.ds(n, 1), :].rearrange("p a t -> p (a t)"))
                nc.vector.tensor_tensor(chunks(vn[t][:]), vg, over(rstd[:], P), ALU.mult).then_inc(s["vn_ready"], 1)
                dve.wait_ge(s["mixed"], n + 1 + CREDIT)
                dve.wait_ge(bias_loaded[t], 16 * (i + 1))
                dve.wait_ge(ya_stored[t], 16 * (i + CREDIT))
                nc.vector.scalar_tensor_tensor(out=chunks(ya[t][:]), in0=out, scalar=C.vnorm[:, bass.ds(n, 1)],
                                               in1=bias[t][:].unsqueeze(1).broadcast_to([P, NT, P]),
                                               op0=ALU.mult, op1=ALU.add).then_inc(s["mix_scaled"], 1)
                W.moved(dve, ROUNDS + i, t)
                dve.wait_ge(s["mix_scaled"], n + 1 + CREDIT)
                nc.vector.tensor_tensor(ya[t][:], ya[t][:], act_out[t][:], ALU.mult).then_inc(s["ya_ready"], 1)

        with st.block() as block:

            @block.sync
            def _(sp):
                for t in range(PER):
                    sp.sem_inc(ya_stored[t], 16 * CREDIT)
                with sp.Fori(0, ROUNDS) as r:
                    for t in range(PER):
                        W.load(sp, r, t, cols(w_in, COL_V + (PER * r + t) * P))
                sp_u_round(sp, 0)
                with sp.Fori(1, ROUNDS) as i:
                    sp_u_round(sp, i)
                    sp_store(sp, i - 1)
                sp_store(sp, ROUNDS - 1)
                for t in range(PER):
                    sp.wait_ge(ya_stored[t], 16 * (ROUNDS + CREDIT))

            @block.scalar
            def _(act):
                W.act_credit(act)
                act.sem_inc(s["wsT_ready"], CREDIT)
                W.split_hi(nc, act, 0, 0)
                with act.Fori(0, ROUNDS) as r:
                    act_v_round(act, r)
                act.wait_ge(s["var_ready"], 1)
                nc.scalar.activation(std[:], var[:], ACT.Sqrt).then_inc(s["std_ready"], 1)
                with act.Fori(0, ROUNDS - 1) as i:
                    act_u_round(act, i, False)
                act_u_round(act, ROUNDS - 1, True)

            @block.gpsimd
            def _(pool):
                W.pool_credit(pool)
                W.split_lo(nc, pool, 0, 0)
                with pool.Fori(0, ROUNDS) as r:
                    pool_v_round(pool, r)
                with pool.Fori(0, ROUNDS - 1) as i:
                    for t in range(PER):
                        pool_split(pool, ROUNDS + i + t, (t + 1) % PER)
                pool_split(pool, 2 * ROUNDS - 1, 1)

            @block.tensor
            def _(pe):
                W.pe_credit(pe)
                for n in ("v_turned", "ws_turned", "mixed"):
                    pe.sem_inc(s[n], CREDIT)
                pe_v_round(pe, 0, True)
                with pe.Fori(1, ROUNDS) as r:
                    pe_v_round(pe, r, False)
                pe_turn_v(pe, ROUNDS - 1, 1)
                with pe.Fori(0, ROUNDS) as i:
                    pe_u_round(pe, i)

            @block.vector
            def _(dve):
                for n in ("v_copied", "v_summed", "mix_scaled", "ya_ready"):
                    dve.sem_inc(s[n], CREDIT)
                with dve.Fori(0, ROUNDS) as r:
                    dve_v_round(dve, r)
                dve.wait_ge(s["v_summed"], GROUPS + CREDIT)
                nc.vector.tensor_reduce(var[:], ssq[:].rearrange("p g c -> p c g"), AX.X, ALU.add).then_inc(s["rstd_ready"], 1)
                dve.wait_ge(s["rstd_ready"], 1)
                nc.vector.tensor_scalar(var[:], var[:], 1.0 / D, EPS, ALU.mult, ALU.add).then_inc(s["var_ready"], 1)
                dve.wait_ge(s["std_ready"], 1)
                nc.vector.reciprocal(rstd[:], std[:]).then_inc(s["rstd_ready"], 1)
                dve.wait_ge(s["rstd_ready"], 2)
                with dve.Fori(0, ROUNDS) as i:
                    dve_u_round(dve, i)


class RowSplit:

    def __init__(self, st, src, ring, parts, hi, lo):
        self.src, self.ring, self.hi, self.lo = src, ring, hi, lo
        n = T // parts
        self.pieces = [(k, slice(i * n, (i + 1) * n)) for k in range(KC) for i in range(parts)]
        self.loaded = [st.sem(f"row_loaded{b}") for b in range(len(ring))]
        self.hi_ready, self.lo_even, self.lo_odd = (st.sem(n) for n in ("row_hi_ready", "row_lo_even", "row_lo_odd"))

    def load(self, sp):
        for i, (k, c) in enumerate(self.pieces):
            old = i - len(self.ring)
            if old >= 0:
                sp.wait_ge(self.hi_ready, old + 1)
                sp.wait_ge((self.lo_even, self.lo_odd)[old % 2], old // 2 + 1)
            b = i % len(self.ring)
            sp.dma_start(self.ring[b], self.src[k * P:(k + 1) * P, c]).then_inc(self.loaded[b], 16)

    def split_hi(self, nc, act, i):
        k, c = self.pieces[i]
        b = i % len(self.ring)
        act.wait_ge(self.loaded[b], 16 * (i // len(self.ring) + 1))
        nc.scalar.activation(self.hi[:, k, c], self.ring[b], ACT.Copy).then_inc(self.hi_ready, 1)

    def split_lo(self, eng, ops, parity, done):
        for i, (k, c) in enumerate(self.pieces):
            if i % 2 == parity:
                eng.wait_ge(self.hi_ready, i + 1)
                ops.tensor_tensor(self.lo[:, k, c], self.ring[i % len(self.ring)], self.hi[:, k, c].bitcast(F32),
                                  ALU.subtract).then_inc(done, 1)

    def ready(self, eng, k=KC - 1):
        n = (k + 1) * len(self.pieces) // KC
        eng.wait_ge(self.lo_even, (n + 1) // 2)
        if n > 1:
            eng.wait_ge(self.lo_odd, n // 2)


def merge(nc, name, w_in, col_gate, w_branch, y_dram, m_in, m_out, h_hi, h_lo):
    PER = 2
    GATE, BRANCH = 0, 1
    with Stage(nc, name) as st:
        W = WeightStream(st, PER)
        y_hi = st.sb("y_hi", [P, KC, T], F32R)
        y_lo = st.sb("y_lo", [P, KC, T], F32R)
        sg, m, m_prev = (st.sb(n, [P, T]) for n in ("sg", "m", "m_prev"))
        s = {n: st.sem(n) for n in ("added", "m_stored", "m_prev_loaded")}
        rows = RowSplit(st, y_dram, [a[:, i * T // 2:(i + 1) * T // 2] for a in (m, m_prev) for i in range(2)], 2, y_hi, y_lo)
        adds = m_in is not None

        def sp_round(sp, r):
            W.load(sp, r, GATE, cols(w_in, col_gate + r * P))
            W.load(sp, r, BRANCH, cols(w_branch, r * P))

        def sp_tail(sp, r):
            if adds:
                sp.wait_ge(s["added"], PARTS * (r + 1) + PARTS * CREDIT)
            else:
                W.moved(sp, r, BRANCH)
            sp.dma_start(m_out[bass.ds(r * P, P), :], m[:]).then_inc(s["m_stored"], 16)

        def sp_prev(sp, r):
            if adds:
                sp.wait_ge(s["added"], PARTS * (r + CREDIT))
                st.stand(sp)
                sp.dma_start(m_prev[:], m_in[bass.ds(r * P, P), :]).then_inc(s["m_prev_loaded"], 16)

        def act_gate(act, r, part):
            out, free = W.result(act, r, GATE, part)
            nc.scalar.activation(sg[:, part * PART:(part + 1) * PART], out, ACT.Sigmoid).then_inc(free, 1)

        def act_round(act, r, last):
            W.split_hi(nc, act, r, BRANCH)
            W.moved(act, r - 1, BRANCH)
            for part in range(PARTS):
                act_gate(act, r, part)
            if not last:
                W.split_hi(nc, act, r + 1, GATE)

        def dve_round(dve, r):
            W.moved(dve, r, GATE)
            dve.wait_ge(s["m_stored"], 16 * (r + CREDIT))
            if adds:
                dve.wait_ge(s["m_prev_loaded"], 16 * (r + 1))
            for part in range(PARTS):
                c = slice(part * PART, (part + 1) * PART)
                out, free = W.result(dve, r, BRANCH, part)
                nc.vector.tensor_tensor(m[:, c], out, sg[:, c], ALU.mult).then_inc(free, 1)
                if adds:
                    W_done = PARTS // 2 * (PER * r + BRANCH) + part // 2 + 1 + CREDIT
                    dve.wait_ge(W.bank_free[(PARTS * BRANCH + part) % 2], W_done)
                    nc.vector.tensor_tensor(m[:, c], m[:, c], m_prev[:, c], ALU.add).then_inc(s["added"], 1)

        with st.block() as block:

            @block.sync
            def _(sp):
                sp.sem_inc(s["m_stored"], 16 * CREDIT)
                sp_round(sp, 0)
                rows.load(sp)
                rows.ready(sp)
                sp_prev(sp, 0)
                with sp.Fori(1, KC) as r:
                    sp_round(sp, r)
                    sp_tail(sp, r - 1)
                    sp_prev(sp, r)
                sp_tail(sp, KC - 1)
                sp.wait_ge(s["m_stored"], 16 * (KC + CREDIT))

            @block.scalar
            def _(act):
                W.act_credit(act)
                W.split_hi(nc, act, 0, GATE)
                gate_after = {len(rows.pieces) * (part + 1) // PARTS - 2: part for part in range(PARTS)}
                for i in range(len(rows.pieces)):
                    rows.split_hi(nc, act, i)
                    if i == 1:
                        W.split_hi(nc, act, 0, BRANCH)
                    if i in gate_after:
                        act_gate(act, 0, gate_after[i])
                W.split_hi(nc, act, 1, GATE)
                with act.Fori(1, KC - 1) as r:
                    act_round(act, r, False)
                act_round(act, KC - 1, True)

            @block.gpsimd
            def _(pool):
                W.pool_credit(pool)
                W.split_lo(nc, pool, 0, GATE)
                rows.split_lo(pool, nc.gpsimd, 0, rows.lo_even)
                W.split_lo(nc, pool, 0, BRANCH)
                with pool.Fori(1, KC) as r:
                    W.split_lo(nc, pool, r, GATE)
                    W.split_lo(nc, pool, r, BRANCH)

            @block.tensor
            def _(pe):
                W.pe_credit(pe)

                def pe_round(r):
                    for part in range(PARTS):
                        W.multiply(nc, pe, r, GATE, part, h_hi, h_lo)
                    rows.ready(pe)
                    for part in range(PARTS):
                        W.multiply(nc, pe, r, BRANCH, part, y_hi, y_lo)

                with pe.Fori(0, KC) as r:
                    pe_round(r)

            @block.vector
            def _(dve):
                dve.sem_inc(s["added"], PARTS * CREDIT)
                rows.split_lo(dve, nc.vector, 1, rows.lo_odd)
                rows.ready(dve)
                with dve.Fori(0, KC) as r:
                    dve_round(dve, r)


def residual(nc, C, x_prompt, x_sample, w_out, m_dram, x2):
    PER, ROUNDS = 2, KC // 2
    with Stage(nc, "wo") as st:
        W = WeightStream(st, PER)
        m_hi = st.sb("m_hi", [P, KC, T], F32R)
        m_lo = st.sb("m_lo", [P, KC, T], F32R)
        o = [st.sb(f"o{t}", [P, T]) for t in range(PER)]
        G = st.ps("G", [P, 6, 4, P])
        Gc = G[:].rearrange("p b c t -> p (b c) t")
        s = {n: st.sem(n) for n in ("turned", "added", "x_loaded")}
        m = [st.sb(f"m{k}", [P, T]) for k in range(KC)]
        rows = RowSplit(st, m_dram, [a[:] for a in m], 1, m_hi, m_lo)

        def pe_turn(pe, r, t):
            W.moved(pe, r, t)
            pe.wait_ge(s["added"], PER * r + t - 1 + CREDIT)
            for c in range(NT):
                mm = nc.tensor.transpose(Gc[:, 12 * t + c, :], o[t][:, c * P:(c + 1) * P], C.ident[:])
            mm.then_inc(s["turned"], 1)

        def pe_round(pe, r, first):
            for t in range(PER):
                for part in range(PARTS):
                    W.multiply(nc, pe, r, t, part, m_hi, m_lo, rows if first and t == 0 and part == 0 else None)
                    if part == 1 and not (first and t == 0):
                        pe_turn(pe, *((r, 0) if t == 1 else (r - 1, 1)))

        def act_round(act, r, last):
            for t in range(PER):
                if not (last and t == PER - 1):
                    W.split_hi(nc, act, r + t, (t + 1) % PER)
                act.wait_ge(s["turned"], PER * r + t - 1 + CREDIT)
                for part in range(PARTS):
                    out, free = W.result(act, r, t, part)
                    nc.scalar.activation(o[t][:, part * PART:(part + 1) * PART], out, ACT.Copy).then_inc(free, 1)

        with st.block() as block:

            @block.sync
            def _(sp):
                for t in range(PER):
                    W.load(sp, 0, t, cols(w_out, t * P))
                rows.load(sp)
                sp.dma_start(x2[:, 0:NT_PROMPT, :], x_prompt.rearrange("b (t p) d -> p (b t) d", p=P)).then_inc(s["x_loaded"], 16)
                sp.dma_start(x2[:, NT_PROMPT:NT, :], x_sample.rearrange("b (t p) d -> p (b t) d", p=P)).then_inc(s["x_loaded"], 16)
                with sp.Fori(1, ROUNDS) as r:
                    for t in range(PER):
                        W.load(sp, r, t, cols(w_out, (PER * r + t) * P))

            @block.scalar
            def _(act):
                W.act_credit(act)
                W.split_hi(nc, act, 0, 0)
                for k in range(KC):
                    rows.split_hi(nc, act, k)
                with act.Fori(0, ROUNDS - 1) as r:
                    act_round(act, r, False)
                act_round(act, ROUNDS - 1, True)

            @block.gpsimd
            def _(pool):
                W.pool_credit(pool)
                W.split_lo(nc, pool, 0, 0)
                rows.split_lo(pool, nc.gpsimd, 0, rows.lo_even)
                W.split_lo(nc, pool, 0, 1)
                with pool.Fori(1, ROUNDS) as r:
                    for t in range(PER):
                        W.split_lo(nc, pool, r, t)

            @block.tensor
            def _(pe):
                W.pe_credit(pe)
                pe.sem_inc(s["turned"], CREDIT)
                pe_round(pe, 0, True)
                with pe.Fori(1, ROUNDS) as r:
                    pe_round(pe, r, False)
                pe_turn(pe, ROUNDS - 1, 1)

            @block.vector
            def _(dve):
                dve.sem_inc(s["added"], CREDIT)
                rows.split_lo(dve, nc.vector, 1, rows.lo_odd)
                dve.wait_ge(s["x_loaded"], 32)
                with dve.Fori(0, ROUNDS) as r:
                    for t in range(PER):
                        n = PER * r + t
                        dve.wait_ge(s["turned"], n + 1 + CREDIT)
                        x = x2[:, :, bass.ds(n * P, P)]
                        nc.vector.tensor_tensor(x, Gc[:, 12 * t:12 * t + NT, :], x, ALU.add).then_inc(s["added"], 1)


def route(nc, C, norm2_g, w_router, x2, x3, h2, aff):
    PAIRS = NT // 2
    with Stage(nc, "rt") as st:
        gain, junk = st.sb("gain", [P, D]), st.sb("junk", [P, D])
        wr = st.sb("wr", [P, KC, NE])
        h = st.sb("h", [P, NT, D])
        hT = st.sb("hT", [P, 2, KC, P])
        ssq, var, std, rstd, top, total, inv = (st.sb(n, [P, NT]) for n in ("ssq", "var", "std", "rstd", "top", "total", "inv"))
        shifted, expo, prob = (st.sb(n, [P, NT, NE]) for n in ("shifted", "expo", "prob"))
        turned = st.ps("turned", [P, 2, KC, P])
        logits_bank = st.ps("logits", [P, 512])
        logits = logits_bank[:, 0:NT * NE].rearrange("p (t e) -> p t e", e=NE)
        affT = st.ps("affT", [P, 3 * 512])
        s = {n: st.sem(n) for n in ("loaded", "x3_stored", "ssq_ready", "var_ready", "std_ready", "rstd_ready",
                                    "h_ready", "h_turned", "hT_ready", "logits_ready", "top_ready", "shifted_ready",
                                    "exp_ready", "total_ready", "inv_ready", "prob_ready", "aff_turned", "h_stored")}

        def wide(x):
            return x[:].unsqueeze(2).broadcast_to([P, NT, NE])

        with st.block() as block:

            @block.sync
            def _(sp):
                sp.dma_start(gain[:], norm2_g.broadcast_to([P, D])).then_inc(s["loaded"], 16)
                sp.dma_start(wr[:], w_router.rearrange("(k p) e -> p k e", p=P)).then_inc(s["loaded"], 16)
                for dst, a, z in ((x3[0], 0, NT_PROMPT), (x3[1], NT_PROMPT, NT)):
                    sp.dma_start(dst.rearrange("(t p) d -> p t d", p=P), x2[:, a:z, :]).then_inc(s["x3_stored"], 16)
                h2_rows = [x.rearrange("(t p) d -> p t d", p=P) for x in h2]
                for j in range(PAIRS):
                    sp.wait_ge(s["h_ready"], 2 * j + 2)
                    dst = h2_rows[0] if j == 0 else h2_rows[1][:, 2 * j - 2:2 * j, :]
                    sp.dma_start(dst, h[:, 2 * j:2 * j + 2, :]).then_inc(s["h_stored"], 16)
                sp.wait_ge(s["x3_stored"], 32)
                sp.wait_ge(s["h_stored"], 16 * PAIRS)

            @block.scalar
            def _(act):
                def square(t):
                    if t:
                        act.wait_ge(s["ssq_ready"], t)
                    nc.scalar.activation(junk[:], x2[:, t, :], ACT.Square, accum_out=ssq[:, t:t + 1]).then_inc(s["ssq_ready"], 1)

                def root(t):
                    act.wait_ge(s["var_ready"], t + 1)
                    nc.scalar.activation(std[:, t:t + 1], var[:, t:t + 1], ACT.Sqrt).then_inc(s["std_ready"], 1)

                square(0)
                square(1)
                root(0)
                for t in range(NT):
                    if t + 2 < NT:
                        square(t + 2)
                    if t + 1 < NT:
                        root(t + 1)
                    act.wait_ge(s["h_turned"], t + 1)
                    if t >= 2:
                        act.wait_ge(s["logits_ready"], t - 1)
                    nc.scalar.activation(hT[:, t % 2], turned[:, t % 2], ACT.Copy).then_inc(s["hT_ready"], 1)
                act.wait_ge(s["shifted_ready"], 1)
                nc.scalar.activation(expo[:], shifted[:], ACT.Exp).then_inc(s["exp_ready"], 1)

            @block.tensor
            def _(pe):
                def logit(t):
                    pe.wait_ge(s["hT_ready"], t + 1)
                    for k in range(KC):
                        mm = nc.tensor.matmul(logits[:, t, :], hT[:, t % 2, k, :], wr[:, k, :], start=(k == 0), stop=(k == KC - 1))
                    mm.then_inc(s["logits_ready"], 1)

                for t in range(NT):
                    pe.wait_ge(s["h_ready"], t + 1)
                    if t >= 2:
                        pe.wait_ge(s["hT_ready"], t - 1)
                    for k in range(KC):
                        mm = nc.tensor.transpose(turned[:, t % 2, k, :], h[:, t, k * P:(k + 1) * P], C.ident[:])
                    mm.then_inc(s["h_turned"], 1)
                    if t:
                        logit(t - 1)
                logit(NT - 1)
                pe.wait_ge(s["prob_ready"], 1)
                for t in range(NT):
                    mm = nc.tensor.transpose(affT[0:NE, t * P:(t + 1) * P], prob[:, t, :], C.ident[:])
                mm.then_inc(s["aff_turned"], 1)

            @block.vector
            def _(dve):
                dve.wait_ge(s["loaded"], 32)
                for t in range(NT):
                    c = slice(t, t + 1)
                    dve.wait_ge(s["ssq_ready"], t + 1)
                    nc.vector.tensor_scalar(var[:, c], ssq[:, c], 1.0 / D, EPS, ALU.mult, ALU.add).then_inc(s["var_ready"], 1)
                    dve.wait_ge(s["std_ready"], t + 1)
                    nc.vector.reciprocal(rstd[:, c], std[:, c]).then_inc(s["rstd_ready"], 1)
                    dve.wait_ge(s["rstd_ready"], t + 1)
                    nc.vector.scalar_tensor_tensor(out=h[:, t, :], in0=x2[:, t, :], scalar=rstd[:, c], in1=gain[:],
                                                   op0=ALU.mult, op1=ALU.mult).then_inc(s["h_ready"], 1)
                dve.wait_ge(s["logits_ready"], NT)
                nc.vector.tensor_reduce(top[:], logits, AX.X, ALU.max).then_inc(s["top_ready"], 1)
                dve.wait_ge(s["top_ready"], 1)
                nc.vector.tensor_tensor(shifted[:], logits, wide(top), ALU.subtract).then_inc(s["shifted_ready"], 1)
                dve.wait_ge(s["exp_ready"], 1)
                nc.vector.tensor_reduce(total[:], expo[:], AX.X, ALU.add).then_inc(s["total_ready"], 1)
                dve.wait_ge(s["total_ready"], 1)
                nc.vector.reciprocal(inv[:], total[:]).then_inc(s["inv_ready"], 1)
                dve.wait_ge(s["inv_ready"], 1)
                nc.vector.tensor_tensor(prob[:], expo[:], wide(inv), ALU.mult).then_inc(s["prob_ready"], 1)
                dve.wait_ge(s["aff_turned"], 1)
                nc.vector.tensor_copy(aff[:], affT[0:NE, 0:T])


def experts(nc, C, aff, h2, x3, w_g, w_u, w_d):
    WAVES_S, WAVES_P = CAP_S // 8, CAP_P // 8
    TILES = 3 * KC
    FIRST_DOWN = 2 * KC
    WIDTH = 2 * P
    PIECES = 3 * D // WIDTH
    RAW = PIECES // 2
    FIRST_DOWN_PIECE = 2 * D // WIDTH
    RING, BANKS = 12, 3
    AHEAD = 10
    DVE_AHEAD = 6
    BANKX = 3
    CR = TILES
    TURN_X = FIRST_DOWN + 2
    ADD, GATHER = 1, 3

    def piece_of(t):
        if t < FIRST_DOWN:
            j, which = t // 2, t % 2
            return 2 * (j // 2) + which, (j % 2) * P
        j = t - FIRST_DOWN
        return FIRST_DOWN_PIECE + j // 2, (j % 2) * P

    def lo_done(e, t):
        return s["w_lo_pool"] if t % 2 else s["w_lo_dve"], TILES // 2 * e + t // 2 + 1

    with Stage(nc, "ex") as st:
        work_s, work_p = st.sb("work_s", [NE, T_SAMPLE]), st.sb("work_p", [NE, T_PROMPT])
        val_s, val_p = st.sb("val_s", [NE, CAP_S]), st.sb("val_p", [NE, CAP_P])
        idx_s, idx_p = st.sb("idx_s", [NE, CAP_S], U32), st.sb("idx_p", [NE, CAP_P], U32)
        idxf_s, idxf_p = st.sb("idxf_s", [NE, CAP_S]), st.sb("idxf_p", [NE, CAP_P])
        gate_s, gate_p = st.sb("gate_s", [P, NE]), st.sb("gate_p", [CAP_P, NE])
        col_s, col_p = st.sb("col_s", [P, NE], U32), st.sb("col_p", [CAP_P, NE], U32)
        cur_s, cur_p = st.sb("cur_s", [P, 1], U32), st.sb("cur_p", [CAP_P, 1], U32)
        out_s, out_p = st.sb("out_s", [P, 1], U32), st.sb("out_p", [CAP_P, 1], U32)
        raw = [st.sb(f"raw{p}", [P, KC, WIDTH]) for p in range(RAW)]
        w_hi = [st.sb(f"w_hi{i}", [P, KC, P], F32R) for i in range(RING)]
        w_lo = [st.sb(f"w_lo{i}", [P, KC, P], F32R) for i in range(RING)]
        x_s, x_p = st.sb("x_s", [P, D]), st.sb("x_p", [CAP_P, D])
        xT = st.sb("xT", [P, KC, 2 * SLOTS], F32R)
        hT = st.sb("hT", [P, KC, 2 * SLOTS], F32R)
        gs, sig, us = (st.sb(n, [P, 2, SLOTS]) for n in ("gs", "sig", "us"))
        yT = st.sb("yT", [P, 2, SLOTS])
        y_s, y_p = st.sb("y_s", [P, D]), st.sb("y_p", [CAP_P, D])
        out = [st.ps(f"out{i}", [P, 512]) for i in range(BANKS)]
        X = st.ps("X", [P, 3, 512])
        Y = [st.ps(f"Y{b}", [P, 4, P]) for b in range(2)]
        s = {n: st.sem(n) for n in (
            "max_found", "index_found", "replaced", "listed", "turned", "columns_ready", "cur_ready", "gathered_s",
            "gathered_p", "x_turned", "xT_hi", "xT_lo", "w_hi_ready", "w_lo_dve", "w_lo_pool", "tile_done",
            "summed", "sig_ready", "u_gated", "h_made", "h_hi_ready", "h_ready", "y_turned", "y_moved", "out_ready",
            "added_s", "added_p", "work_ready")}
        loaded = [st.sem(f"loaded{p}") for p in range(RAW)]

        def sp_load(sp, e, p):
            w = (w_g, w_u)[p % 2] if p < FIRST_DOWN_PIECE else w_d
            c = (p // 2 if p < FIRST_DOWN_PIECE else p - FIRST_DOWN_PIECE) * WIDTH
            src = w[bass.ds(e, 1), :, c:c + WIDTH].rearrange("a (k p) n -> p (a k) n", p=P)
            sp.dma_start(raw[p % RAW][:], src).then_inc(loaded[p % RAW], 16)

        def sp_reload(sp, e, p):
            old_e, old_p = (e, p - RAW) if p >= RAW else (e - 1, p + RAW)
            tiles = [t for t in range(TILES) if piece_of(t)[0] == old_p]
            for parity in {t % 2 for t in tiles}:
                sp.wait_ge(*lo_done(old_e, max(t for t in tiles if t % 2 == parity)))
                st.stand(sp)
            sp_load(sp, e, p)

        def split_hi(act, e, t):
            p, c = piece_of(t)
            act.wait_ge(loaded[p % RAW], 16 * (2 * e + p // RAW + 1))
            act.wait_ge(s["tile_done"], TILES * e + t - RING + 1 + CR)
            nc.scalar.activation(w_hi[t % RING][:], raw[p % RAW][:, :, c:c + P], ACT.Copy).then_inc(s["w_hi_ready"], 1)

        def split_lo(eng, ops, e, t):
            p, c = piece_of(t)
            eng.wait_ge(s["w_hi_ready"], TILES * e + t + 1)
            ops.tensor_tensor(w_lo[t % RING][:], raw[p % RAW][:, :, c:c + P], w_hi[t % RING][:].bitcast(F32),
                              ALU.subtract).then_inc(lo_done(e, t)[0], 1)

        def x_chunks(b):
            ks = slice(BANKX * b, min(BANKX * b + BANKX, KC))
            return ks, X[:, b, 0:(ks.stop - ks.start) * SLOTS].rearrange("p (k c) -> p k c", c=SLOTS)

        def act_x(act, e):
            act.wait_ge(s["x_turned"], e + 1)
            for b in range(3):
                ks, src = x_chunks(b)
                nc.scalar.activation(xT[:, ks, 0:SLOTS], src, ACT.Copy).then_inc(s["xT_hi"], 1)

        def dve_x(dve, e):
            for b in range(3):
                ks, src = x_chunks(b)
                dve.wait_ge(s["xT_hi"], 3 * e + b + 1)
                nc.vector.tensor_tensor(xT[:, ks, SLOTS:], src, xT[:, ks, 0:SLOTS].bitcast(F32),
                                        ALU.subtract).then_inc(s["xT_lo"], 1)

        def act_sigmoid(act, e, j):
            act.wait_ge(s["summed"], TILES * e + 2 * j + 1 + CR)
            act.wait_ge(s["h_made"], KC * e + j - 1 + CR)
            nc.scalar.activation(sig[:, j % 2, :], gs[:, j % 2, :], ACT.Sigmoid).then_inc(s["sig_ready"], 1)

        def act_move_y(act, e, d, first):
            act.wait_ge(s["y_turned"], KC * e + d + 1)
            if d == 0 and not first:
                act.wait_ge(s["added_s"], 16 * e)
                act.wait_ge(s["added_p"], 16 * e)
            c = slice(d * P, (d + 1) * P)
            st.stand(act)
            nc.scalar.activation(y_s[:, c], Y[d % 2][:, 0, :], ACT.Copy, scale=gate_s[:, bass.ds(e, 1)])
            nc.scalar.activation(y_p[:, c], Y[d % 2][0:CAP_P, 1, :], ACT.Copy, scale=gate_p[:, bass.ds(e, 1)]).then_inc(s["y_moved"], 1)

        def act_expert(act, e, first, last):
            for t in range(TILES):
                if t == FIRST_DOWN - 1:
                    act_sigmoid(act, e, KC - 1)
                if t + AHEAD < TILES:
                    split_hi(act, e, t + AHEAD)
                elif not last:
                    split_hi(act, e + 1, t + AHEAD - TILES)
                if t < FIRST_DOWN and t % 2 == 0 and t:
                    act_sigmoid(act, e, t // 2 - 1)
                if t == TURN_X + 1 and not last:
                    act_x(act, e + 1)
                if t == 1 and not first:
                    act_move_y(act, e - 1, KC - 1, False)
                if t >= FIRST_DOWN + 2:
                    act_move_y(act, e, t - FIRST_DOWN - 2, first)
            act_move_y(act, e, KC - 2, first)
            if last:
                act_move_y(act, e, KC - 1, first)

        def dve_sum(dve, e, t, first):
            halves = out[t % BANKS][:, 0:2 * SLOTS].rearrange("p (two c) -> p c two", two=2)
            if t < FIRST_DOWN:
                j = t // 2
                dst = (gs, us)[t % 2][:, j % 2, :]
                dve.wait_ge(s["h_made" if t % 2 else "u_gated"], KC * e + j - 1 + CR)
            else:
                d = t - FIRST_DOWN
                dst = yT[:, d % 2, :]
                if d >= 2 or not first:
                    dve.wait_ge(s["y_turned"], KC * e + d - 1)
            dve.wait_ge(s["tile_done"], TILES * e + t + 1 + CR)
            nc.vector.tensor_reduce(dst, halves, AX.X, ALU.add).then_inc(s["summed"], 1)

        def dve_gate(dve, e, j):
            u, g = us[:, j % 2, :], gs[:, j % 2, :]
            dve.wait_ge(s["summed"], TILES * e + 2 * j + 2 + CR)
            nc.vector.tensor_tensor(u, u, g, ALU.mult).then_inc(s["u_gated"], 1)

        def dve_h(dve, e, j):
            u = us[:, j % 2, :]
            dve.wait_ge(s["u_gated"], KC * e + j + 1 + CR)
            dve.wait_ge(s["sig_ready"], KC * e + j + 1)
            nc.vector.tensor_tensor(u, u, sig[:, j % 2, :], ALU.mult).then_inc(s["h_made"], 1)
            dve.wait_ge(s["h_made"], KC * e + j + 1 + CR)
            nc.vector.tensor_copy(hT[:, j, 0:SLOTS], u).then_inc(s["h_hi_ready"], 1)
            dve.wait_ge(s["h_hi_ready"], KC * e + j + 1)
            nc.vector.tensor_tensor(hT[:, j, SLOTS:], u, hT[:, j, 0:SLOTS].bitcast(F32),
                                    ALU.subtract).then_inc(s["h_ready"], 1)

        def dve_expert(dve, e, first, last):
            for t in range(TILES):
                n = t + DVE_AHEAD
                if n % 2 == 0 and not (last and n >= TILES):
                    split_lo(dve, nc.vector, e + n // TILES, n % TILES)
                dve_sum(dve, e, t, first)
                if t < FIRST_DOWN and t % 2:
                    dve_gate(dve, e, t // 2)
                    if t == FIRST_DOWN - 1:
                        dve_h(dve, e, KC - 1)
                if t < FIRST_DOWN and t % 2 == 0 and t:
                    dve_h(dve, e, t // 2 - 1)
                if t == TURN_X + 1 and not last:
                    dve_x(dve, e + 1)

        def pool_gather(pool, e):
            nc.gpsimd.tensor_copy(cur_s[:], col_s[:, bass.ds(e, 1)])
            nc.gpsimd.tensor_copy(cur_p[:], col_p[:, bass.ds(e, 1)]).then_inc(s["cur_ready"], 1)
            pool.wait_ge(s["cur_ready"], e + 1)
            st.stand(pool)
            nc.gpsimd.indirect_dma_start(x_s[:], None, h2[1], bass.IndirectOffsetOnAxis(ap=cur_s[:], axis=0)).then_inc(s["gathered_s"], 16)
            nc.gpsimd.indirect_dma_start(x_p[:], None, h2[0], bass.IndirectOffsetOnAxis(ap=cur_p[:], axis=0)).then_inc(s["gathered_p"], 16)

        def pool_add(pool, e, first):
            if not first:
                pool.wait_ge(s["added_s"], 16 * e)
                pool.wait_ge(s["added_p"], 16 * e)
            nc.gpsimd.tensor_copy(out_s[:], col_s[:, bass.ds(e, 1)])
            nc.gpsimd.tensor_copy(out_p[:], col_p[:, bass.ds(e, 1)]).then_inc(s["out_ready"], 1)
            pool.wait_ge(s["out_ready"], e + 1)
            pool.wait_ge(s["y_moved"], KC * (e + 1) + CR)
            st.stand(pool)
            nc.gpsimd.indirect_dma_start(x3[1], bass.IndirectOffsetOnAxis(ap=out_s[:], axis=0), y_s[:], None,
                                         compute_op=ALU.add).then_inc(s["added_s"], 16)
            nc.gpsimd.indirect_dma_start(x3[0], bass.IndirectOffsetOnAxis(ap=out_p[:], axis=0), y_p[:], None,
                                         compute_op=ALU.add).then_inc(s["added_p"], 16)

        def pool_expert(pool, e, first, last):
            for t in range(TILES):
                n = t + AHEAD
                if n % 2 and not (last and n >= TILES):
                    split_lo(pool, nc.gpsimd, e + n // TILES, n % TILES)
                if t == ADD and not first:
                    pool_add(pool, e - 1, False)
                if t == GATHER and not last:
                    pool.wait_ge(s["x_turned"], e + 1)
                    pool.wait_ge(s["gathered_s"], 16 * (e + 1))
                    pool.wait_ge(s["gathered_p"], 16 * (e + 1))
                    pool_gather(pool, e + 1)

        def pe_turn_x(pe, e):
            pe.wait_ge(s["gathered_s"], 16 * (e + 1))
            pe.wait_ge(s["gathered_p"], 16 * (e + 1))
            for k in range(KC):
                dst = X[:, k // BANKX, (k % BANKX) * SLOTS:(k % BANKX + 1) * SLOTS]
                nc.tensor.transpose(dst[:, 0:CAP_S], x_s[:, k * P:(k + 1) * P], C.ident[:])
                mm = nc.tensor.transpose(dst[:, CAP_S:], x_p[:, k * P:(k + 1) * P], C.ident[0:CAP_P, 0:CAP_P])
            mm.then_inc(s["x_turned"], 1)

        def pe_turn_y(pe, e, d):
            pe.wait_ge(s["summed"], TILES * e + FIRST_DOWN + d + 1 + CR)
            pe.wait_ge(s["y_moved"], KC * e + d - 1 + CR)
            nc.tensor.transpose(Y[d % 2][:, 0, :], yT[:, d % 2, 0:CAP_S], C.ident[:])
            nc.tensor.transpose(Y[d % 2][0:CAP_P, 1, :], yT[:, d % 2, CAP_S:], C.ident[:]).then_inc(s["y_turned"], 1)

        def pe_tile(pe, e, t):
            i, bank = t % RING, out[t % BANKS]
            if t == 0:
                pe.wait_ge(s["xT_lo"], 3 * (e + 1))
            pe.wait_ge(*lo_done(e, t))
            pe.wait_ge(s["summed"], TILES * e + t - BANKS + 1 + CR)
            B = xT if t < FIRST_DOWN else hT
            for k in range(KC):
                if t == FIRST_DOWN:
                    pe.wait_ge(s["h_ready"], KC * e + k + 1)
                nc.tensor.matmul(bank[:, 0:2 * SLOTS], w_hi[i][:, k, :], B[:, k, :], start=(k == 0), stop=False)
                mm = nc.tensor.matmul(bank[:, SLOTS:2 * SLOTS], w_lo[i][:, k, :], B[:, k, 0:SLOTS], start=False,
                                      stop=(k == KC - 1))
            mm.then_inc(s["tile_done"], 1)

        def pe_expert(pe, e, first, last):
            for t in range(TILES):
                pe_tile(pe, e, t)
                if t == 0 and not first:
                    pe_turn_y(pe, e - 1, KC - 1)
                if t > FIRST_DOWN:
                    pe_turn_y(pe, e, t - FIRST_DOWN - 1)
                if t == TURN_X and not last:
                    pe_turn_x(pe, e + 1)
            if last:
                pe_turn_y(pe, e, KC - 1)

        def find(dve, work, val, idx, waves, done):
            for w in range(waves):
                c = slice(8 * w, 8 * w + 8)
                if done + w:
                    dve.wait_ge(s["replaced"], done + w)
                nc.vector.max(val[:, c], work[:]).then_inc(s["max_found"], 1)
                dve.wait_ge(s["max_found"], done + w + 1)
                nc.vector.max_index(idx[:, c], val[:, c], work[:]).then_inc(s["index_found"], 1)
                dve.wait_ge(s["index_found"], done + w + 1)
                nc.vector.match_replace(work[:], val[:, c], work[:], -1.0).then_inc(s["replaced"], 1)

        lists = ((val_s, gate_s, CAP_S, out[0]), (idxf_s, col_s, CAP_S, out[1]),
                 (val_p, gate_p, CAP_P, out[2]), (idxf_p, col_p, CAP_P, X[:, 0, :]))

        with st.block() as block:

            @block.sync
            def _(sp):
                for p in range(RAW):
                    sp_load(sp, 0, p)
                for p in range(RAW, PIECES):
                    sp_reload(sp, 0, p)
                with sp.Fori(1, NE) as e:
                    for p in range(PIECES):
                        sp_reload(sp, e, p)
                sp.wait_ge(s["added_s"], 16 * NE)
                sp.wait_ge(s["added_p"], 16 * NE)

            @block.scalar
            def _(act):
                act.sem_inc(s["y_moved"], CR)
                for t in range(AHEAD):
                    split_hi(act, 0, t)
                act_x(act, 0)
                act_expert(act, 0, True, False)
                with act.Fori(1, NE - 1) as e:
                    act_expert(act, e, False, False)
                act_expert(act, NE - 1, False, True)

            @block.gpsimd
            def _(pool):
                nc.gpsimd.tensor_copy(work_s[:], aff[:, T_PROMPT:]).then_inc(s["work_ready"], 1)
                nc.gpsimd.tensor_copy(work_p[:], aff[:, 0:T_PROMPT]).then_inc(s["work_ready"], 1)
                for t in range(1, AHEAD, 2):
                    split_lo(pool, nc.gpsimd, 0, t)
                pool.wait_ge(s["columns_ready"], 4)
                pool_gather(pool, 0)
                pool_expert(pool, 0, True, False)
                with pool.Fori(1, NE - 1) as e:
                    pool_expert(pool, e, False, False)
                pool_expert(pool, NE - 1, False, True)
                pool_add(pool, NE - 1, False)

            @block.tensor
            def _(pe):
                pe.sem_inc(s["tile_done"], CR)
                pe.wait_ge(s["listed"], 2)
                for src, _, cap, dst in lists:
                    nc.tensor.transpose(dst[0:cap, 0:NE], src[:], C.ident[0:NE, 0:NE]).then_inc(s["turned"], 1)
                pe_turn_x(pe, 0)
                pe_expert(pe, 0, True, False)
                with pe.Fori(1, NE - 1) as e:
                    pe_expert(pe, e, False, False)
                pe_expert(pe, NE - 1, False, True)

            @block.vector
            def _(dve):
                for n in ("summed", "u_gated", "h_made"):
                    dve.sem_inc(s[n], CR)
                dve.wait_ge(s["work_ready"], 2)
                find(dve, work_s, val_s, idx_s, WAVES_S, 0)
                find(dve, work_p, val_p, idx_p, WAVES_P, WAVES_S)
                nc.vector.tensor_copy(idxf_s[:], idx_s[:]).then_inc(s["listed"], 1)
                nc.vector.tensor_copy(idxf_p[:], idx_p[:]).then_inc(s["listed"], 1)
                for n, (_, dst, cap, src) in enumerate(lists):
                    dve.wait_ge(s["turned"], n + 1)
                    nc.vector.tensor_copy(dst[0:cap, :], src[0:cap, 0:NE]).then_inc(s["columns_ready"], 1)
                for t in range(0, DVE_AHEAD, 2):
                    split_lo(dve, nc.vector, 0, t)
                dve_x(dve, 0)
                dve_expert(dve, 0, True, False)
                with dve.Fori(1, NE - 1) as e:
                    dve_expert(dve, e, False, False)
                dve_expert(dve, NE - 1, False, True)


def norm_out(nc, C, x3, final_g, y_prompt, y_sample):
    with Stage(nc, "no") as st:
        x = st.sb("x", [P, NT, D])
        gain, junk = st.sb("gain", [P, D]), st.sb("junk", [P, D])
        ssq, var, std, rstd = (st.sb(n, [P, NT]) for n in ("ssq", "var", "std", "rstd"))
        x_loaded = [st.sem(f"x_loaded{t}") for t in range(NT)]
        s = {n: st.sem(n) for n in ("gain_loaded", "ssq_ready", "var_ready", "std_ready", "rstd_ready", "y_ready", "y_stored")}

        def rows(pair, t):
            a, n = (pair[0], t) if t < NT_PROMPT else (pair[1], t - NT_PROMPT)
            return a[n * P:(n + 1) * P, :]

        with st.block() as block:

            @block.sync
            def _(sp):
                for t in range(NT):
                    sp.dma_start(x[:, t, :], rows(x3, t)).then_inc(x_loaded[t], 16)
                    if t == 0:
                        sp.dma_start(gain[:], final_g.rearrange("(a d) -> a d", a=1).broadcast_to([P, D])).then_inc(s["gain_loaded"], 16)
                for t in range(NT):
                    sp.wait_ge(s["y_ready"], t + 1)
                    sp.dma_start(rows((y_prompt[0], y_sample[0]), t), x[:, t, :]).then_inc(s["y_stored"], 16)
                sp.wait_ge(s["y_stored"], 16 * NT)

            @block.scalar
            def _(act):
                for t in range(NT):
                    act.wait_ge(x_loaded[t], 16)
                    if t:
                        act.wait_ge(s["ssq_ready"], t)
                    nc.scalar.activation(junk[:], x[:, t, :], ACT.Square, accum_out=ssq[:, t:t + 1]).then_inc(s["ssq_ready"], 1)
                    act.wait_ge(s["var_ready"], t + 1)
                    nc.scalar.activation(std[:, t:t + 1], var[:, t:t + 1], ACT.Sqrt).then_inc(s["std_ready"], 1)

            @block.vector
            def _(dve):
                dve.wait_ge(s["gain_loaded"], 16)
                for t in range(NT):
                    dve.wait_ge(s["ssq_ready"], t + 1)
                    nc.vector.tensor_scalar(var[:, t:t + 1], ssq[:, t:t + 1], 1.0 / D, EPS, ALU.mult, ALU.add).then_inc(s["var_ready"], 1)
                    dve.wait_ge(s["std_ready"], t + 1)
                    nc.vector.reciprocal(rstd[:, t:t + 1], std[:, t:t + 1]).then_inc(s["rstd_ready"], 1)
                    dve.wait_ge(s["rstd_ready"], t + 1)
                    nc.vector.scalar_tensor_tensor(out=x[:, t, :], in0=x[:, t, :], scalar=rstd[:, t:t + 1], in1=gain[:],
                                                   op0=ALU.mult, op1=ALU.mult).then_inc(s["y_ready"], 1)


def build(nc, I, y_prompt, y_sample):
    class C:
        pass

    def scratch(name, shape):
        return nc.dram_tensor(name, shape, F32).ap()

    ya, yb, m_a, m_ab = (scratch(n, (D, T)) for n in ("ya", "yb", "m_a", "m_ab"))
    x3 = scratch("x3_prompt", (T_PROMPT, D)), scratch("x3_sample", (T_SAMPLE, D))
    h2 = scratch("h2_prompt", (T_PROMPT, D)), scratch("h2_sample", (T_SAMPLE, D))
    w_in = I["w_in"][0]
    with Stage(nc, "all") as top:
        constants(nc, C, top, I["b_lb_logits"], I["b_onorm_g"], I["a_vnorm_g"])
        with Stage(nc, "trunk") as st:
            h_hi = st.sb("h_hi", [P, KC, T], F32R)
            h_lo = st.sb("h_lo", [P, KC, T], F32R)
            norm_in(nc, C, I["x_prompt"], I["x_sample"], I["norm1_g"], h_hi, h_lo)
            gmlp(nc, C, w_in, I["a_spatial_w"][0], I["a_spatial_b"][0], h_hi, h_lo, ya)
            merge(nc, "ma", w_in, COL_GA, I["w_branch_a"][0], ya, None, m_a, h_hi, h_lo)
            hgrn2(nc, C, w_in, h_hi, h_lo, yb)
            merge(nc, "mb", w_in, COL_GB, I["w_branch_b"][0], yb, m_a, m_ab, h_hi, h_lo)
        aff = top.sb("aff", [NE, T])
        with Stage(nc, "mixed") as st:
            x2 = st.sb("x2", [P, NT, D])
            residual(nc, C, I["x_prompt"], I["x_sample"], I["w_out"][0], m_ab, x2)
            route(nc, C, I["norm2_g"], I["w_router"][0], x2, x3, h2, aff)
        experts(nc, C, aff, h2, x3, I["w_exp_gate"][0], I["w_exp_up"][0], I["w_exp_down"][0])
        norm_out(nc, C, x3, I["final_g"], y_prompt, y_sample)


_INS = ["x_prompt", "x_sample", "norm1_g", "w_in", "a_vnorm_g", "a_spatial_w", "a_spatial_b", "b_lb_logits",
        "b_onorm_g", "w_branch_a", "w_branch_b", "w_out", "norm2_g", "w_router", "w_exp_gate", "w_exp_up",
        "w_exp_down", "final_g"]
_OUTS = [((1, T_PROMPT, D), "float32"), ((1, T_SAMPLE, D), "float32")]


def kernel(**inputs):
    import numpy as _np
    import concourse.bacc as _bacc
    from concourse import mybir as _mybir
    from concourse.bass_utils import run_bass_kernel_spmd as _run

    nc = _bacc.Bacc("TRN2", target_bir_lowering=False, num_devices=1)
    arrays, aps = {}, {}
    for name in _INS:
        a = _np.ascontiguousarray(inputs[name])
        arrays[f"in_{name}_dram"] = a
        aps[name] = nc.dram_tensor(f"in_{name}_dram", a.shape, _mybir.dt.from_np(a.dtype), kind="ExternalInput").ap()
    outs = [nc.dram_tensor(f"out_{i}_dram", shape, _mybir.dt.from_np(_np.dtype(dtype)), kind="ExternalOutput").ap()
            for i, (shape, dtype) in enumerate(_OUTS)]
    build(nc, aps, *outs)
    r = _run(nc, [arrays], core_ids=[0])
    return tuple(r.results[0][f"out_{i}_dram"] for i in range(len(_OUTS)))
```

```python
from contextlib import ExitStack

import concourse.bass as bass
from concourse import mybir

F32 = mybir.dt.float32
F32R = mybir.dt.float32r
U32 = mybir.dt.uint32
U8 = mybir.dt.uint8
ALU = mybir.AluOpType
ACT = mybir.ActivationFunctionType
AX = mybir.AxisListType

P = 128
D = 1024
KC = D // P
T_PROMPT = 256
T_SAMPLE = 1024
T = T_PROMPT + T_SAMPLE
NT = T // P
NT_PROMPT = T_PROMPT // P
GROUPS = D // P
HEADS = D // P
NE = 16
CAP_S = 2 * T_SAMPLE // NE
CAP_P = 2 * T_PROMPT // NE
SLOTS = CAP_S + CAP_P
HALF_S = T_SAMPLE // 2
EPS = 1e-6
PART = 320
PARTS = T // PART
LEVELS = 7
CREDIT = 8
COL_U, COL_V, COL_Q, COL_I, COL_ZF, COL_ZB, COL_GO, COL_GA, COL_GB = (j * D for j in range(9))
SEQS = ((0, NT_PROMPT), (NT_PROMPT, NT))


def cols(w, c0):
    return w.rearrange("(k p) n -> p k n", p=P)[:, :, bass.ds(c0, P)]


class Stage:

    def __init__(self, nc, name):
        self.nc, self.name, self.ctx, self.sems = nc, name, ExitStack(), []
        self.waited = None

    def __enter__(self):
        self.ctx.__enter__()
        return self

    def __exit__(self, *a):
        if self.sems and a[0] is None:
            for sem in self.sems:
                self.nc.gpsimd.sem_clear(sem)
                self.nc.release_semaphore(sem)
        return self.ctx.__exit__(*a)

    def sb(self, name, shape, dt=F32):
        return self.ctx.enter_context(self.nc.sbuf_tensor(f"{self.name}_{name}", shape, dt))

    def ps(self, name, shape, dt=F32):
        return self.ctx.enter_context(self.nc.psum_tensor(f"{self.name}_{name}", shape, dt))

    def sem(self, name):
        self.sems.append(self.nc.alloc_semaphore(f"{self.name}_{name}"))
        return self.sems[-1]

    def stand(self, eng):
        self.waited = self.waited or self.sem("waited")
        eng.sem_inc(self.waited, 1)

    def block(self):
        return self.nc.Block()


def weight_buffers(st, i, with_raw=True):
    raw = st.sb(f"w_raw{i}", [P, KC, P]) if with_raw else None
    return raw, st.sb(f"w_hi{i}", [P, KC, P], F32R), st.sb(f"w_lo{i}", [P, KC, P], F32R)


class WeightStream:

    def __init__(self, st, per, first_tile=None):
        self.st, self.per = st, per
        self.prepared = int(first_tile is not None)
        ring = 2 if per % 2 == 0 else 3
        self.raw_slot = [t % 2 for t in range(per)]
        self.slot = [t % ring for t in range(per)]
        if first_tile is None:
            first_tile = weight_buffers(st, 0)
        self.raw, self.hi, self.lo = ([x] for x in first_tile)
        for i in range(1, ring):
            raw, hi, lo = weight_buffers(st, i, i < 2)
            self.raw.append(raw)
            self.hi.append(hi)
            self.lo.append(lo)
        self.out = [st.ps(f"proj{i}", [P, 512]) for i in range(2)]
        self.loaded = [st.sem(f"w_loaded{i}") for i in range(2)]
        self.hi_ready = st.sem("w_hi_ready")
        self.lo_ready = st.sem("w_lo_ready")
        self.group_done = st.sem("proj_group_done")
        self.bank_free = [st.sem(f"proj_bank_free{i}") for i in range(2)]

    def back(self, slots, t):
        return next(d for d in range(1, self.per + 1) if slots[(t - d) % self.per] == slots[t])

    def load(self, sp, r, t, src):
        n = self.per * r + t - self.back(self.raw_slot, t)
        sp.wait_ge(self.hi_ready, n + 1 + CREDIT)
        sp.wait_ge(self.lo_ready, n + 1 + CREDIT)
        self.st.stand(sp)
        sp.dma_start(self.raw[self.raw_slot[t]][:], src).then_inc(self.loaded[self.raw_slot[t]], 16)

    def split_hi(self, nc, act, r, t):
        rs, s = self.raw_slot[t], self.slot[t]
        n = self.per * r + t - self.back(self.slot, t)
        turn = self.raw_slot.count(rs) * r + self.raw_slot[:t + 1].count(rs)
        act.wait_ge(self.group_done, PARTS * (n + 1 + CREDIT))
        act.wait_ge(self.loaded[rs], 16 * turn)
        nc.scalar.activation(self.hi[s][:], self.raw[rs][:], ACT.Copy).then_inc(self.hi_ready, 1)

    def split_lo(self, nc, pool, r, t):
        rs, s = self.raw_slot[t], self.slot[t]
        pool.wait_ge(self.hi_ready, self.per * r + t + 1 + CREDIT)
        nc.gpsimd.tensor_tensor(self.lo[s][:], self.raw[rs][:], self.hi[s][:].bitcast(F32),
                                ALU.subtract).then_inc(self.lo_ready, 1)

    def multiply(self, nc, pe, r, t, part, x_hi, x_lo, rows=None):
        g = PARTS * t + part
        s, b = self.slot[t], g % 2
        if part == 0:
            pe.wait_ge(self.lo_ready, self.per * r + t + 1 + CREDIT)
        pe.wait_ge(self.bank_free[b], PARTS // 2 * self.per * r + g // 2 + CREDIT)
        out, c = self.out[b][:, 0:PART], slice(part * PART, (part + 1) * PART)
        for k in range(KC):
            if rows is not None:
                rows.ready(pe, k + 1)
            nc.tensor.matmul(out, self.hi[s][:, k, :], x_hi[:, k, c], start=(k == 0), stop=False)
            nc.tensor.matmul(out, self.hi[s][:, k, :], x_lo[:, k, c], start=False, stop=False)
            mm = nc.tensor.matmul(out, self.lo[s][:, k, :], x_hi[:, k, c], start=False, stop=(k == KC - 1))
        mm.then_inc(self.group_done, 1)

    def result(self, eng, r, t, part):
        g = PARTS * t + part
        eng.wait_ge(self.group_done, PARTS * self.per * r + g + 1 + PARTS * CREDIT)
        return self.out[g % 2][:, 0:PART], self.bank_free[g % 2]

    def moved(self, eng, r, t):
        for b in range(2):
            eng.wait_ge(self.bank_free[b], PARTS // 2 * (self.per * r + t + 1) + CREDIT)

    def pe_credit(self, pe):
        pe.sem_inc(self.group_done, PARTS * CREDIT)

    def act_credit(self, act):
        act.sem_inc(self.hi_ready, CREDIT + self.prepared)
        for b in range(2):
            act.sem_inc(self.bank_free[b], CREDIT)

    def pool_credit(self, pool):
        pool.sem_inc(self.lo_ready, CREDIT + self.prepared)

    def sp_credit(self, sp):
        if self.prepared:
            sp.sem_inc(self.loaded[0], 16)


def norm_in(nc, C, x_prompt, x_sample, norm1_g, b_lb_logits, b_onorm_g, a_vnorm_g, h_hi, h_lo, next_tile):
    PAIRS = NT // 2
    with Stage(nc, "n1") as st:
        x = st.sb("x", [P, NT, D])
        gain = st.sb("gain", [P, D])
        junk = st.sb("junk", [P, D])
        xn = st.sb("xn", [P, 2, D])
        ssq, var, std, rstd = (st.sb(n, [P, NT]) for n in ("ssq", "var", "std", "rstd"))
        xT = st.ps("xT", [P, 2, KC, P])
        x_loaded = [st.sem(f"x_loaded{j}") for j in range(PAIRS)]
        w_raw, w_hi, w_lo = C.first_tile
        w_loaded, w_hi_ready, w_lo_ready = (st.sem(n) for n in ("w_loaded", "w_hi_ready", "w_lo_ready"))
        gain_loaded, ssq_ready, var_ready, std_ready = (st.sem(n) for n in ("gain_loaded", "ssq_ready", "var_ready", "std_ready"))
        rstd_ready, xn_ready, xT_ready, hi_ready, lo_ready = (st.sem(n) for n in ("rstd_ready", "xn_ready", "xT_ready", "hi_ready", "lo_ready"))
        def load(sp):
            sp.dma_start(x[:, 0:2, :], x_prompt.rearrange("b (t p) d -> p (b t) d", p=P)).then_inc(x_loaded[0], 16)
            sp.dma_start(gain[:], norm1_g.broadcast_to([P, D])).then_inc(gain_loaded, 16)
            xs = x_sample.rearrange("b (t p) d -> p (b t) d", p=P)
            for j in range(1, PAIRS):
                sp.dma_start(x[:, 2 * j:2 * j + 2, :], xs[:, 2 * j - 2:2 * j, :]).then_inc(x_loaded[j], 16)
            sp.dma_start(w_raw[:], next_tile).then_inc(w_loaded, 16)

        constants(nc, C, b_lb_logits, b_onorm_g, a_vnorm_g, load)
        with st.block() as block:

            @block.gpsimd
            def _(pool):
                pool.wait_ge(w_hi_ready, 1)
                nc.gpsimd.tensor_tensor(w_lo[:], w_raw[:], w_hi[:].bitcast(F32), ALU.subtract).then_inc(w_lo_ready, 1)
                pool.wait_ge(w_lo_ready, 1)

            @block.scalar
            def _(act):
                def square(t):
                    act.wait_ge(x_loaded[t // 2], 16)
                    if t:
                        act.wait_ge(ssq_ready, t)
                    nc.scalar.activation(junk[:], x[:, t, :], ACT.Square,
                                         accum_out=ssq[:, t:t + 1]).then_inc(ssq_ready, 1)

                def root(t):
                    act.wait_ge(var_ready, t + 1)
                    nc.scalar.activation(std[:, t:t + 1], var[:, t:t + 1], ACT.Sqrt).then_inc(std_ready, 1)

                square(0)
                root(0)
                for t in range(NT):
                    if t + 1 < NT:
                        square(t + 1)
                        root(t + 1)
                    act.wait_ge(xT_ready, t + 1)
                    nc.scalar.activation(h_hi[:, :, t * P:(t + 1) * P], xT[:, t % 2], ACT.Copy).then_inc(hi_ready, 1)
                    if t == NT // 2:
                        act.wait_ge(w_loaded, 16)
                        nc.scalar.activation(w_hi[:], w_raw[:], ACT.Copy).then_inc(w_hi_ready, 1)

            @block.vector
            def _(dve):
                def scale(t):
                    dve.wait_ge(ssq_ready, t + 1)
                    nc.vector.tensor_scalar(var[:, t:t + 1], ssq[:, t:t + 1], 1.0 / D, EPS, ALU.mult,
                                            ALU.add).then_inc(var_ready, 1)
                    dve.wait_ge(std_ready, t + 1)
                    nc.vector.reciprocal(rstd[:, t:t + 1], std[:, t:t + 1]).then_inc(rstd_ready, 1)
                    dve.wait_ge(rstd_ready, t + 1)
                    if t >= 2:
                        dve.wait_ge(xT_ready, t - 1)
                    nc.vector.scalar_tensor_tensor(out=xn[:, t % 2, :], in0=x[:, t, :], scalar=rstd[:, t:t + 1],
                                                   in1=gain[:], op0=ALU.mult, op1=ALU.mult).then_inc(xn_ready, 1)

                dve.wait_ge(gain_loaded, 16)
                scale(0)
                for t in range(NT):
                    if t + 1 < NT:
                        scale(t + 1)
                    dve.wait_ge(hi_ready, t + 1)
                    c = slice(t * P, (t + 1) * P)
                    nc.vector.tensor_tensor(h_lo[:, :, c], xT[:, t % 2], h_hi[:, :, c].bitcast(F32),
                                            ALU.subtract).then_inc(lo_ready, 1)

            @block.tensor
            def _(pe):
                for t in range(NT):
                    pe.wait_ge(xn_ready, t + 1)
                    if t >= 2:
                        pe.wait_ge(lo_ready, t - 1)
                    for k in range(KC):
                        mm = nc.tensor.transpose(xT[:, t % 2, k, :], xn[:, t % 2, k * P:(k + 1) * P], C.ident[:])
                    mm.then_inc(xT_ready, 1)


def constant_buffers(C, st):
    C.ident = st.sb("ident", [P, P])
    C.ones = st.sb("ones", [P, P])
    C.eps = st.sb("eps", [P, 1])
    C.mask = st.sb("mask", [P, LEVELS + 1, P], U8)
    C.lb = st.sb("lb", [P, 2, HEADS])
    C.one_minus_lb = st.sb("one_minus_lb", [P, 2, HEADS])
    C.onorm = st.sb("onorm", [P, 1])
    C.vnorm = st.sb("vnorm", [P, GROUPS])


def constants(nc, C, b_lb_logits, b_onorm_g, a_vnorm_g, load_ahead):
    with Stage(nc, "const") as s:
        logits = s.sb("logits", [P, 2, HEADS])
        top, expo, prob = (s.sb(n, [P, 2, HEADS]) for n in ("top", "expo", "prob"))
        same = s.sb("same", [P, LEVELS + 1, P])
        diff = s.sb("diff", [P, LEVELS + 1, P])
        cut = s.sb("cut", [P, LEVELS + 1, P])
        loaded, filled, half, made, lb_step = (s.sem(n) for n in ("loaded", "filled", "half", "made", "lb_step"))
        expo_ready = s.sem("expo_ready")
        with s.block() as block:

            @block.sync
            def _(sp):
                sp.dma_start(logits[:], b_lb_logits.rearrange("z a (h p) -> p (z a) h", p=P), allow_slow_non_contiguous=True).then_inc(loaded, 16)
                sp.dma_start(C.onorm[:], b_onorm_g.rearrange("a p -> p a"), allow_slow_non_contiguous=True).then_inc(loaded, 16)
                sp.dma_start(C.vnorm[:], a_vnorm_g.rearrange("a (g p) -> p (a g)", p=P), allow_slow_non_contiguous=True).then_inc(loaded, 16)
                load_ahead(sp)
                sp.wait_ge(loaded, 48)

            @block.gpsimd
            def _(pool):
                nc.gpsimd.memset(C.ones[:], 1.0)
                nc.gpsimd.memset(C.eps[:], EPS)
                nc.gpsimd.memset(same[:], 1.0).then_inc(filled, 1)
                pool.wait_ge(filled, 1)
                for l in range(LEVELS):
                    b = 1 << l
                    blocks = cut[:, l, :].rearrange("p (n b) -> p n b", b=b)
                    ones = same[:, l, :].rearrange("p (n b) -> p n b", b=b)
                    nc.gpsimd.affine_select(out=blocks, in_=ones, compare_op=ALU.is_ge, fill=0.0, base=0,
                                            pattern=[[-b, P // b], [0, b]], channel_multiplier=1).then_inc(half, 1)
                pool.wait_ge(half, LEVELS)
                for l in range(LEVELS):
                    b = 1 << l
                    blocks = cut[:, l, :].rearrange("p (n b) -> p n b", b=b)
                    ones = same[:, l, :].rearrange("p (n b) -> p n b", b=b)
                    nc.gpsimd.affine_select(out=ones, in_=blocks, compare_op=ALU.is_ge, fill=0.0, base=b - 1,
                                            pattern=[[b, P // b], [0, b]], channel_multiplier=-1).then_inc(made, 1)

            @block.vector
            def _(dve):
                dve.wait_ge(made, LEVELS)
                nc.vector.tensor_copy(C.ident[:], same[:, 0, :])
                nc.vector.tensor_copy(C.mask[:, 0, :], same[:, 0, :])
                nc.vector.tensor_tensor(diff[:, 1:, :], same[:, 1:, :], same[:, 0:LEVELS, :], ALU.subtract).then_inc(lb_step, 1)
                dve.wait_ge(lb_step, 1)
                nc.vector.tensor_copy(C.mask[:, 1:, :], diff[:, 1:, :])
                dve.wait_ge(loaded, 48)
                nc.vector.tensor_copy(top[:], logits[:]).then_inc(lb_step, 1)
                dve.wait_ge(lb_step, 2)
                nc.vector.tensor_tensor(logits[:], logits[:], top[:], ALU.subtract).then_inc(lb_step, 1)
                dve.wait_ge(expo_ready, 1)
                nc.vector.reciprocal(top[:], expo[:]).then_inc(lb_step, 1)
                dve.wait_ge(lb_step, 4)
                nc.vector.tensor_tensor(prob[:], expo[:], top[:], ALU.mult).then_inc(lb_step, 1)
                dve.wait_ge(lb_step, 5)
                nc.vector.tensor_tensor(C.lb[:], prob[:], prob[:], ALU.subtract).then_inc(lb_step, 1)
                dve.wait_ge(lb_step, 6)
                nc.vector.tensor_scalar(C.one_minus_lb[:], C.lb[:], -1.0, 1.0, ALU.mult, ALU.add)

            @block.scalar
            def _(act):
                act.wait_ge(lb_step, 3)
                nc.scalar.activation(expo[:], logits[:], ACT.Exp).then_inc(expo_ready, 1)


def pairs(ap, b):
    return ap.rearrange("p (n two b) -> p n two b", two=2, b=b)


def crossed(both, row, t0, n, b):
    ap = both[:]
    return bass.AP(tensor=ap.tensor, offset=ap.offset + t0, ap=[list(ap.ap[0]), [2 * b, n // (2 * b)], [row + b, 2], [1, b]])


def over(ap, n):
    return ap.unsqueeze(2).broadcast_to([P, ap.shape[1], n])


def hgrn2(nc, C, w_in, h_hi, h_lo, yb_dram, next_tile):
    order = (COL_Q, COL_ZF, COL_ZB, COL_I, COL_GO)
    TQ, TZF, TZB, TI, TGO = range(5)
    with Stage(nc, "hg") as st:
        W = WeightStream(st, len(order), C.first_tile)
        q, vT, v, so, A, Kt_f, Kt_b = (st.sb(n, [P, T]) for n in ("q", "vT", "v", "so", "A", "Kt_f", "Kt_b"))
        f_f, f_b, tot_f, tot_b = (st.sb(n, [P, T]) for n in ("f_f", "f_b", "tot_f", "tot_b"))
        Q = st.sb("Q", [P, 2, T])
        Q_b, Q_f = Q[:, 0, :], Q[:, 1, :]
        K_odd, K_even, K_rest = (st.sb(n, [P, T]) for n in ("K_odd", "K_even", "K_rest"))
        go = vT
        k_f, k_b, K_f, K_b = K_odd, K_even, K_even, K_rest
        S_f = st.sb("S_f", [P, NT, P])
        S_b = st.sb("S_b", [P, NT, P])
        k_sum, sq, rt, y = Kt_f, tot_f, tot_b, Kt_b
        G = st.ps("G", [P, 6, 4, P])
        Gc = G[:].rearrange("p b c t -> p (b c) t")

        def K_at(j):
            return (K_even, K_odd)[j % 2]

        def quarters(x, j):
            n = 4 if j < LEVELS else 2
            return x[:].rearrange("p (m n b) -> p m n b", n=n, b=1 << (j - 1)), n

        def bank_cols(base, c):
            return Gc[:, 4 * base + c, :]

        def spans(base):
            return [(G[:, base + j, 0:min(4, NT - 4 * j), :], 4 * j, min(4 * j + 4, NT)) for j in range(3)]

        names = ("v_ready", "gates_ready", "Q_ready", "K_ready",
                 "tot_ready", "k_sum_ready", "K_copied", "A_merged", "gla_step", "v_step", "Kt_ready", "S_ready", "sq_ready",
                 "rt_ready", "y_ready", "y_stored", "A_clear", "so_used", "silu_ready")
        s = {n: st.sem(n) for n in names}
        STEPS = 13
        DIAG, KTF, KTB, STATE, OUT, ONES = 0, 8, 9, 10, 11, 12
        NQ = 2 * (LEVELS + 1)
        NY = 3
        state_f = [c for a, z in SEQS for c in range(a, z - 1)]
        state_b = [c for a, z in SEQS for c in range(z - 1, a, -1)]
        firsts_f, firsts_b = [a for a, _ in SEQS], [z - 1 for _, z in SEQS]
        def tiles_with(g):
            return [(g, TGO)] + [(g + 1, t) for t in (TQ, TZF, TZB, TI)]

        tiles_before, tiles_last = tiles_with(-1)[1:], [(HEADS - 1, TGO)]

        def following(r, t):
            return (r, t + 1) if t < TGO else (r + 1, TQ)

        def sp_round(sp, r, done, first=False):
            for t, c in enumerate(order):
                if not (first and t == 0):
                    W.load(sp, r, t, cols(w_in, c + r * P))
                if t == 0 and done is not None:
                    store(sp, done)

        def store(sp, g):
            sp.wait_ge(s["y_ready"], NY * (g + 1) + CREDIT)
            st.stand(sp)
            sp.dma_start(yb_dram[bass.ds(g * P, P), :], y[:]).then_inc(s["y_stored"], 16)

        def act_buffers(act, r, t):
            if t == TI:
                act.wait_ge(s["v_step"], r + CREDIT)
                act.wait_ge(s["silu_ready"], r + CREDIT)
            if t == TQ:
                act.wait_ge(s["gla_step"], STEPS * (r - 1) + DIAG + 1 + 2 * STEPS)
                act.wait_ge(s["Q_ready"], NQ * (r - 1) + 2 + 2 * NQ)
            if t == TZF:
                act.wait_ge(s["gla_step"], STEPS * (r - 1) + KTF + 1 + 2 * STEPS)
                act.wait_ge(s["Q_ready"], NQ * (r - 1) + 4 + 2 * NQ)
            if t == TZB:
                act.wait_ge(s["gla_step"], STEPS * (r - 1) + KTB + 1 + 2 * STEPS)
            if t in (TZF, TZB):
                act.wait_ge(s["K_ready"], LEVELS * (r - 1) + 1 + 2 * LEVELS)
            if t == TGO:
                act.wait_ge(s["so_used"], r + CREDIT)
                act.wait_ge(s["v_step"], r + 1 + CREDIT)

        def act_move(act, r, t, part):
            out, free = W.result(act, r, t, part)
            c = slice(part * PART, (part + 1) * PART)
            if t == TI:
                nc.scalar.activation(vT[:, c], out, ACT.Copy).then_inc(free, 1)
            elif t == TQ:
                nc.scalar.activation(q[:, c], out, ACT.Copy).then_inc(free, 1)
            elif t in (TZF, TZB):
                f, k = ((f_f, k_f), (f_b, k_b))[t == TZB]
                nc.scalar.activation(f[:, c], out, ACT.Sigmoid)
                nc.scalar.activation(k[:, c], out, ACT.Sigmoid, scale=-1.0).then_inc(free, 1)
            else:
                nc.scalar.activation(so[:, c], out, ACT.Sigmoid)
                nc.scalar.activation(go[:, c], out, ACT.Copy).then_inc(free, 1)

        def dve_project(dve, r):
            every = [x[:].rearrange("p (n two) -> p n two", two=2) for x in (K_odd, K_even, K_rest)]
            odd, even, rest = every
            for z, (f, k, t) in enumerate(((f_f, odd, TZF), (f_b, even, TZB))):
                lb, om = C.lb[:, z, bass.ds(r, 1)], C.one_minus_lb[:, z, bass.ds(r, 1)]
                for b in range(2):
                    dve.wait_ge(W.bank_free[b], PARTS // 2 * (W.per * r + t + 1) + CREDIT)
                nc.vector.tensor_scalar(f[:], f[:], om, lb, ALU.mult, ALU.add).then_inc(s["gates_ready"], 1)
                nc.vector.tensor_scalar(rest[:, :, 1 - z], k[:, :, 1 - z], om, None, ALU.mult).then_inc(s["gates_ready"], 1)
                if z:
                    dve.wait_ge(s["gates_ready"], 6 * r + 2)
                nc.vector.tensor_scalar(odd[:, :, z], k[:, :, z], om, None, ALU.mult).then_inc(s["gates_ready"], 1)

        def dve_output_gate(dve, r):
            W.moved(dve, r, TGO)
            nc.vector.tensor_tensor(so[:], go[:], so[:], ALU.mult).then_inc(s["silu_ready"], 1)

        def pe_values(pe, r):
            for b in range(2):
                pe.wait_ge(W.bank_free[b], PARTS // 2 * (W.per * r + TI + 1) + CREDIT)
            pe.wait_ge(s["y_ready"], NY * r + CREDIT)
            for c in range(NT):
                mm = nc.tensor.transpose(bank_cols(0, c), vT[:, c * P:(c + 1) * P], C.ident[:])
            mm.then_inc(s["v_step"], 1)

        def act_values(act, r):
            act.wait_ge(s["v_step"], r + 1 + CREDIT)
            act.wait_ge(s["gla_step"], STEPS * (r - 1) + OUT + 1 + 2 * STEPS)
            nc.scalar.activation(v[:].rearrange("p (c t) -> p c t", t=P), Gc[:, 0:NT, :], ACT.Copy).then_inc(s["v_ready"], 1)

        def gla_at(g, step):
            return STEPS * g + step + 1 + 2 * STEPS

        def pe_step(pe, g, j):
            base = 3 * (j % 2)
            if j == DIAG:
                pe.wait_ge(s["v_ready"], g + 1)
                pe.wait_ge(s["k_sum_ready"], g + 1)
                for c in range(NT):
                    t = slice(c * P, (c + 1) * P)
                    mm = nc.tensor.matmul(bank_cols(0, c), k_sum[:, t], q[:, t], start=True, stop=True)
            elif j <= LEVELS:
                pe.wait_ge(s["Q_ready"], NQ * g + 2 * j + 2 * NQ)
                if j == 1:
                    pe.wait_ge(s["rt_ready"], g + CREDIT)
                    pe.wait_ge(s["gates_ready"], 6 * (g + 1))
                else:
                    pe.wait_ge(s["K_ready"], LEVELS * g + j - 1 + 2 * LEVELS)
                    pe.wait_ge(s["A_merged"], 8 * g + j - 1)
                b = 1 << (j - 1)
                for c in range(NT):
                    mm = nc.tensor.matmul(bank_cols(base, c), K_at(j)[:, c * P:(c + 1) * P], crossed(Q, T, c * P, P, b),
                                          start=True, stop=True)
            elif j in (KTF, KTB):
                pe.wait_ge(s["A_merged"], 8 * g + j - 1)
                pe.wait_ge(s["K_ready"], LEVELS * g + LEVELS + 2 * LEVELS)
                k = (K_f, K_b)[j == KTB]
                for c in range(NT):
                    mm = nc.tensor.transpose(bank_cols(base, c), k[:, c * P:(c + 1) * P], C.ident[:])
            elif j == STATE:
                pe.wait_ge(s["Kt_ready"], 2 * g + 2)
                for n, (Kt, c) in enumerate([(Kt_f, c) for c in state_f] + [(Kt_b, c) for c in state_b]):
                    t = slice(c * P, (c + 1) * P)
                    mm = nc.tensor.matmul(Gc[:, n, :], Kt[:, t], v[:, t], start=True, stop=True)
            elif j == OUT:
                pe.wait_ge(s["S_ready"], 16 * (g + 1))
                pe.wait_ge(s["A_merged"], 8 * g + 8)
                pe.wait_ge(s["Q_ready"], NQ * g + NQ + 2 * NQ)
                for c in range(NT):
                    t = slice(c * P, (c + 1) * P)
                    terms = [(v[:, t], A[:, t])]
                    if c not in firsts_f:
                        terms.append((S_f[:, c, :], Q_f[:, t]))
                    if c not in firsts_b:
                        terms.append((S_b[:, c, :], Q_b[:, t]))
                    for n, (lhs, rhs) in enumerate(terms):
                        mm = nc.tensor.matmul(bank_cols(0, c), lhs, rhs, start=(n == 0), stop=(n == len(terms) - 1))
            else:
                pe.wait_ge(s["sq_ready"], g + 1)
                for a in range(0, T, 512):
                    z = min(a + 512, T)
                    mm = nc.tensor.matmul(G[:, 3 + a // 512, :, :].rearrange("p c t -> p (c t)")[:, 0:z - a],
                                          C.ones[:], sq[:, a:z], start=True, stop=True)
            mm.then_inc(s["gla_step"], 1)

        def pe_round(pe, tiles, g):
            for n in range(PARTS * len(order)):
                if n < PARTS * len(tiles):
                    W.multiply(nc, pe, *tiles[n // PARTS], n % PARTS, h_hi, h_lo)
                if g is not None and n < STEPS:
                    pe_step(pe, g, n)
            if tiles[-1][1] == TI:
                pe_values(pe, tiles[-1][0])

        def act_gla(act, g, j):
            if j in (KTF, KTB):
                act.wait_ge(s["gla_step"], gla_at(g, j))
                Kt = (Kt_f, Kt_b)[j == KTB]
                base = 12 * (j % 2)
                if j == KTB:
                    act.wait_ge(s["y_stored"], 16 * (g + CREDIT))
                nc.scalar.activation(Kt[:].rearrange("p (c t) -> p c t", t=P), Gc[:, base:base + NT, :],
                                     ACT.Copy).then_inc(s["Kt_ready"], 1)
            elif j == OUT:
                act.wait_ge(s["gla_step"], gla_at(g, OUT))
                nc.scalar.activation(sq[:].rearrange("p (c t) -> p c t", t=P), Gc[:, 0:NT, :],
                                     ACT.Square).then_inc(s["sq_ready"], 1)
            elif j == ONES:
                act.wait_ge(s["gla_step"], gla_at(g, ONES))
                nc.scalar.activation(rt[:].rearrange("p (c t) -> p c t", t=P), Gc[:, 12:12 + NT, :], ACT.Sqrt,
                                     bias=C.eps[:], scale=1.0 / P).then_inc(s["rt_ready"], 1)

        def act_round(act, tiles, g):
            for n in range(PARTS * len(order)):
                if n < PARTS * len(tiles):
                    r, t = tiles[n // PARTS]
                    if n % PARTS == 0:
                        W.split_hi(nc, act, *following(r, t))
                        act_buffers(act, r, t)
                    act_move(act, r, t, n % PARTS)
                if g is not None:
                    act_gla(act, g, n)
            if tiles[-1][1] == TI:
                act_values(act, tiles[-1][0])

        def pool_round(pool, tiles, g):
            levels = list(range(1, LEVELS + 1))
            if g is not None:
                pool.wait_ge(s["gates_ready"], 6 * (g + 1))
                pool.wait_ge(s["gla_step"], gla_at(g - 1, STATE))
                nc.gpsimd.tensor_tensor(k_sum[:], K_odd[:], K_rest[:], ALU.add).then_inc(s["k_sum_ready"], 1)
            for i in range(len(order)):
                if i < len(tiles):
                    W.split_lo(nc, pool, *following(*tiles[i]))
                if g is not None:
                    for j in levels[PARTS * i:PARTS * (i + 1)]:
                        pool_level(pool, g, j)

        def pool_level(pool, g, j):
            pool.wait_ge(s["K_copied"], LEVELS * g + j)
            if j >= 2:
                pool.wait_ge(s["K_ready"], LEVELS * g + j - 1 + 2 * LEVELS)
            else:
                pool.wait_ge(s["k_sum_ready"], g + 1)
            pool.wait_ge(s["tot_ready"], 2 * (LEVELS * g + j))
            (old, n), (new, _), (rest, _) = quarters(K_at(j), j), quarters(K_at(j + 1), j), quarters(K_rest, j)
            for i in range(n):
                F, tot = ((f_f, tot_f), (f_b, tot_b))[i % 2]
                total = total_of(F, tot, j - 1).rearrange("p (m n) -> p m n", n=n)[:, :, i ^ 1]
                dst = new if i in (0, 3) else rest
                op = nc.gpsimd.tensor_tensor(dst[:, :, i, :], old[:, :, i, :], over(total, 1 << (j - 1)), ALU.mult)
            op.then_inc(s["K_ready"], 1)

        def dve_copy(dve, g, j):
            if j >= 2:
                dve.wait_ge(s["gla_step"], gla_at(g, j - 1))
                dve.wait_ge(s["K_ready"], LEVELS * g + j - 1 + 2 * LEVELS)
                st.stand(dve)
            (new, n), (rest, _) = quarters(K_at(j + 1), j), quarters(K_rest, j)
            c = slice(1, 3) if n == 4 else slice(1, 2)
            nc.vector.tensor_copy(new[:, :, c, :], rest[:, :, c, :]).then_inc(s["K_copied"], 1)

        tot_at = [0]
        for l in range(1, LEVELS + 1):
            tot_at.append(tot_at[-1] + (T >> l))

        def total_of(F, tot, l):
            return F[:] if l == 0 else tot[:, tot_at[l - 1]:tot_at[l]]

        def level_total(F, tot, j):
            return total_of(F, tot, j - 1).rearrange("p (n two) -> p n two", two=2)

        def dve_start(dve, g):
            dve.wait_ge(s["gates_ready"], 6 * (g + 1))
            for b in range(2):
                dve.wait_ge(W.bank_free[b], PARTS // 2 * (W.per * g + TQ + 1) + CREDIT)
            dve.wait_ge(s["gla_step"], gla_at(g - 1, OUT))
            dve.wait_ge(s["rt_ready"], g + CREDIT)
            nc.vector.tensor_tensor(Q_f[:], q[:], f_f[:], ALU.mult).then_inc(s["Q_ready"], 1)
            nc.vector.tensor_tensor(Q_b[:], q[:], f_b[:], ALU.mult).then_inc(s["Q_ready"], 1)
            for l in range(1, LEVELS + 1):
                if l >= 2:
                    dve.wait_ge(s["tot_ready"], 2 * (LEVELS * g + l - 1))
                for F, tot in ((f_f, tot_f), (f_b, tot_b)):
                    two = level_total(F, tot, l)
                    nc.vector.tensor_tensor(total_of(F, tot, l), two[:, :, 0], two[:, :, 1], ALU.mult).then_inc(s["tot_ready"], 1)

        def dve_merge(dve, g, j):
            if j == DIAG:
                dve.wait_ge(s["A_clear"], 1)
            else:
                dve.wait_ge(s["A_merged"], 8 * g + j)
            dve.wait_ge(s["gla_step"], gla_at(g, j))
            st.stand(dve)
            for out, c0, c1 in spans(3 * (j % 2)):
                n = c1 - c0
                cp = nc.vector.copy_predicated(A[:, c0 * P:c1 * P].rearrange("p (c t) -> p c t", t=P),
                                               C.mask[:, j, :].unsqueeze(1).broadcast_to([P, n, P]), out)
            cp.then_inc(s["A_merged"], 1)

        def dve_level(dve, g, j):
            b = 1 << (j - 1)
            dve.wait_ge(s["gla_step"], gla_at(g, j))
            dve.wait_ge(s["Q_ready"], NQ * g + 2 * j + 2 * NQ)
            for Q, F, tot, side in ((Q_f, f_f, tot_f, 1), (Q_b, f_b, tot_b, 0)):
                total = level_total(F, tot, j)
                half = pairs(Q[:], b)[:, :, side, :]
                nc.vector.tensor_tensor(half, half, over(total[:, :, 1 - side], b), ALU.mult).then_inc(s["Q_ready"], 1)

        def dve_states(dve, g):
            dve.wait_ge(s["gla_step"], gla_at(g, STATE))
            totf, totb = total_of(f_f, tot_f, LEVELS), total_of(f_b, tot_b, LEVELS)
            runs = [(n, c, c + 1, S_f, totf, c in firsts_f) for n, c in enumerate(state_f)]
            runs += [(n + len(state_f), c, c - 1, S_b, totb, c in firsts_b) for n, c in enumerate(state_b)]
            half = len(state_f)
            for i in range(half):
                for n, c, to, S, tot, first in (runs[i], runs[i + half]):
                    done = 2 * i + (S is S_b)
                    if not first:
                        dve.wait_ge(s["S_ready"], 16 * g + done - 1)
                    if first:
                        nc.vector.tensor_copy(S[:, to, :], Gc[:, n, :]).then_inc(s["S_ready"], 1)
                    else:
                        nc.vector.scalar_tensor_tensor(out=S[:, to, :], in0=S[:, c, :], scalar=tot[:, c:c + 1],
                                                       in1=Gc[:, n, :], op0=ALU.mult, op1=ALU.add).then_inc(s["S_ready"], 1)

        def dve_output(dve, g):
            dve.wait_ge(s["silu_ready"], g + 1 + CREDIT)
            nc.vector.tensor_scalar(y[:], so[:], C.onorm[:], None, ALU.mult).then_inc(s["so_used"], 1)
            dve.wait_ge(s["rt_ready"], g + 1 + CREDIT)
            nc.vector.reciprocal(rt[:], rt[:]).then_inc(s["y_ready"], 1)
            dve.wait_ge(s["y_ready"], NY * g + 1 + CREDIT)
            dve.wait_ge(s["so_used"], g + 1 + CREDIT)
            nc.vector.tensor_tensor(y[:], y[:], rt[:], ALU.mult).then_inc(s["y_ready"], 1)
            dve.wait_ge(s["y_ready"], NY * g + 2 + CREDIT)
            y3 = y[:].rearrange("p (c t) -> p c t", t=P)
            nc.vector.tensor_tensor(y3, Gc[:, 0:NT, :], y3, ALU.mult).then_inc(s["y_ready"], 1)

        def dve_round(dve, r, g):
            if g is not None:
                dve_start(dve, g)
                for j in range(LEVELS + 1):
                    if j:
                        dve_level(dve, g, j)
                    if j < LEVELS:
                        dve_copy(dve, g, j + 1)
                    dve_merge(dve, g, j)
                    if j == PARTS:
                        dve_output_gate(dve, g)
                dve_states(dve, g)
                dve_output(dve, g)
            if r is not None:
                dve_project(dve, r)

        with st.block() as block:

            @block.sync
            def _(sp):
                sp.sem_inc(s["y_stored"], 16 * CREDIT)
                W.sp_credit(sp)
                sp_round(sp, 0, None, first=True)
                sp_round(sp, 1, None)
                with sp.Fori(2, HEADS) as r:
                    sp_round(sp, r, r - 2)
                W.load(sp, HEADS, 0, next_tile)
                store(sp, HEADS - 2)
                store(sp, HEADS - 1)
                sp.wait_ge(s["y_stored"], 16 * (HEADS + CREDIT))

            @block.scalar
            def _(act):
                W.act_credit(act)
                act.sem_inc(s["rt_ready"], CREDIT)
                act_round(act, tiles_before, None)
                with act.Fori(0, HEADS - 1) as g:
                    act_round(act, tiles_with(g), g)
                act_round(act, tiles_last, HEADS - 1)

            @block.gpsimd
            def _(pool):
                W.pool_credit(pool)
                pool.sem_inc(s["K_ready"], 2 * LEVELS)
                nc.gpsimd.memset(A[:], 0.0).then_inc(s["A_clear"], 1)
                pool_round(pool, tiles_before, None)
                with pool.Fori(0, HEADS - 1) as g:
                    pool_round(pool, tiles_with(g), g)
                pool_round(pool, tiles_last, HEADS - 1)

            @block.tensor
            def _(pe):
                W.pe_credit(pe)
                pe.sem_inc(s["gla_step"], 2 * STEPS)
                pe.sem_inc(s["v_step"], CREDIT)
                pe_round(pe, tiles_before, None)
                with pe.Fori(0, HEADS - 1) as g:
                    pe_round(pe, tiles_with(g), g)
                pe_round(pe, tiles_last, HEADS - 1)

            @block.vector
            def _(dve):
                dve.sem_inc(s["Q_ready"], 2 * NQ)
                dve.sem_inc(s["y_ready"], CREDIT)
                dve.sem_inc(s["so_used"], CREDIT)
                dve.sem_inc(s["silu_ready"], CREDIT)
                dve_round(dve, 0, None)
                with dve.Fori(0, HEADS - 1) as g:
                    dve_round(dve, g + 1, g)
                dve_round(dve, None, HEADS - 1)


def chunks(ap):
    return ap.rearrange("p (c t) -> p c t", t=P)


def gmlp(nc, C, w_in, w_s, b_s, h_hi, h_lo, ya_dram, next_tile):
    PER, ROUNDS = 2, GROUPS // 2
    with Stage(nc, "gm") as st:
        W = WeightStream(st, PER, C.first_tile)
        v = st.sb("v", [P, GROUPS, T])
        act_out = [st.sb(f"act_out{t}", [P, T]) for t in range(PER)]
        vn = [st.sb(f"vn{t}", [P, T]) for t in range(PER)]
        ya = [st.sb(f"ya{t}", [P, T]) for t in range(PER)]
        sq = ya
        ws = [st.sb(f"ws{t}", [P, P]) for t in range(PER)]
        wsT = [st.sb(f"wsT{t}", [P, P]) for t in range(PER)]
        bias = [st.sb(f"bias{t}", [P, P]) for t in range(PER)]
        ssq = st.sb("ssq", [P, GROUPS, NT])
        var, std, rstd = (st.sb(n, [P, NT]) for n in ("var", "std", "rstd"))
        G = st.ps("G", [P, 6, 4, P])
        Gc = G[:].rearrange("p b c t -> p (b c) t")
        s = {n: st.sem(n) for n in ("v_turned", "v_copied", "v_squared", "v_summed", "var_ready", "std_ready",
                                    "rstd_ready", "vn_ready", "ws_turned", "wsT_ready", "mixed", "mix_scaled",
                                    "ya_ready")}
        ws_loaded = [st.sem(f"ws_loaded{t}") for t in range(PER)]
        bias_loaded = [st.sem(f"bias_loaded{t}") for t in range(PER)]
        ya_stored = [st.sem(f"ya_stored{t}") for t in range(PER)]

        def bank_set(t):
            return Gc[:, 12 * t:12 * t + NT, :], Gc[:, 12 * t + NT, :]

        def pe_turn_v(pe, r, t):
            n = PER * r + t
            W.moved(pe, r, t)
            pe.wait_ge(s["v_copied"], n - 1 + CREDIT)
            out, _ = bank_set(t)
            for c in range(NT):
                mm = nc.tensor.transpose(out[:, c, :], act_out[t][:, c * P:(c + 1) * P], C.ident[:])
            mm.then_inc(s["v_turned"], 1)

        def pe_v_round(pe, r, first):
            for t in range(PER):
                for part in range(PARTS):
                    W.multiply(nc, pe, r, t, part, h_hi, h_lo)
                    if part == 1 and not (first and t == 0):
                        pe_turn_v(pe, *((r, 0) if t == 1 else (r - 1, 1)))

        def act_move(act, r, t):
            for part in range(PARTS):
                out, free = W.result(act, r, t, part)
                nc.scalar.activation(act_out[t][:, part * PART:(part + 1) * PART], out,
                                     ACT.Gelu_apprx_tanh).then_inc(free, 1)

        def act_v_round(act, r):
            for t in range(PER):
                W.split_hi(nc, act, r + t, (t + 1) % PER)
                act.wait_ge(s["v_turned"], PER * r + t - 1 + CREDIT)
                act_move(act, r, t)

        def dve_v_round(dve, r):
            for t in range(PER):
                n = PER * r + t
                dve.wait_ge(s["v_turned"], n + 1 + CREDIT)
                out, _ = bank_set(t)
                nc.vector.tensor_copy(chunks(v[:, bass.ds(n, 1), :].rearrange("p a t -> p (a t)")), out).then_inc(s["v_copied"], 1)
                dve.wait_ge(s["v_squared"], n + 1)
                nc.vector.tensor_reduce(ssq[:, bass.ds(n, 1), :].rearrange("p a c -> p (a c)"), chunks(sq[t][:]),
                                        AX.X, ALU.add).then_inc(s["v_summed"], 1)

        def pool_v_round(pool, r):
            for t in range(PER):
                n = PER * r + t
                pool_split(pool, r + t, (t + 1) % PER)
                pool.wait_ge(s["v_copied"], n + 1 + CREDIT)
                pool.wait_ge(s["v_summed"], n - 1 + CREDIT)
                src = v[:, bass.ds(n, 1), :].rearrange("p a t -> p (a t)")
                nc.gpsimd.tensor_tensor(sq[t][:], src, src, ALU.mult).then_inc(s["v_squared"], 1)

        def pool_split(pool, r, t):
            W.split_lo(nc, pool, r, t)

        def sp_u_round(sp, i):
            for t in range(PER):
                n = PER * i + t
                W.load(sp, ROUNDS + i, t, cols(w_in, COL_U + n * P))
                sp.wait_ge(s["ws_turned"], n - 1 + CREDIT)
                st.stand(sp)
                sp.dma_start(ws[t][:], w_s[bass.ds(n, 1)].rearrange("g t s -> (g t) s")).then_inc(ws_loaded[t], 16)
                sp.wait_ge(s["mix_scaled"], n - 1 + CREDIT)
                st.stand(sp)
                sp.dma_start(bias[t][:], b_s[bass.ds(n, 1), :].broadcast_to([P, P])).then_inc(bias_loaded[t], 16)

        def sp_store(sp, i):
            for t in range(PER):
                n = PER * i + t
                sp.wait_ge(s["ya_ready"], n + 1 + CREDIT)
                st.stand(sp)
                sp.dma_start(ya_dram[bass.ds(n * P, P), :], ya[t][:]).then_inc(ya_stored[t], 16)

        def pe_u_round(pe, i):
            for t in range(PER):
                n = PER * i + t
                out, turned = bank_set(t)
                for part in range(PARTS):
                    W.multiply(nc, pe, ROUNDS + i, t, part, h_hi, h_lo)
                    if part == 0:
                        pe.wait_ge(ws_loaded[t], 16 * (i + 1))
                        pe.wait_ge(s["wsT_ready"], n - 1 + CREDIT)
                        nc.tensor.transpose(turned, ws[t][:], C.ident[:]).then_inc(s["ws_turned"], 1)
                    if part == 2:
                        pe.wait_ge(s["wsT_ready"], n + 1 + CREDIT)
                        pe.wait_ge(s["vn_ready"], n + 1)
                        pe.wait_ge(s["mix_scaled"], n - 1 + CREDIT)
                        for c in range(NT):
                            mm = nc.tensor.matmul(out[:, c, :], vn[t][:, c * P:(c + 1) * P], wsT[t][:], start=True, stop=True)
                        mm.then_inc(s["mixed"], 1)

        def act_u_round(act, i):
            for t in range(PER):
                n = PER * i + t
                W.split_hi(nc, act, ROUNDS + i + t, (t + 1) % PER)
                _, turned = bank_set(t)
                act.wait_ge(s["ws_turned"], n + 1 + CREDIT)
                act.wait_ge(s["mixed"], n - 1 + CREDIT)
                nc.scalar.activation(wsT[t][:], turned, ACT.Copy).then_inc(s["wsT_ready"], 1)
                act.wait_ge(s["ya_ready"], n - 1 + CREDIT)
                act_move(act, ROUNDS + i, t)

        def dve_u_round(dve, i):
            for t in range(PER):
                n = PER * i + t
                out, _ = bank_set(t)
                dve.wait_ge(s["mixed"], n - 1 + CREDIT)
                vg = chunks(v[:, bass.ds(n, 1), :].rearrange("p a t -> p (a t)"))
                nc.vector.tensor_tensor(chunks(vn[t][:]), vg, over(rstd[:], P), ALU.mult).then_inc(s["vn_ready"], 1)
                dve.wait_ge(s["mixed"], n + 1 + CREDIT)
                dve.wait_ge(bias_loaded[t], 16 * (i + 1))
                dve.wait_ge(ya_stored[t], 16 * (i + CREDIT))
                nc.vector.scalar_tensor_tensor(out=chunks(ya[t][:]), in0=out, scalar=C.vnorm[:, bass.ds(n, 1)],
                                               in1=bias[t][:].unsqueeze(1).broadcast_to([P, NT, P]),
                                               op0=ALU.mult, op1=ALU.add).then_inc(s["mix_scaled"], 1)
                W.moved(dve, ROUNDS + i, t)
                dve.wait_ge(s["mix_scaled"], n + 1 + CREDIT)
                nc.vector.tensor_tensor(ya[t][:], ya[t][:], act_out[t][:], ALU.mult).then_inc(s["ya_ready"], 1)

        with st.block() as block:

            @block.sync
            def _(sp):
                for t in range(PER):
                    sp.sem_inc(ya_stored[t], 16 * CREDIT)
                W.sp_credit(sp)
                W.load(sp, 0, 1, cols(w_in, COL_V + P))
                with sp.Fori(1, ROUNDS) as r:
                    for t in range(PER):
                        W.load(sp, r, t, cols(w_in, COL_V + (PER * r + t) * P))
                sp_u_round(sp, 0)
                with sp.Fori(1, ROUNDS) as i:
                    sp_u_round(sp, i)
                    sp_store(sp, i - 1)
                W.load(sp, 2 * ROUNDS, 0, next_tile)
                sp_store(sp, ROUNDS - 1)
                for t in range(PER):
                    sp.wait_ge(ya_stored[t], 16 * (ROUNDS + CREDIT))

            @block.scalar
            def _(act):
                W.act_credit(act)
                act.sem_inc(s["wsT_ready"], CREDIT)
                with act.Fori(0, ROUNDS) as r:
                    act_v_round(act, r)
                act.wait_ge(s["var_ready"], 1)
                nc.scalar.activation(std[:], var[:], ACT.Sqrt).then_inc(s["std_ready"], 1)
                with act.Fori(0, ROUNDS) as i:
                    act_u_round(act, i)

            @block.gpsimd
            def _(pool):
                W.pool_credit(pool)
                with pool.Fori(0, ROUNDS) as r:
                    pool_v_round(pool, r)
                with pool.Fori(0, ROUNDS) as i:
                    for t in range(PER):
                        pool_split(pool, ROUNDS + i + t, (t + 1) % PER)

            @block.tensor
            def _(pe):
                W.pe_credit(pe)
                for n in ("v_turned", "ws_turned", "mixed"):
                    pe.sem_inc(s[n], CREDIT)
                pe_v_round(pe, 0, True)
                with pe.Fori(1, ROUNDS) as r:
                    pe_v_round(pe, r, False)
                pe_turn_v(pe, ROUNDS - 1, 1)
                with pe.Fori(0, ROUNDS) as i:
                    pe_u_round(pe, i)

            @block.vector
            def _(dve):
                for n in ("v_copied", "v_summed", "mix_scaled", "ya_ready"):
                    dve.sem_inc(s[n], CREDIT)
                with dve.Fori(0, ROUNDS) as r:
                    dve_v_round(dve, r)
                dve.wait_ge(s["v_summed"], GROUPS + CREDIT)
                nc.vector.tensor_reduce(var[:], ssq[:].rearrange("p g c -> p c g"), AX.X, ALU.add).then_inc(s["rstd_ready"], 1)
                dve.wait_ge(s["rstd_ready"], 1)
                nc.vector.tensor_scalar(var[:], var[:], 1.0 / D, EPS, ALU.mult, ALU.add).then_inc(s["var_ready"], 1)
                dve.wait_ge(s["std_ready"], 1)
                nc.vector.reciprocal(rstd[:], std[:]).then_inc(s["rstd_ready"], 1)
                dve.wait_ge(s["rstd_ready"], 2)
                with dve.Fori(0, ROUNDS) as i:
                    dve_u_round(dve, i)


class RowSplit:

    def __init__(self, st, src, ring, parts, hi, lo):
        self.src, self.ring, self.hi, self.lo = src, ring, hi, lo
        n = T // parts
        self.pieces = [(k, slice(i * n, (i + 1) * n)) for i in range(parts) for k in range(KC)]
        self.loaded = [st.sem(f"row_loaded{b}") for b in range(len(ring))]
        self.hi_ready, self.lo_even, self.lo_odd = (st.sem(n) for n in ("row_hi_ready", "row_lo_even", "row_lo_odd"))

    def load(self, sp):
        for i, (k, c) in enumerate(self.pieces):
            old = i - len(self.ring)
            if old >= 0:
                sp.wait_ge(self.hi_ready, old + 1)
                sp.wait_ge((self.lo_even, self.lo_odd)[old % 2], old // 2 + 1)
            b = i % len(self.ring)
            sp.dma_start(self.ring[b], self.src[k * P:(k + 1) * P, c]).then_inc(self.loaded[b], 16)

    def split_hi(self, nc, act, i):
        k, c = self.pieces[i]
        b = i % len(self.ring)
        act.wait_ge(self.loaded[b], 16 * (i // len(self.ring) + 1))
        nc.scalar.activation(self.hi[:, k, c], self.ring[b], ACT.Copy).then_inc(self.hi_ready, 1)

    def split_lo(self, eng, ops, parity, done, start=0, stop=None):
        for i, (k, c) in enumerate(self.pieces):
            if i % 2 == parity and start <= i < (stop or len(self.pieces)):
                eng.wait_ge(self.hi_ready, i + 1)
                ops.tensor_tensor(self.lo[:, k, c], self.ring[i % len(self.ring)], self.hi[:, k, c].bitcast(F32),
                                  ALU.subtract).then_inc(done, 1)

    def ready(self, eng, n=None):
        n = n or len(self.pieces)
        eng.wait_ge(self.lo_even, (n + 1) // 2)
        if n > 1:
            eng.wait_ge(self.lo_odd, n // 2)


def merge(nc, C, name, w_in, col_gate, w_branch, y_dram, m_in, m_out, h_hi, h_lo, next_tile):
    PER = 2
    GATE, BRANCH = 0, 1
    with Stage(nc, name) as st:
        W = WeightStream(st, PER, C.first_tile)
        y_hi = st.sb("y_hi", [P, KC, T], F32R)
        y_lo = st.sb("y_lo", [P, KC, T], F32R)
        sg, m, m_prev = (st.sb(n, [P, T]) for n in ("sg", "m", "m_prev"))
        s = {n: st.sem(n) for n in ("added", "m_stored", "m_prev_loaded")}
        rows = RowSplit(st, y_dram, [a[:, i * T // 2:(i + 1) * T // 2] for a in (m, m_prev) for i in range(2)], 2, y_hi, y_lo)
        adds = m_in is not None

        def sp_round(sp, r):
            W.load(sp, r, GATE, cols(w_in, col_gate + r * P))
            W.load(sp, r, BRANCH, cols(w_branch, r * P))

        def sp_tail(sp, r):
            if adds:
                sp.wait_ge(s["added"], PARTS * (r + 1) + PARTS * CREDIT)
            else:
                W.moved(sp, r, BRANCH)
            sp.dma_start(m_out[bass.ds(r * P, P), :], m[:]).then_inc(s["m_stored"], 16)

        def sp_prev(sp, r):
            if adds:
                sp.wait_ge(s["added"], PARTS * (r + CREDIT))
                st.stand(sp)
                sp.dma_start(m_prev[:], m_in[bass.ds(r * P, P), :]).then_inc(s["m_prev_loaded"], 16)

        def act_gate(act, r, part):
            out, free = W.result(act, r, GATE, part)
            nc.scalar.activation(sg[:, part * PART:(part + 1) * PART], out, ACT.Sigmoid).then_inc(free, 1)

        def act_round(act, r, last):
            W.split_hi(nc, act, r, BRANCH)
            W.moved(act, r - 1, BRANCH)
            for part in range(PARTS):
                act_gate(act, r, part)
            if not last:
                W.split_hi(nc, act, r + 1, GATE)

        def dve_round(dve, r):
            W.moved(dve, r, GATE)
            dve.wait_ge(s["m_stored"], 16 * (r + CREDIT))
            if adds:
                dve.wait_ge(s["m_prev_loaded"], 16 * (r + 1))
            for part in range(PARTS):
                c = slice(part * PART, (part + 1) * PART)
                out, free = W.result(dve, r, BRANCH, part)
                nc.vector.tensor_tensor(m[:, c], out, sg[:, c], ALU.mult).then_inc(free, 1)
                if adds:
                    W_done = PARTS // 2 * (PER * r + BRANCH) + part // 2 + 1 + CREDIT
                    dve.wait_ge(W.bank_free[(PARTS * BRANCH + part) % 2], W_done)
                    nc.vector.tensor_tensor(m[:, c], m[:, c], m_prev[:, c], ALU.add).then_inc(s["added"], 1)

        with st.block() as block:

            @block.sync
            def _(sp):
                sp.sem_inc(s["m_stored"], 16 * CREDIT)
                W.sp_credit(sp)
                W.load(sp, 0, BRANCH, cols(w_branch, 0))
                rows.load(sp)
                rows.ready(sp)
                sp_prev(sp, 0)
                with sp.Fori(1, KC) as r:
                    sp_round(sp, r)
                    sp_tail(sp, r - 1)
                    sp_prev(sp, r)
                if next_tile is not None:
                    W.load(sp, KC, GATE, next_tile)
                sp_tail(sp, KC - 1)
                sp.wait_ge(s["m_stored"], 16 * (KC + CREDIT))

            @block.scalar
            def _(act):
                W.act_credit(act)
                gate_after = {len(rows.pieces) * (part + 1) // PARTS - 2: part for part in range(PARTS)}
                for i in range(len(rows.pieces)):
                    rows.split_hi(nc, act, i)
                    if i == 1:
                        W.split_hi(nc, act, 0, BRANCH)
                    if i in gate_after:
                        act_gate(act, 0, gate_after[i])
                W.split_hi(nc, act, 1, GATE)
                with act.Fori(1, KC - 1) as r:
                    act_round(act, r, False)
                act_round(act, KC - 1, next_tile is None)

            @block.gpsimd
            def _(pool):
                W.pool_credit(pool)
                rows.split_lo(pool, nc.gpsimd, 0, rows.lo_even, 0, KC)
                W.split_lo(nc, pool, 0, BRANCH)
                rows.split_lo(pool, nc.gpsimd, 0, rows.lo_even, KC)
                with pool.Fori(1, KC) as r:
                    W.split_lo(nc, pool, r, GATE)
                    W.split_lo(nc, pool, r, BRANCH)
                if next_tile is not None:
                    W.split_lo(nc, pool, KC, GATE)

            @block.tensor
            def _(pe):
                W.pe_credit(pe)

                def pe_round(r, first):
                    for part in range(PARTS):
                        W.multiply(nc, pe, r, GATE, part, h_hi, h_lo)
                    for part in range(PARTS):
                        if first:
                            rows.ready(pe, KC * (1 + 2 * part // PARTS))
                        W.multiply(nc, pe, r, BRANCH, part, y_hi, y_lo)

                pe_round(0, True)
                with pe.Fori(1, KC) as r:
                    pe_round(r, False)

            @block.vector
            def _(dve):
                dve.sem_inc(s["added"], PARTS * CREDIT)
                rows.split_lo(dve, nc.vector, 1, rows.lo_odd)
                rows.ready(dve)
                with dve.Fori(0, KC) as r:
                    dve_round(dve, r)


def residual(nc, C, x_prompt, x_sample, w_out, m_dram, x2):
    PER, ROUNDS = 2, KC // 2
    with Stage(nc, "wo") as st:
        W = WeightStream(st, PER)
        m_hi = st.sb("m_hi", [P, KC, T], F32R)
        m_lo = st.sb("m_lo", [P, KC, T], F32R)
        o = [st.sb(f"o{t}", [P, T]) for t in range(PER)]
        G = st.ps("G", [P, 6, 4, P])
        Gc = G[:].rearrange("p b c t -> p (b c) t")
        s = {n: st.sem(n) for n in ("turned", "added", "x_loaded")}
        m = [st.sb(f"m{k}", [P, T]) for k in range(KC)]
        rows = RowSplit(st, m_dram, [a[:] for a in m], 1, m_hi, m_lo)

        def pe_turn(pe, r, t):
            W.moved(pe, r, t)
            pe.wait_ge(s["added"], PER * r + t - 1 + CREDIT)
            for c in range(NT):
                mm = nc.tensor.transpose(Gc[:, 12 * t + c, :], o[t][:, c * P:(c + 1) * P], C.ident[:])
            mm.then_inc(s["turned"], 1)

        def pe_round(pe, r, first):
            for t in range(PER):
                for part in range(PARTS):
                    W.multiply(nc, pe, r, t, part, m_hi, m_lo, rows if first and t == 0 and part == 0 else None)
                    if part == 1 and not (first and t == 0):
                        pe_turn(pe, *((r, 0) if t == 1 else (r - 1, 1)))

        def act_round(act, r, last):
            for t in range(PER):
                if not (last and t == PER - 1):
                    W.split_hi(nc, act, r + t, (t + 1) % PER)
                act.wait_ge(s["turned"], PER * r + t - 1 + CREDIT)
                for part in range(PARTS):
                    out, free = W.result(act, r, t, part)
                    nc.scalar.activation(o[t][:, part * PART:(part + 1) * PART], out, ACT.Copy).then_inc(free, 1)

        with st.block() as block:

            @block.sync
            def _(sp):
                for t in range(PER):
                    W.load(sp, 0, t, cols(w_out, t * P))
                rows.load(sp)
                sp.dma_start(x2[:, 0:NT_PROMPT, :], x_prompt.rearrange("b (t p) d -> p (b t) d", p=P)).then_inc(s["x_loaded"], 16)
                sp.dma_start(x2[:, NT_PROMPT:NT, :], x_sample.rearrange("b (t p) d -> p (b t) d", p=P)).then_inc(s["x_loaded"], 16)
                with sp.Fori(1, ROUNDS) as r:
                    for t in range(PER):
                        W.load(sp, r, t, cols(w_out, (PER * r + t) * P))

            @block.scalar
            def _(act):
                W.act_credit(act)
                W.split_hi(nc, act, 0, 0)
                for k in range(KC):
                    rows.split_hi(nc, act, k)
                with act.Fori(0, ROUNDS - 1) as r:
                    act_round(act, r, False)
                act_round(act, ROUNDS - 1, True)

            @block.gpsimd
            def _(pool):
                W.pool_credit(pool)
                W.split_lo(nc, pool, 0, 0)
                rows.split_lo(pool, nc.gpsimd, 0, rows.lo_even)
                W.split_lo(nc, pool, 0, 1)
                with pool.Fori(1, ROUNDS) as r:
                    for t in range(PER):
                        W.split_lo(nc, pool, r, t)

            @block.tensor
            def _(pe):
                W.pe_credit(pe)
                pe.sem_inc(s["turned"], CREDIT)
                pe_round(pe, 0, True)
                with pe.Fori(1, ROUNDS) as r:
                    pe_round(pe, r, False)
                pe_turn(pe, ROUNDS - 1, 1)

            @block.vector
            def _(dve):
                dve.sem_inc(s["added"], CREDIT)
                rows.split_lo(dve, nc.vector, 1, rows.lo_odd)
                dve.wait_ge(s["x_loaded"], 32)
                with dve.Fori(0, ROUNDS) as r:
                    for t in range(PER):
                        n = PER * r + t
                        dve.wait_ge(s["turned"], n + 1 + CREDIT)
                        x = x2[:, :, bass.ds(n * P, P)]
                        nc.vector.tensor_tensor(x, Gc[:, 12 * t:12 * t + NT, :], x, ALU.add).then_inc(s["added"], 1)


def route(nc, C, norm2_g, w_router, x2, x3, h2, aff_p, aff_s):
    PAIRS = NT // 2
    with Stage(nc, "rt") as st:
        gain, junk = st.sb("gain", [P, D]), st.sb("junk", [P, D])
        wr = st.sb("wr", [P, KC, NE])
        h = st.sb("h", [P, NT, D])
        hT = st.sb("hT", [P, 2, KC, 2 * P])
        router = st.sb("router", [NE, T])
        ssq, var, std, rstd, top, total, inv = (st.sb(n, [P, NT]) for n in ("ssq", "var", "std", "rstd", "top", "total", "inv"))
        shifted, expo = (st.sb(n, [P, NT, NE]) for n in ("shifted", "expo"))
        prob_p, prob_s = st.sb("prob_p", [P, NT_PROMPT, NE]), st.sb("prob_s", [P, HALF_S // P, 2, NE])
        turned = st.ps("turned", [P, 2, KC, P])
        pair_out = st.ps("pair_out", [P, 4, 512])
        banks = turned[:].rearrange("p a k t -> p (a k t)")
        logits = banks[:, 0:NT * NE].rearrange("p (t e) -> p t e", e=NE)
        affT_p, affT_s = banks[:, 512:1024], banks[:, 1024:1536]
        s = {n: st.sem(n) for n in ("loaded", "x3_stored", "ssq_ready", "var_ready", "std_ready", "rstd_ready",
                                    "h_ready", "h_turned", "hT_ready", "pair_done", "pair_copied", "logits_ready", "top_ready", "shifted_ready",
                                    "exp_ready", "total_ready", "inv_ready", "prob_ready", "aff_turned", "h_stored")}

        def wide(x):
            return x[:].unsqueeze(2).broadcast_to([P, NT, NE])

        with st.block() as block:

            @block.sync
            def _(sp):
                sp.dma_start(gain[:], norm2_g.broadcast_to([P, D])).then_inc(s["loaded"], 16)
                sp.dma_start(wr[:], w_router.rearrange("(k p) e -> p k e", p=P)).then_inc(s["loaded"], 16)
                for dst, a, z in ((x3[0], 0, NT_PROMPT), (x3[1], NT_PROMPT, NT)):
                    sp.dma_start(dst.rearrange("(t p) d -> p t d", p=P), x2[:, a:z, :]).then_inc(s["x3_stored"], 16)
                h2_rows = [x.rearrange("(t p) d -> p t d", p=P) for x in h2]
                for j in range(PAIRS):
                    sp.wait_ge(s["h_ready"], 2 * j + 2)
                    dst = h2_rows[0] if j == 0 else h2_rows[1][:, 2 * j - 2:2 * j, :]
                    sp.dma_start(dst, h[:, 2 * j:2 * j + 2, :]).then_inc(s["h_stored"], 16)
                sp.wait_ge(s["x3_stored"], 32)
                sp.wait_ge(s["h_stored"], 16 * PAIRS)

            @block.scalar
            def _(act):
                def square(t):
                    if t:
                        act.wait_ge(s["ssq_ready"], t)
                    nc.scalar.activation(junk[:], x2[:, t, :], ACT.Square, accum_out=ssq[:, t:t + 1]).then_inc(s["ssq_ready"], 1)

                def root(t):
                    act.wait_ge(s["var_ready"], t + 1)
                    nc.scalar.activation(std[:, t:t + 1], var[:, t:t + 1], ACT.Sqrt).then_inc(s["std_ready"], 1)

                square(0)
                square(1)
                root(0)
                for t in range(NT):
                    if t + 2 < NT:
                        square(t + 2)
                    if t + 1 < NT:
                        root(t + 1)
                    act.wait_ge(s["h_turned"], t + 1)
                    if t >= 4:
                        act.wait_ge(s["pair_done"], t // 2 - 1)
                    nc.scalar.activation(hT[:, t // 2 % 2, :, t % 2 * P:(t % 2 + 1) * P], turned[:, t % 2],
                                         ACT.Copy).then_inc(s["hT_ready"], 1)
                act.wait_ge(s["shifted_ready"], 1)
                nc.scalar.activation(expo[:], shifted[:], ACT.Exp).then_inc(s["exp_ready"], 1)

            @block.tensor
            def _(pe):
                def route_pair(j):
                    pe.wait_ge(s["hT_ready"], 2 * j + 2)
                    if j >= 4:
                        pe.wait_ge(s["pair_copied"], j - 3)
                    for k in range(KC):
                        mm = nc.tensor.matmul(pair_out[0:NE, j % 4, 0:2 * P], wr[:, k, :], hT[:, j % 2, k, :],
                                              start=(k == 0), stop=(k == KC - 1))
                    mm.then_inc(s["pair_done"], 1)

                for t in range(NT):
                    pe.wait_ge(s["h_ready"], t + 1)
                    if t >= 2:
                        pe.wait_ge(s["hT_ready"], t - 1)
                    for k in range(KC):
                        mm = nc.tensor.transpose(turned[:, t % 2, k, :], h[:, t, k * P:(k + 1) * P], C.ident[:])
                    mm.then_inc(s["h_turned"], 1)
                    if t and t % 2 == 0:
                        route_pair(t // 2 - 1)
                route_pair(PAIRS - 1)
                pe.wait_ge(s["pair_copied"], PAIRS)
                for t in range(NT):
                    mm = nc.tensor.transpose(logits[:, t, :], router[:, t * P:(t + 1) * P], C.ident[0:NE, 0:NE])
                mm.then_inc(s["logits_ready"], 1)
                pe.wait_ge(s["prob_ready"], 2)
                for t in range(NT_PROMPT):
                    nc.tensor.transpose(affT_p[0:NE, t * P:(t + 1) * P], prob_p[:, t, :], C.ident[:])
                for t in range(HALF_S // P):
                    mm = nc.tensor.transpose(affT_s[0:2 * NE, t * P:(t + 1) * P],
                                             prob_s[:, t].rearrange("p h e -> p (h e)"), C.ident[:])
                mm.then_inc(s["aff_turned"], 1)

            @block.vector
            def _(dve):
                def variance(t):
                    dve.wait_ge(s["ssq_ready"], t + 1)
                    nc.vector.tensor_scalar(var[:, t:t + 1], ssq[:, t:t + 1], 1.0 / D, EPS, ALU.mult, ALU.add).then_inc(s["var_ready"], 1)

                variance(0)
                dve.wait_ge(s["loaded"], 32)
                for t in range(NT):
                    c = slice(t, t + 1)
                    if t + 1 < NT:
                        variance(t + 1)
                    dve.wait_ge(s["std_ready"], t + 1)
                    nc.vector.reciprocal(rstd[:, c], std[:, c]).then_inc(s["rstd_ready"], 1)
                    dve.wait_ge(s["rstd_ready"], t + 1)
                    nc.vector.scalar_tensor_tensor(out=h[:, t, :], in0=x2[:, t, :], scalar=rstd[:, c], in1=gain[:],
                                                   op0=ALU.mult, op1=ALU.mult).then_inc(s["h_ready"], 1)
                for j in range(PAIRS):
                    dve.wait_ge(s["pair_done"], j + 1)
                    nc.vector.tensor_copy(router[:, 2 * j * P:2 * (j + 1) * P], pair_out[0:NE, j % 4, 0:2 * P]).then_inc(s["pair_copied"], 1)
                dve.wait_ge(s["logits_ready"], 1)
                nc.vector.tensor_reduce(top[:], logits, AX.X, ALU.max).then_inc(s["top_ready"], 1)
                dve.wait_ge(s["top_ready"], 1)
                nc.vector.tensor_tensor(shifted[:], logits, wide(top), ALU.subtract).then_inc(s["shifted_ready"], 1)
                dve.wait_ge(s["exp_ready"], 1)
                nc.vector.tensor_reduce(total[:], expo[:], AX.X, ALU.add).then_inc(s["total_ready"], 1)
                dve.wait_ge(s["total_ready"], 1)
                nc.vector.reciprocal(inv[:], total[:]).then_inc(s["inv_ready"], 1)
                dve.wait_ge(s["inv_ready"], 1)
                nc.vector.tensor_tensor(prob_p[:], expo[:, 0:NT_PROMPT, :], wide(inv)[:, 0:NT_PROMPT, :],
                                        ALU.mult).then_inc(s["prob_ready"], 1)
                halves = "p (h t) e -> p h t e"
                nc.vector.tensor_tensor(prob_s[:].rearrange("p t h e -> p h t e"),
                                        expo[:, NT_PROMPT:, :].rearrange(halves, h=2),
                                        inv[:, NT_PROMPT:].rearrange("p (h t) -> p h t", h=2).unsqueeze(3).broadcast_to([P, 2, HALF_S // P, NE]),
                                        ALU.mult).then_inc(s["prob_ready"], 1)
                dve.wait_ge(s["aff_turned"], 1)
                nc.vector.tensor_copy(aff_p[:], affT_p[0:NE, 0:T_PROMPT])
                nc.vector.tensor_copy(aff_s[:], affT_s[0:2 * NE, 0:HALF_S])


def experts(nc, C, aff_p, aff_s, h2, x3, w_g, w_u, w_d):
    WAVES_S, WAVES_P = CAP_S // 8, CAP_P // 8
    TILES = 3 * KC
    FIRST_DOWN = 2 * KC
    WIDTH = 2 * P
    PIECES = 3 * D // WIDTH
    RAW = PIECES // 2
    FIRST_DOWN_PIECE = 2 * D // WIDTH
    RING, BANKS = 12, 3
    AHEAD = 10
    DVE_AHEAD = 6
    BANKX = 3
    CR = TILES
    TURN_X = FIRST_DOWN + 2
    ADD, GATHER = 1, 3

    def piece_of(t):
        if t < FIRST_DOWN:
            j, which = t // 2, t % 2
            return 2 * (j // 2) + which, (j % 2) * P
        j = t - FIRST_DOWN
        return FIRST_DOWN_PIECE + j // 2, (j % 2) * P

    def lo_done(e, t):
        return s["w_lo_pool"] if t % 2 else s["w_lo_dve"], TILES // 2 * e + t // 2 + 1

    with Stage(nc, "ex") as st:
        val_s, val_p = st.sb("val_s", [2 * NE, CAP_S]), st.sb("val_p", [NE, CAP_P])
        idx_s, idx_p = st.sb("idx_s", [2 * NE, CAP_S], U32), st.sb("idx_p", [NE, CAP_P], U32)
        idxf_s, idxf_p = st.sb("idxf_s", [2 * NE, CAP_S]), st.sb("idxf_p", [NE, CAP_P])
        first, second = st.sb("first", [P, 2, NE]), st.sb("second", [P, 2, NE])
        flip_part, flip = st.sb("flip_part", [P, P]), st.sb("flip", [P, P])
        wins, wins_mask, best = st.sb("wins", [P, NE]), st.sb("wins_mask", [P, NE], U8), st.sb("best", [P, NE])
        gate_s, gate_p = st.sb("gate_s", [P, NE]), st.sb("gate_p", [CAP_P, NE])
        col_s, col_p = st.sb("col_s", [P, NE], U32), st.sb("col_p", [CAP_P, NE], U32)
        cur_s, cur_p = st.sb("cur_s", [P, 1], U32), st.sb("cur_p", [CAP_P, 1], U32)
        out_s, out_p = st.sb("out_s", [P, 1], U32), st.sb("out_p", [CAP_P, 1], U32)
        raw = [st.sb(f"raw{p}", [P, KC, WIDTH]) for p in range(RAW)]
        w_hi = [st.sb(f"w_hi{i}", [P, KC, P], F32R) for i in range(RING)]
        w_lo = [st.sb(f"w_lo{i}", [P, KC, P], F32R) for i in range(RING)]
        x_s, x_p = st.sb("x_s", [P, D]), st.sb("x_p", [CAP_P, D])
        xT = st.sb("xT", [P, KC, 2 * SLOTS], F32R)
        hT = st.sb("hT", [P, KC, 2 * SLOTS], F32R)
        gs, sig, us = (st.sb(n, [P, 2, SLOTS]) for n in ("gs", "sig", "us"))
        yT = st.sb("yT", [P, 2, SLOTS])
        y_s, y_p = st.sb("y_s", [P, D]), st.sb("y_p", [CAP_P, D])
        out = [st.ps(f"out{i}", [P, 512]) for i in range(BANKS)]
        X = st.ps("X", [P, 3, 512])
        Y = [st.ps(f"Y{b}", [P, 4, P]) for b in range(2)]
        s = {n: st.sem(n) for n in (
            "flip_half", "flip_ready", "merge_step", "flipped", "max_found", "index_found", "replaced", "listed", "turned", "columns_ready", "cur_ready", "gathered_s",
            "gathered_p", "x_turned", "xT_hi", "xT_lo", "w_hi_ready", "w_lo_dve", "w_lo_pool", "tile_done",
            "summed", "sig_ready", "u_gated", "h_made", "h_hi_ready", "h_ready", "y_turned", "y_moved", "out_ready",
            "added_s", "added_p")}
        loaded = [st.sem(f"loaded{p}") for p in range(RAW)]

        def sp_load(sp, e, p):
            w = (w_g, w_u)[p % 2] if p < FIRST_DOWN_PIECE else w_d
            c = (p // 2 if p < FIRST_DOWN_PIECE else p - FIRST_DOWN_PIECE) * WIDTH
            src = w[bass.ds(e, 1), :, c:c + WIDTH].rearrange("a (k p) n -> p (a k) n", p=P)
            sp.dma_start(raw[p % RAW][:], src).then_inc(loaded[p % RAW], 16)

        def sp_reload(sp, e, p):
            old_e, old_p = (e, p - RAW) if p >= RAW else (e - 1, p + RAW)
            tiles = [t for t in range(TILES) if piece_of(t)[0] == old_p]
            for parity in {t % 2 for t in tiles}:
                sp.wait_ge(*lo_done(old_e, max(t for t in tiles if t % 2 == parity)))
                st.stand(sp)
            sp_load(sp, e, p)

        def split_hi(act, e, t):
            p, c = piece_of(t)
            act.wait_ge(loaded[p % RAW], 16 * (2 * e + p // RAW + 1))
            act.wait_ge(s["tile_done"], TILES * e + t - RING + 1 + CR)
            nc.scalar.activation(w_hi[t % RING][:], raw[p % RAW][:, :, c:c + P], ACT.Copy).then_inc(s["w_hi_ready"], 1)

        def split_lo(eng, ops, e, t):
            p, c = piece_of(t)
            eng.wait_ge(s["w_hi_ready"], TILES * e + t + 1)
            ops.tensor_tensor(w_lo[t % RING][:], raw[p % RAW][:, :, c:c + P], w_hi[t % RING][:].bitcast(F32),
                              ALU.subtract).then_inc(lo_done(e, t)[0], 1)

        def x_chunks(b):
            ks = slice(BANKX * b, min(BANKX * b + BANKX, KC))
            return ks, X[:, b, 0:(ks.stop - ks.start) * SLOTS].rearrange("p (k c) -> p k c", c=SLOTS)

        def act_x(act, e):
            act.wait_ge(s["x_turned"], e + 1)
            for b in range(3):
                ks, src = x_chunks(b)
                nc.scalar.activation(xT[:, ks, 0:SLOTS], src, ACT.Copy).then_inc(s["xT_hi"], 1)

        def dve_x(dve, e):
            for b in range(3):
                ks, src = x_chunks(b)
                dve.wait_ge(s["xT_hi"], 3 * e + b + 1)
                nc.vector.tensor_tensor(xT[:, ks, SLOTS:], src, xT[:, ks, 0:SLOTS].bitcast(F32),
                                        ALU.subtract).then_inc(s["xT_lo"], 1)

        def act_sigmoid(act, e, j):
            act.wait_ge(s["summed"], TILES * e + 2 * j + 1 + CR)
            act.wait_ge(s["h_made"], KC * e + j - 1 + CR)
            nc.scalar.activation(sig[:, j % 2, :], gs[:, j % 2, :], ACT.Sigmoid).then_inc(s["sig_ready"], 1)

        def act_move_y(act, e, d, first):
            act.wait_ge(s["y_turned"], KC * e + d + 1)
            if d == 0 and not first:
                act.wait_ge(s["added_s"], 16 * e)
                act.wait_ge(s["added_p"], 16 * e)
            c = slice(d * P, (d + 1) * P)
            st.stand(act)
            nc.scalar.activation(y_s[:, c], Y[d % 2][:, 0, :], ACT.Copy, scale=gate_s[:, bass.ds(e, 1)])
            nc.scalar.activation(y_p[:, c], Y[d % 2][0:CAP_P, 1, :], ACT.Copy, scale=gate_p[:, bass.ds(e, 1)]).then_inc(s["y_moved"], 1)

        def act_expert(act, e, first, last):
            for t in range(TILES):
                if t == FIRST_DOWN - 1:
                    act_sigmoid(act, e, KC - 1)
                if t + AHEAD < TILES:
                    split_hi(act, e, t + AHEAD)
                elif not last:
                    split_hi(act, e + 1, t + AHEAD - TILES)
                if t < FIRST_DOWN and t % 2 == 0 and t:
                    act_sigmoid(act, e, t // 2 - 1)
                if t == TURN_X + 1 and not last:
                    act_x(act, e + 1)
                if t == 1 and not first:
                    act_move_y(act, e - 1, KC - 1, False)
                if t >= FIRST_DOWN + 2:
                    act_move_y(act, e, t - FIRST_DOWN - 2, first)
            act_move_y(act, e, KC - 2, first)
            if last:
                act_move_y(act, e, KC - 1, first)

        def dve_sum(dve, e, t, first):
            halves = out[t % BANKS][:, 0:2 * SLOTS].rearrange("p (two c) -> p c two", two=2)
            if t < FIRST_DOWN:
                j = t // 2
                dst = (gs, us)[t % 2][:, j % 2, :]
                dve.wait_ge(s["h_made" if t % 2 else "u_gated"], KC * e + j - 1 + CR)
            else:
                d = t - FIRST_DOWN
                dst = yT[:, d % 2, :]
                if d >= 2 or not first:
                    dve.wait_ge(s["y_turned"], KC * e + d - 1)
            dve.wait_ge(s["tile_done"], TILES * e + t + 1 + CR)
            nc.vector.tensor_reduce(dst, halves, AX.X, ALU.add).then_inc(s["summed"], 1)

        def dve_gate(dve, e, j):
            u, g = us[:, j % 2, :], gs[:, j % 2, :]
            dve.wait_ge(s["summed"], TILES * e + 2 * j + 2 + CR)
            nc.vector.tensor_tensor(u, u, g, ALU.mult).then_inc(s["u_gated"], 1)

        def dve_h(dve, e, j):
            u = us[:, j % 2, :]
            dve.wait_ge(s["u_gated"], KC * e + j + 1 + CR)
            dve.wait_ge(s["sig_ready"], KC * e + j + 1)
            nc.vector.tensor_tensor(u, u, sig[:, j % 2, :], ALU.mult).then_inc(s["h_made"], 1)
            dve.wait_ge(s["h_made"], KC * e + j + 1 + CR)
            nc.vector.tensor_copy(hT[:, j, 0:SLOTS], u).then_inc(s["h_hi_ready"], 1)
            dve.wait_ge(s["h_hi_ready"], KC * e + j + 1)
            nc.vector.tensor_tensor(hT[:, j, SLOTS:], u, hT[:, j, 0:SLOTS].bitcast(F32),
                                    ALU.subtract).then_inc(s["h_ready"], 1)

        def dve_expert(dve, e, first, last):
            for t in range(TILES):
                n = t + DVE_AHEAD
                if n % 2 == 0 and not (last and n >= TILES):
                    split_lo(dve, nc.vector, e + n // TILES, n % TILES)
                dve_sum(dve, e, t, first)
                if t < FIRST_DOWN and t % 2:
                    dve_gate(dve, e, t // 2)
                    if t == FIRST_DOWN - 1:
                        dve_h(dve, e, KC - 1)
                if t < FIRST_DOWN and t % 2 == 0 and t:
                    dve_h(dve, e, t // 2 - 1)
                if t == TURN_X + 1 and not last:
                    dve_x(dve, e + 1)

        def pool_gather(pool, e):
            nc.gpsimd.tensor_copy(cur_s[:], col_s[:, bass.ds(e, 1)])
            nc.gpsimd.tensor_copy(cur_p[:], col_p[:, bass.ds(e, 1)]).then_inc(s["cur_ready"], 1)
            pool.wait_ge(s["cur_ready"], e + 1)
            st.stand(pool)
            nc.gpsimd.indirect_dma_start(x_s[:], None, h2[1], bass.IndirectOffsetOnAxis(ap=cur_s[:], axis=0)).then_inc(s["gathered_s"], 16)
            nc.gpsimd.indirect_dma_start(x_p[:], None, h2[0], bass.IndirectOffsetOnAxis(ap=cur_p[:], axis=0)).then_inc(s["gathered_p"], 16)

        def pool_add(pool, e, first):
            if not first:
                pool.wait_ge(s["added_s"], 16 * e)
                pool.wait_ge(s["added_p"], 16 * e)
            nc.gpsimd.tensor_copy(out_s[:], col_s[:, bass.ds(e, 1)])
            nc.gpsimd.tensor_copy(out_p[:], col_p[:, bass.ds(e, 1)]).then_inc(s["out_ready"], 1)
            pool.wait_ge(s["out_ready"], e + 1)
            pool.wait_ge(s["y_moved"], KC * (e + 1) + CR)
            st.stand(pool)
            nc.gpsimd.indirect_dma_start(x3[1], bass.IndirectOffsetOnAxis(ap=out_s[:], axis=0), y_s[:], None,
                                         compute_op=ALU.add).then_inc(s["added_s"], 16)
            nc.gpsimd.indirect_dma_start(x3[0], bass.IndirectOffsetOnAxis(ap=out_p[:], axis=0), y_p[:], None,
                                         compute_op=ALU.add).then_inc(s["added_p"], 16)

        def pool_expert(pool, e, first, last):
            for t in range(TILES):
                n = t + AHEAD
                if n % 2 and not (last and n >= TILES):
                    split_lo(pool, nc.gpsimd, e + n // TILES, n % TILES)
                if t == ADD and not first:
                    pool_add(pool, e - 1, False)
                if t == GATHER and not last:
                    pool.wait_ge(s["x_turned"], e + 1)
                    pool.wait_ge(s["gathered_s"], 16 * (e + 1))
                    pool.wait_ge(s["gathered_p"], 16 * (e + 1))
                    pool_gather(pool, e + 1)

        def pe_turn_x(pe, e):
            pe.wait_ge(s["gathered_s"], 16 * (e + 1))
            pe.wait_ge(s["gathered_p"], 16 * (e + 1))
            for k in range(KC):
                dst = X[:, k // BANKX, (k % BANKX) * SLOTS:(k % BANKX + 1) * SLOTS]
                nc.tensor.transpose(dst[:, 0:CAP_S], x_s[:, k * P:(k + 1) * P], C.ident[:])
                mm = nc.tensor.transpose(dst[:, CAP_S:], x_p[:, k * P:(k + 1) * P], C.ident[0:CAP_P, 0:CAP_P])
            mm.then_inc(s["x_turned"], 1)

        def pe_turn_y(pe, e, d):
            pe.wait_ge(s["summed"], TILES * e + FIRST_DOWN + d + 1 + CR)
            pe.wait_ge(s["y_moved"], KC * e + d - 1 + CR)
            nc.tensor.transpose(Y[d % 2][:, 0, :], yT[:, d % 2, 0:CAP_S], C.ident[:])
            nc.tensor.transpose(Y[d % 2][0:CAP_P, 1, :], yT[:, d % 2, CAP_S:], C.ident[:]).then_inc(s["y_turned"], 1)

        def pe_tile(pe, e, t):
            i, bank = t % RING, out[t % BANKS]
            if t == 0:
                pe.wait_ge(s["xT_lo"], 3 * (e + 1))
            pe.wait_ge(*lo_done(e, t))
            pe.wait_ge(s["summed"], TILES * e + t - BANKS + 1 + CR)
            B = xT if t < FIRST_DOWN else hT
            for k in range(KC):
                if t == FIRST_DOWN:
                    pe.wait_ge(s["h_ready"], KC * e + k + 1)
                nc.tensor.matmul(bank[:, 0:2 * SLOTS], w_hi[i][:, k, :], B[:, k, :], start=(k == 0), stop=False)
                mm = nc.tensor.matmul(bank[:, SLOTS:2 * SLOTS], w_lo[i][:, k, :], B[:, k, 0:SLOTS], start=False,
                                      stop=(k == KC - 1))
            mm.then_inc(s["tile_done"], 1)

        def pe_expert(pe, e, first, last):
            for t in range(TILES):
                pe_tile(pe, e, t)
                if t == 0 and not first:
                    pe_turn_y(pe, e - 1, KC - 1)
                if t > FIRST_DOWN:
                    pe_turn_y(pe, e, t - FIRST_DOWN - 1)
                if t == TURN_X and not last:
                    pe_turn_x(pe, e + 1)
            if last:
                pe_turn_y(pe, e, KC - 1)

        def find(dve, work, val, idx, waves, done):
            for w in range(waves):
                c = slice(8 * w, 8 * w + 8)
                if done + w:
                    dve.wait_ge(s["replaced"], done + w)
                nc.vector.max(val[:, c], work).then_inc(s["max_found"], 1)
                dve.wait_ge(s["max_found"], done + w + 1)
                nc.vector.max_index(idx[:, c], val[:, c], work).then_inc(s["index_found"], 1)
                dve.wait_ge(s["index_found"], done + w + 1)
                nc.vector.match_replace(work, val[:, c], work, -1.0).then_inc(s["replaced"], 1)

        lists = ((val_s, CAP_S, out[0]), (idxf_s, CAP_S, out[1]), (val_p, CAP_P, out[2]), (idxf_p, CAP_P, X[:, 0, :]))
        flipped = Y[0][:, 0, 0:2 * NE]

        def merge_halves(dve):
            for n, add in enumerate((0.0, float(HALF_S))):
                dve.wait_ge(s["turned"], n + 1)
                nc.vector.tensor_copy(first[:, n, :], out[n][:, 0:NE]).then_inc(s["merge_step"], 1)
                nc.vector.tensor_scalar(second[:, n, :], out[n][:, NE:2 * NE], add, None, ALU.add).then_inc(s["merge_step"], 1)
            dve.wait_ge(s["flipped"], 1)
            dve.wait_ge(s["merge_step"], 4)
            nc.vector.tensor_tensor(wins[:], first[:, 0, :], flipped[:, 0:NE], ALU.is_ge).then_inc(s["merge_step"], 1)
            nc.vector.tensor_tensor(gate_s[:], first[:, 0, :], flipped[:, 0:NE], ALU.max).then_inc(s["columns_ready"], 1)
            nc.vector.tensor_copy(best[:], flipped[:, NE:2 * NE]).then_inc(s["merge_step"], 1)
            dve.wait_ge(s["merge_step"], 5)
            nc.vector.tensor_copy(wins_mask[:], wins[:]).then_inc(s["merge_step"], 1)
            dve.wait_ge(s["merge_step"], 7)
            nc.vector.copy_predicated(best[:], wins_mask[:], first[:, 1, :]).then_inc(s["merge_step"], 1)
            dve.wait_ge(s["merge_step"], 8)
            nc.vector.tensor_copy(col_s[:], best[:]).then_inc(s["columns_ready"], 1)

        with st.block() as block:

            @block.sync
            def _(sp):
                for p in range(RAW):
                    sp_load(sp, 0, p)
                for p in range(RAW, PIECES):
                    sp_reload(sp, 0, p)
                with sp.Fori(1, NE) as e:
                    for p in range(PIECES):
                        sp_reload(sp, e, p)
                sp.wait_ge(s["added_s"], 16 * NE)
                sp.wait_ge(s["added_p"], 16 * NE)

            @block.scalar
            def _(act):
                act.sem_inc(s["y_moved"], CR)
                for t in range(AHEAD):
                    split_hi(act, 0, t)
                act_x(act, 0)
                act_expert(act, 0, True, False)
                with act.Fori(1, NE - 1) as e:
                    act_expert(act, e, False, False)
                act_expert(act, NE - 1, False, True)

            @block.gpsimd
            def _(pool):
                nc.gpsimd.affine_select(out=flip_part[:], in_=C.ones[:], compare_op=ALU.is_ge, fill=0.0, base=1 - CAP_S,
                                        pattern=[[1, P]], channel_multiplier=1).then_inc(s["flip_half"], 1)
                pool.wait_ge(s["flip_half"], 1)
                nc.gpsimd.affine_select(out=flip[:], in_=flip_part[:], compare_op=ALU.is_ge, fill=0.0, base=CAP_S - 1,
                                        pattern=[[-1, P]], channel_multiplier=-1).then_inc(s["flip_ready"], 1)
                for t in range(1, AHEAD, 2):
                    split_lo(pool, nc.gpsimd, 0, t)
                pool.wait_ge(s["columns_ready"], 4)
                pool_gather(pool, 0)
                pool_expert(pool, 0, True, False)
                with pool.Fori(1, NE - 1) as e:
                    pool_expert(pool, e, False, False)
                pool_expert(pool, NE - 1, False, True)
                pool_add(pool, NE - 1, False)

            @block.tensor
            def _(pe):
                pe.sem_inc(s["tile_done"], CR)
                pe.wait_ge(s["listed"], 2)
                for src, cap, dst in lists:
                    n = src.shape[0]
                    nc.tensor.transpose(dst[0:cap, 0:n], src[:], C.ident[0:n, 0:n]).then_inc(s["turned"], 1)
                pe.wait_ge(s["flip_ready"], 1)
                pe.wait_ge(s["merge_step"], 4)
                nc.tensor.matmul(flipped, flip[:], second[:].rearrange("p a e -> p (a e)"), start=True, stop=True).then_inc(s["flipped"], 1)
                pe_turn_x(pe, 0)
                pe_expert(pe, 0, True, False)
                with pe.Fori(1, NE - 1) as e:
                    pe_expert(pe, e, False, False)
                pe_expert(pe, NE - 1, False, True)

            @block.vector
            def _(dve):
                for n in ("summed", "u_gated", "h_made"):
                    dve.sem_inc(s[n], CR)
                find(dve, aff_s[:], val_s, idx_s, WAVES_S, 0)
                find(dve, aff_p[:], val_p, idx_p, WAVES_P, WAVES_S)
                nc.vector.tensor_copy(idxf_s[:], idx_s[:]).then_inc(s["listed"], 1)
                nc.vector.tensor_copy(idxf_p[:], idx_p[:]).then_inc(s["listed"], 1)
                merge_halves(dve)
                for n, dst in ((2, gate_p), (3, col_p)):
                    dve.wait_ge(s["turned"], n + 1)
                    nc.vector.tensor_copy(dst[:], lists[n][2][0:CAP_P, 0:NE]).then_inc(s["columns_ready"], 1)
                for t in range(0, DVE_AHEAD, 2):
                    split_lo(dve, nc.vector, 0, t)
                dve_x(dve, 0)
                dve_expert(dve, 0, True, False)
                with dve.Fori(1, NE - 1) as e:
                    dve_expert(dve, e, False, False)
                dve_expert(dve, NE - 1, False, True)


def norm_out(nc, C, x3, final_g, y_prompt, y_sample):
    with Stage(nc, "no") as st:
        x = st.sb("x", [P, NT, D])
        gain, junk = st.sb("gain", [P, D]), st.sb("junk", [P, D])
        ssq, var, std, rstd = (st.sb(n, [P, NT]) for n in ("ssq", "var", "std", "rstd"))
        x_loaded = [st.sem(f"x_loaded{t}") for t in range(NT)]
        s = {n: st.sem(n) for n in ("gain_loaded", "ssq_ready", "var_ready", "std_ready", "rstd_ready", "y_ready", "y_stored")}

        def rows(pair, t):
            a, n = (pair[0], t) if t < NT_PROMPT else (pair[1], t - NT_PROMPT)
            return a[n * P:(n + 1) * P, :]

        with st.block() as block:

            @block.sync
            def _(sp):
                for t in range(NT):
                    sp.dma_start(x[:, t, :], rows(x3, t)).then_inc(x_loaded[t], 16)
                    if t == 0:
                        sp.dma_start(gain[:], final_g.rearrange("(a d) -> a d", a=1).broadcast_to([P, D])).then_inc(s["gain_loaded"], 16)
                for t in range(NT):
                    sp.wait_ge(s["y_ready"], t + 1)
                    sp.dma_start(rows((y_prompt[0], y_sample[0]), t), x[:, t, :]).then_inc(s["y_stored"], 16)
                sp.wait_ge(s["y_stored"], 16 * NT)

            @block.scalar
            def _(act):
                def square(t):
                    act.wait_ge(x_loaded[t], 16)
                    if t:
                        act.wait_ge(s["ssq_ready"], t)
                    nc.scalar.activation(junk[:], x[:, t, :], ACT.Square, accum_out=ssq[:, t:t + 1]).then_inc(s["ssq_ready"], 1)

                square(0)
                for t in range(NT):
                    if t + 1 < NT:
                        square(t + 1)
                    act.wait_ge(s["var_ready"], t + 1)
                    nc.scalar.activation(std[:, t:t + 1], var[:, t:t + 1], ACT.Sqrt).then_inc(s["std_ready"], 1)

            @block.vector
            def _(dve):
                def variance(t):
                    dve.wait_ge(s["ssq_ready"], t + 1)
                    nc.vector.tensor_scalar(var[:, t:t + 1], ssq[:, t:t + 1], 1.0 / D, EPS, ALU.mult, ALU.add).then_inc(s["var_ready"], 1)

                variance(0)
                dve.wait_ge(s["gain_loaded"], 16)
                for t in range(NT):
                    if t + 1 < NT:
                        variance(t + 1)
                    dve.wait_ge(s["std_ready"], t + 1)
                    nc.vector.reciprocal(rstd[:, t:t + 1], std[:, t:t + 1]).then_inc(s["rstd_ready"], 1)
                    dve.wait_ge(s["rstd_ready"], t + 1)
                    nc.vector.scalar_tensor_tensor(out=x[:, t, :], in0=x[:, t, :], scalar=rstd[:, t:t + 1], in1=gain[:],
                                                   op0=ALU.mult, op1=ALU.mult).then_inc(s["y_ready"], 1)


def build(nc, I, y_prompt, y_sample):
    class C:
        pass

    def scratch(name, shape):
        return nc.dram_tensor(name, shape, F32).ap()

    ya, yb, m_a, m_ab = (scratch(n, (D, T)) for n in ("ya", "yb", "m_a", "m_ab"))
    x3 = scratch("x3_prompt", (T_PROMPT, D)), scratch("x3_sample", (T_SAMPLE, D))
    h2 = scratch("h2_prompt", (T_PROMPT, D)), scratch("h2_sample", (T_SAMPLE, D))
    w_in = I["w_in"][0]
    with Stage(nc, "all") as top:
        constant_buffers(C, top)
        with Stage(nc, "trunk") as st:
            h_hi = st.sb("h_hi", [P, KC, T], F32R)
            h_lo = st.sb("h_lo", [P, KC, T], F32R)
            C.first_tile = weight_buffers(st, 0)
            norm_in(nc, C, I["x_prompt"], I["x_sample"], I["norm1_g"], I["b_lb_logits"], I["b_onorm_g"],
                    I["a_vnorm_g"], h_hi, h_lo, cols(w_in, COL_V))
            gmlp(nc, C, w_in, I["a_spatial_w"][0], I["a_spatial_b"][0], h_hi, h_lo, ya, cols(w_in, COL_GA))
            merge(nc, C, "ma", w_in, COL_GA, I["w_branch_a"][0], ya, None, m_a, h_hi, h_lo, cols(w_in, COL_Q))
            hgrn2(nc, C, w_in, h_hi, h_lo, yb, cols(w_in, COL_GB))
            merge(nc, C, "mb", w_in, COL_GB, I["w_branch_b"][0], yb, m_a, m_ab, h_hi, h_lo, None)
        aff_p, aff_s = top.sb("aff_p", [NE, T_PROMPT]), top.sb("aff_s", [2 * NE, HALF_S])
        with Stage(nc, "mixed") as st:
            x2 = st.sb("x2", [P, NT, D])
            residual(nc, C, I["x_prompt"], I["x_sample"], I["w_out"][0], m_ab, x2)
            route(nc, C, I["norm2_g"], I["w_router"][0], x2, x3, h2, aff_p, aff_s)
        experts(nc, C, aff_p, aff_s, h2, x3, I["w_exp_gate"][0], I["w_exp_up"][0], I["w_exp_down"][0])
        norm_out(nc, C, x3, I["final_g"], y_prompt, y_sample)


_INS = ["x_prompt", "x_sample", "norm1_g", "w_in", "a_vnorm_g", "a_spatial_w", "a_spatial_b", "b_lb_logits",
        "b_onorm_g", "w_branch_a", "w_branch_b", "w_out", "norm2_g", "w_router", "w_exp_gate", "w_exp_up",
        "w_exp_down", "final_g"]
_OUTS = [((1, T_PROMPT, D), "float32"), ((1, T_SAMPLE, D), "float32")]


def kernel(**inputs):
    import numpy as _np
    import concourse.bacc as _bacc
    from concourse import mybir as _mybir
    from concourse.bass_utils import run_bass_kernel_spmd as _run

    nc = _bacc.Bacc("TRN2", target_bir_lowering=False, num_devices=1)
    arrays, aps = {}, {}
    for name in _INS:
        a = _np.ascontiguousarray(inputs[name])
        arrays[f"in_{name}_dram"] = a
        aps[name] = nc.dram_tensor(f"in_{name}_dram", a.shape, _mybir.dt.from_np(a.dtype), kind="ExternalInput").ap()
    outs = [nc.dram_tensor(f"out_{i}_dram", shape, _mybir.dt.from_np(_np.dtype(dtype)), kind="ExternalOutput").ap()
            for i, (shape, dtype) in enumerate(_OUTS)]
    build(nc, aps, *outs)
    r = _run(nc, [arrays], core_ids=[0])
    return tuple(r.results[0][f"out_{i}_dram"] for i in range(len(_OUTS)))
```
